# Optimizing a Trainium2 kernel written in Bass

```python
import jax, jax.numpy as jnp
from jax import lax
import numpy as np

D_MODEL = 1024
BATCH = 1
SEQ = 256
DEPTH = 2

GRID_W = 64
NORM_EPS = 1e-6
N_DIR = 2
RW_HEADS = 8
RW_HEAD_DIM = 64
RW_WIDTH = RW_HEADS * RW_HEAD_DIM
RW_DECAY_LORA = 64
RW_ICLR_LORA = 64
RW_GATE_LORA = 128
RW_LN_EPS = 64e-5
CV_GROUPS = 8
CV_WIDTH = CV_GROUPS * 64
CV_KSIZE = 3
AT_Q_HEADS = 8
AT_KV_HEADS = 2
AT_HEAD_DIM = 64
AT_Q_BLOCK = 128
ROPE_THETA = 10000.0
N_BRANCH = 3
BRANCH_WIDTH = 512
D_FF = 4 * D_MODEL

RW_COLS = 3 * RW_WIDTH + N_DIR * RW_DECAY_LORA + N_DIR * RW_ICLR_LORA + RW_GATE_LORA
CV_COLS = 3 * CV_WIDTH
AT_COLS = (AT_Q_HEADS + 2 * AT_KV_HEADS) * AT_HEAD_DIM
GATE_COLS = N_BRANCH * D_MODEL
IN_COLS = RW_COLS + CV_COLS + AT_COLS + GATE_COLS

kernel_name = "hybrid_rwkv7_conv_gqa_gated_encoder"

def rmsnorm(x, g, eps=NORM_EPS):
    xf = x.astype(jnp.float32)
    y = xf * lax.rsqrt(jnp.mean(xf * xf, axis=-1, keepdims=True) + eps)
    return (y * g.astype(jnp.float32)).astype(x.dtype)

def split_cols(z, sizes):
    offs = np.concatenate([[0], np.cumsum(sizes)]).astype(int)
    return [z[..., int(offs[i]):int(offs[i + 1])] for i in range(len(sizes))]

def token_shift_centred(z, mu_prev, mu_next):
    zp = jnp.pad(z, ((0, 0), (1, 0), (0, 0)))[:, :-1]
    zn = jnp.pad(z, ((0, 0), (0, 1), (0, 0)))[:, 1:]
    return z + mu_prev * (zp - z) + mu_next * (zn - z)

def to_dir_scan(z):
    z = jnp.stack([z[:, :, 0], jnp.flip(z[:, :, 1], axis=1)], axis=0)
    return jnp.moveaxis(z, 2, 0)

def rwkv7_bidir(cols, mu_prev, mu_next, w0, w2, a0, a2, g2, k_k, k_a, r_k, ln_g, ln_b):
    B, S, _ = cols.shape
    H, N = RW_HEADS, RW_HEAD_DIM
    z = token_shift_centred(cols.astype(jnp.float32), mu_prev, mu_next)
    r, k, v, wd, ad, gd = split_cols(z, [RW_WIDTH] * 3 + [N_DIR * RW_DECAY_LORA, N_DIR * RW_ICLR_LORA, RW_GATE_LORA])
    heads = lambda t: t.reshape(t.shape[:-1] + (H, N))
    shared = lambda t: jnp.broadcast_to(t[:, :, None], (B, S, N_DIR, H, N))
    w_raw = w0 + jnp.einsum('bsdr,drc->bsdc', jnp.tanh(wd.reshape(B, S, N_DIR, RW_DECAY_LORA)), w2)
    decay = jnp.exp(-jnp.exp(-jax.nn.softplus(-w_raw) - 0.5))
    a = jax.nn.sigmoid(a0 + jnp.einsum('bsdr,drc->bsdc', ad.reshape(B, S, N_DIR, RW_ICLR_LORA), a2))
    g = jnp.einsum('bsr,rc->bsc', jax.nn.sigmoid(gd), g2)
    kk = heads(k * k_k)
    kk = kk / jnp.maximum(jnp.sqrt(jnp.sum(kk * kk, axis=-1, keepdims=True)), 1e-12)
    k_dir = k[:, :, None, :] * (1.0 + (a - 1.0) * k_a)
    kka = kk[:, :, None] * heads(a)
    xs = (to_dir_scan(shared(heads(r))), to_dir_scan(heads(decay)), to_dir_scan(heads(k_dir)),
          to_dir_scan(shared(heads(v))), to_dir_scan(shared(kk)), to_dir_scan(kka))

    def step(state, inp):
        r_t, w_t, k_t, v_t, kk_t, kka_t = inp
        sa = jnp.einsum('dbhvk,dbhk->dbhv', state, kk_t)
        state = state * w_t[..., None, :] - sa[..., :, None] * kka_t[..., None, :] + v_t[..., :, None] * k_t[..., None, :]
        y = jnp.einsum('dbhvk,dbhk->dbhv', state, r_t)
        return state, y

    state0 = jnp.zeros((N_DIR, B, H, N, N), jnp.float32)
    _, ys = lax.scan(step, state0, xs)
    y = jnp.moveaxis(ys[:, 0] + jnp.flip(ys[:, 1], axis=0), 0, 1)
    mu = jnp.mean(y, axis=-1, keepdims=True)
    var = jnp.mean(jnp.square(y - mu), axis=-1, keepdims=True)
    y = ((y - mu) * lax.rsqrt(var + RW_LN_EPS)).reshape(B, S, RW_WIDTH) * ln_g + ln_b
    k_bonus = heads(jnp.mean(k_dir, axis=2))
    bonus = jnp.sum(heads(r) * k_bonus * r_k, axis=-1, keepdims=True) * heads(v)
    return ((y + bonus.reshape(B, S, RW_WIDTH)) * g).astype(cols.dtype)

def short_gated_conv(cols, w, b):
    b_gate, c_gate, x_in = split_cols(cols, [CV_WIDTH] * 3)
    z = c_gate * x_in
    S = z.shape[1]
    zp = jnp.pad(z, ((0, 0), (1, 1), (0, 0)))
    conv = b + sum(w[j] * zp[:, j:j + S] for j in range(CV_KSIZE))
    return b_gate * conv

def axial_rope_tables(S):
    rows = S // GRID_W
    row = jnp.repeat(jnp.arange(rows), GRID_W).astype(jnp.float32)
    col = jnp.tile(jnp.arange(GRID_W), rows).astype(jnp.float32)
    half = AT_HEAD_DIM // 2
    inv = ROPE_THETA ** (-jnp.arange(0, half, 2, dtype=jnp.float32) / half)
    ang_r = row[:, None] * inv
    ang_c = col[:, None] * inv
    return jnp.cos(ang_r), jnp.sin(ang_r), jnp.cos(ang_c), jnp.sin(ang_c)

def rotate_half(x, cos, sin):
    d2 = x.shape[-1] // 2
    x1, x2 = x[..., :d2], x[..., d2:]
    c, s = cos[:, None, :], sin[:, None, :]
    return jnp.concatenate([x1 * c - x2 * s, x2 * c + x1 * s], axis=-1)

def apply_axial_rope(x, tabs):
    cr, sr, cc, sc = tabs
    half = AT_HEAD_DIM // 2
    xf = x.astype(jnp.float32)
    out = jnp.concatenate([rotate_half(xf[..., :half], cr, sr), rotate_half(xf[..., half:], cc, sc)], axis=-1)
    return out.astype(x.dtype)

def gqa_axial(cols, q_g, k_g, tabs):
    B, S, _ = cols.shape
    G = AT_Q_HEADS // AT_KV_HEADS
    q, k, v = split_cols(cols, [AT_Q_HEADS * AT_HEAD_DIM, AT_KV_HEADS * AT_HEAD_DIM, AT_KV_HEADS * AT_HEAD_DIM])
    q = apply_axial_rope(rmsnorm(q.reshape(B, S, AT_Q_HEADS, AT_HEAD_DIM), q_g), tabs)
    k = apply_axial_rope(rmsnorm(k.reshape(B, S, AT_KV_HEADS, AT_HEAD_DIM), k_g), tabs)
    v = v.reshape(B, S, AT_KV_HEADS, AT_HEAD_DIM)
    q = (q * (AT_HEAD_DIM ** -0.5)).reshape(B, S // AT_Q_BLOCK, AT_Q_BLOCK, AT_KV_HEADS, G, AT_HEAD_DIM)
    q = jnp.moveaxis(q, 1, 0)

    def block(qb):
        s = jnp.einsum('bqkgd,bskd->bkgqs', qb, k).astype(jnp.float32)
        p = jax.nn.softmax(s, axis=-1).astype(v.dtype)
        return jnp.einsum('bkgqs,bskd->bqkgd', p, v)

    o = lax.map(block, q)
    return jnp.moveaxis(o, 0, 1).reshape(B, S, AT_Q_HEADS * AT_HEAD_DIM)

def setup_inputs(seed: int = 0) -> dict:
    key = jax.random.key(seed)
    ks = jax.random.split(key, 32)
    L, D = DEPTH, D_MODEL
    nrm = lambda k, shape, s: jax.random.normal(k, shape, jnp.float32) * s
    uni = lambda k, shape, lo, hi: jax.random.uniform(k, shape, jnp.float32, lo, hi)
    return {
        "x": nrm(ks[0], (BATCH, SEQ, D), 1.0),
        "norm1_g": 1.0 + nrm(ks[1], (L, D), 0.02),
        "w_in": nrm(ks[2], (L, D, IN_COLS), D ** -0.5),
        "rw_mu_prev": uni(ks[3], (L, RW_COLS), 0.0, 0.5),
        "rw_mu_next": uni(ks[4], (L, RW_COLS), 0.0, 0.5),
        "rw_w0": uni(ks[5], (L, N_DIR, RW_WIDTH), -6.0, 1.0),
        "rw_w2": nrm(ks[6], (L, N_DIR, RW_DECAY_LORA, RW_WIDTH), 0.1),
        "rw_a0": nrm(ks[7], (L, N_DIR, RW_WIDTH), 0.5),
        "rw_a2": nrm(ks[8], (L, N_DIR, RW_ICLR_LORA, RW_WIDTH), 0.1),
        "rw_g2": nrm(ks[9], (L, RW_GATE_LORA, RW_WIDTH), RW_GATE_LORA ** -0.5),
        "rw_k_k": 0.85 + nrm(ks[10], (L, RW_WIDTH), 0.05),
        "rw_k_a": 1.0 + nrm(ks[11], (L, RW_WIDTH), 0.05),
        "rw_r_k": nrm(ks[12], (L, RW_HEADS, RW_HEAD_DIM), 0.1),
        "rw_ln_g": 1.0 + nrm(ks[13], (L, RW_WIDTH), 0.02),
        "rw_ln_b": nrm(ks[14], (L, RW_WIDTH), 0.01),
        "cv_w": nrm(ks[15], (L, CV_KSIZE, CV_WIDTH), 0.5),
        "cv_b": nrm(ks[16], (L, CV_WIDTH), 0.01),
        "at_q_g": 1.0 + nrm(ks[17], (L, AT_HEAD_DIM), 0.02),
        "at_k_g": 1.0 + nrm(ks[18], (L, AT_HEAD_DIM), 0.02),
        "w_branch": nrm(ks[19], (L, N_BRANCH, BRANCH_WIDTH, D), BRANCH_WIDTH ** -0.5),
        "w_out": nrm(ks[20], (L, D, D), D ** -0.5),
        "norm2_g": 1.0 + nrm(ks[21], (L, D), 0.02),
        "w_mlp1": nrm(ks[22], (L, D, D_FF), D ** -0.5),
        "w_mlp2": nrm(ks[23], (L, D_FF, D), D_FF ** -0.5),
    }

def reference(x, norm1_g, w_in, rw_mu_prev, rw_mu_next, rw_w0, rw_w2, rw_a0, rw_a2, rw_g2,
              rw_k_k, rw_k_a, rw_r_k, rw_ln_g, rw_ln_b, cv_w, cv_b, at_q_g, at_k_g,
              w_branch, w_out, norm2_g, w_mlp1, w_mlp2):
    B, S, D = x.shape
    tabs = axial_rope_tables(S)
    for l in range(DEPTH):
        h = rmsnorm(x, norm1_g[l])
        cols = h @ w_in[l]
        rw_c, cv_c, at_c, gate_c = split_cols(cols, [RW_COLS, CV_COLS, AT_COLS, GATE_COLS])
        y_rw = rwkv7_bidir(rw_c, rw_mu_prev[l], rw_mu_next[l], rw_w0[l], rw_w2[l], rw_a0[l], rw_a2[l],
                           rw_g2[l], rw_k_k[l], rw_k_a[l], rw_r_k[l], rw_ln_g[l], rw_ln_b[l])
        y_cv = short_gated_conv(cv_c, cv_w[l], cv_b[l])
        y_at = gqa_axial(at_c, at_q_g[l], at_k_g[l], tabs)
        gates = jax.nn.sigmoid(gate_c.reshape(B, S, N_BRANCH, D))
        merged = (gates[:, :, 0] * (y_rw @ w_branch[l, 0])
                  + gates[:, :, 1] * (y_cv @ w_branch[l, 1])
                  + gates[:, :, 2] * (y_at @ w_branch[l, 2]))
        x = x + (merged @ w_out[l]).astype(x.dtype)
        h = rmsnorm(x, norm2_g[l])
        u = jnp.square(jax.nn.relu(h @ w_mlp1[l]))
        x = x + (u @ w_mlp2[l]).astype(x.dtype)
    return x


_drawn_inputs = setup_inputs


def setup_inputs(seed=0):
    import zlib

    import numpy as np

    out = dict(_drawn_inputs(seed))
    spreads = {}
    factors = {'rw_w2': 3.395,
     'rw_k_k': 3.057,
     'rw_ln_g': 7.789,
     'rw_ln_b': 8.0,
     'cv_b': 8.0,
     'at_q_g': 8.0,
     'at_k_g': 8.0}
    for name, (base, spread) in spreads.items():
        noise = np.random.default_rng([zlib.crc32(name.encode()), seed]).standard_normal(out[name].shape)
        drawn = base * np.exp(spread * noise) if base else spread * noise
        out[name] = __import__('jax').numpy.asarray(drawn.astype(out[name].dtype))
    for name, factor in factors.items():
        out[name] = (out[name] * factor).astype(out[name].dtype)
    return out
```

```python
from contextlib import ExitStack

import numpy as np

import concourse.bass as bass
from concourse import mybir

F32 = mybir.dt.float32
F32R = mybir.dt.float32r
ALU = mybir.AluOpType
ACT = mybir.ActivationFunctionType
AX = mybir.AxisListType

P = 128
D = 1024
SEQ = 256
NT = SEQ // P
KT = D // P
DEPTH = 2
H = 8
HD = 64
RW = H * HD
JT = RW // P
C = 64
FF = 4 * D
EPS = 1e-6
LN_EPS = 64e-5
DECAY = float(np.exp(np.float32(-0.5)))
GRID_W = 64
KV = 2
QKV = (H + 2 * KV) * HD

UNIT = 8 * P
CHUNK = 3
U_RW = 0
U_CV = U_RW + 15
U_AT = U_CV + 12
U_GATE = U_AT + 6
U_OUT = U_GATE + 36
U_MLP = U_OUT + KT
UNITS = U_MLP + 64
CHUNKS = UNITS // CHUNK
RING = 6
LANDS = ((CHUNKS + 1) // 2, CHUNKS // 2)

PARAMS = {}
_at = 0
for _name, _n in (("norm1_g", KT), ("norm2_g", KT), ("mu_prev", 15), ("mu_next", 15), ("w0", 8), ("a0", 8),
                  ("k_k", 4), ("k_a", 4), ("r_k", 4), ("ln_g", 4), ("ln_b", 4), ("cv_w", 12), ("cv_b", 4)):
    PARAMS[_name] = _at
    _at += _n
NPAR = _at
D_MU, D_W0, D_A0, D_KA = 0, 15, 23, 31
NDER = 35

LEVELS = (1, 2, 4, 8, 16, 32)
CONST = {}
_at = 0
for _name, _n in (("ident", P), ("ones", P), ("sel", JT * P), ("rope_c", NT * HD), ("rope_s", NT * HD),
                  ("reset", 2 * SEQ), ("incl", 2 * 2 * P), ("level", 2 * len(LEVELS) * P), ("headsum", 2)):
    CONST[_name] = _at
    _at += _n
NCONST = _at


class Signal:

    def __init__(self, sem, per):
        self.sem, self.per = sem, per

    def after(self, layer, n):
        return self.sem, layer * self.per + n


def build(nc, x_in, stream, params, lora, gains, consts, out):
    with ExitStack() as ctx:
        sem = lambda name: ctx.enter_context(nc.semaphore(name))
        sig = lambda name, per: Signal(sem(name), per)
        bank = [ctx.enter_context(nc.psum_tensor(f"bank{i}", [P, 512], F32)) for i in range(8)]

        place = [nc.sbuf_base + (-nc.sbuf_base) % 32]

        def sb(name, shape, dt=F32):
            size = 4 * int(np.prod(shape[1:]))
            t = nc.alloc_sbuf_tensor_at(name, shape, dt, offset=place[0])
            place[0] += size + (-size) % 32
            return t

        raw = sb("raw", [P, 2, CHUNK * UNIT])
        w_hi = sb("w_hi", [P, RING, UNIT], F32R)
        w_lo = sb("w_lo", [P, RING, UNIT], F32R)
        x = sb("x", [P, NT, D])
        h_hi = sb("h_hi", [P, KT, SEQ], F32R)
        h_lo = sb("h_lo", [P, KT, SEQ], F32R)
        y_hi = sb("y_hi", [P, JT, SEQ], F32R)
        y_lo = sb("y_lo", [P, JT, SEQ], F32R)
        cst = sb("cst", [P, NCONST])
        par = sb("par", [P, NPAR])
        der = sb("der", [P, NDER])
        lor = sb("lor", [P, 3, RW])
        gain = sb("gain", [P, (H + KV) * HD])
        stat = sb("stat", [P, 2])
        mean2 = sb("mean2", [P, 2])
        rstd = sb("rstd", [P, 2])
        mhalf = sb("mhalf", [P, 20])
        overlay = place[0]

        z = sb("z", [P, 15, SEQ])
        kk = sb("kk", [P, JT, SEQ])
        ksum = sb("ksum", [P, JT, SEQ])
        v_tok = sb("v_tok", [P, NT, RW])
        y_tok = sb("y_tok", [P, NT, RW])
        a_t = sb("a_t", [P, JT, SEQ])
        lw = sb("lw", [P, JT, SEQ])
        cum = sb("cum", [P, JT, SEQ])
        e_cum = sb("e_cum", [P, JT, SEQ])
        kr = sb("kr", [P, JT, 2, SEQ])
        kh = sb("kh", [P, JT, SEQ])
        bh = sb("bh", [P, JT, SEQ])
        kh_tok = sb("kh_tok", [P, NT, RW])
        bh_tok = sb("bh_tok", [P, NT, RW])
        bq = sb("bq", [P, H, 2, P])
        kq = sb("kq", [P, H, 2, P])
        xt = sb("xt", [P, H, P])
        state = sb("state", [P, JT, P])
        s_new = sb("s_new", [P, JT, HD])
        small = sb("small", [P, 4, 16])
        rn_t = sb("rn_t", [8, SEQ])
        assert place[0] <= nc.sbuf_usable_end, (place[0], nc.sbuf_usable_end)
        xm = a_t[:, :, :].rearrange("p j (e s) -> p (j e) s", e=2)
        zm = cum[:, :, :].rearrange("p j (e s) -> p (j e) s", e=2)
        r_b = lw[:, 0:2, :].rearrange("p a b -> p (a b)")
        u_b = lw[:, 2:4, :].rearrange("p a b -> p (a b)")
        xn1 = z[:, 0:8, :].rearrange("p (t a) b -> p t (a b)", t=2)

        place[0] = overlay
        yb_hi = sb("yb_hi", [P, 2 * JT, SEQ], F32R)
        yb_lo = sb("yb_lo", [P, 2 * JT, SEQ], F32R)
        m_hi = sb("m_hi", [P, KT, SEQ], F32R)
        m_lo = sb("m_lo", [P, KT, SEQ], F32R)
        overlay3 = place[0]
        cz = sb("cz", [P, 2, SEQ + 2])
        cc = sb("cc", [P, 2, SEQ])
        cv = sb("cv", [P, 2, SEQ])
        qkv = sb("qkv", [P, NT, QKV])
        q_sq = sb("q_sq", [P, NT, (H + KV) * HD])
        q_rt = sb("q_rt", [P, NT, (H + KV) * HD])
        a_st = sb("a_st", [P, 3, 20])
        rot = sb("rot", [P, NT, (H + KV) * HD])
        q_t = sb("q_t", [P, 4, SEQ])
        k_t = sb("k_t", [P, SEQ])
        prob = sb("prob", [P, 2, NT, SEQ])
        p_t = sb("p_t", [P, 2, NT, SEQ])
        nmx = sb("nmx", [P, 8, NT])
        rsum = sb("rsum", [P, 8, NT])
        rinv = sb("rinv", [P, 8, NT])
        gth = sb("gth", [P, 2, 3, SEQ])
        gmul = sb("gmul", [P, 2, 3, SEQ])
        top2 = place[0]
        place[0] = overlay3
        xn2 = sb("xn2", [P, NT, D])
        relu = sb("relu", [P, 3, 512])
        usq = sb("usq", [P, 3, 512])
        u_hi = sb("u_hi", [P, 3, 2, SEQ], F32R)
        u_lo = sb("u_lo", [P, 3, 2, SEQ], F32R)
        assert place[0] <= nc.sbuf_usable_end, (place[0], nc.sbuf_usable_end)

        def con(name, n, at=0, rows=P):
            return cst[0:rows, CONST[name] + at:CONST[name] + at + n]

        def par_of(name, i):
            return par[:, PARAMS[name] + i:PARAMS[name] + i + 1]

        ident = con("ident", P)

        consts_in = sem("consts_in")
        x_in_s = sem("x_in")
        out_s = sem("out_written")
        half_s = sem("exponent_set")
        landed = [sem("landed0"), sem("landed1")]
        pars_in = sem("pars_in")
        lora_in = sem("lora_in")
        gains_in = sem("gains_in")
        hi_ready = sig("hi_ready", UNITS)
        lo_ready = sig("lo_ready", UNITS)
        unit_used = sig("unit_used", UNITS)
        derived = sig("derived", 1)
        x_new = sig("x_new", 8)
        sumsq = sig("sumsq", 4)
        meansq = sig("meansq", 2)
        rstd_s = sig("rstd_ready", 2)
        xn_s = sig("xn_ready", 4)
        ht_ps = sig("ht_in_psum", 16)
        hhi_s = sig("h_hi_ready", 16)
        hlo_s = sig("h_lo_ready", 16)
        rw_sc = sig("rw_scaled", 15)
        rw_sh = sig("rw_shifted", 15)
        lora_act = sig("lora_inputs_ready", 2)
        kksq_s = sig("kk_squared", 1)
        nrm_ps = sig("kk_norm_in_psum", 1)
        nrm_mx = sig("kk_norm_guarded", 1)
        nrm_rs = sig("kk_rnorm", 1)
        vt_ps = sig("v_tok_in_psum", 2)
        vt_s = sig("v_tok_ready", 2)
        rnt_ps = sig("rnorm_t_in_psum", 1)
        rnt_s = sig("rnorm_t_ready", 1)
        kkn_ps = sig("rnorm_spread_in_psum", 2)
        kk_s = sig("kk_ready", 2)
        lora_ps = sig("lora_in_psum", 8)
        lora_th = sig("lora_tanh", 4)
        cum_s = sig("cum_ready", 2)
        exp_s = sig("exps_ready", 6)
        kr_s = sig("kr_ready", 2)
        khb_s = sig("khat_bhat_ready", 4)
        tok_ps = sig("hat_tok_in_psum", 8)
        tok_s = sig("hat_tok_ready", 8)
        st_zero = sig("state_cleared", 2)
        bq_ps = sig("bq_in_psum", 16)
        bq_s = sig("bq_masked", 16)
        a_ps = sig("a_in_psum", 8)
        kq_ps = sig("kq_in_psum", 16)
        kq_s = sig("kq_masked", 16)
        x_up = sig("x_updated", 8 * 5)
        xt_init = sig("xt_started", 8)
        xt_up = sig("xt_updated", 8 * 5)
        zl_ps = sig("z_in_psum", 8 * 5)
        zl_s = sig("z_ready", 8 * 5)
        xz_ps = sig("xz_in_psum", 8 * 4)
        zx_ps = sig("zx_in_psum", 8 * 5)
        r_ps = sig("rhs_in_psum", 8)
        r_s = sig("rhs_ready", 8)
        u_ps = sig("u_in_psum", 8)
        u_s = sig("u_ready", 8)
        st_ps = sig("state_in_psum", 8)
        st_s = sig("state_ready", 8)
        y_ps = sig("y_in_psum", 4)
        y0_s = sig("y_copied", 2)
        y1_s = sig("y_added", 2)
        gn_var = sig("gn_var", 1)
        gn_rs = sig("gn_rstd", 1)
        yn_s = sig("yn_ready", 1)
        yt_ps = sig("yt_in_psum", 2)
        bon_in = sig("bonus_in", 1)
        bon_ps = sig("bonus_in_psum", 2)
        gd_s = sig("gd_ready", 1)
        g_ps = sig("g_in_psum", 2)
        yl_s = sig("y_affine", 2)
        yo_s = sig("y_gated", 2)
        yhi_s = sig("y_hi_ready", 1)
        ylo_s = sig("y_lo_ready", 1)
        cc_s = sig("c_gate_ready", 4)
        cv_s = sig("cv_ready", 4)
        cvhi_s = sig("cv_hi_ready", 4)
        cvlo_s = sig("cv_lo_ready", 4)
        at_ps = sig("qkv_in_psum", 2)
        at_s = sig("qkv_ready", 4)
        qss_s = sig("q_meansq", 1)
        qrs_s = sig("q_rstd", 1)
        rope_s = sig("roped", 2)
        qt_ps = sig("qt_in_psum", 3)
        qt_s = sig("qt_ready", 3)
        sc_ps = sig("scores_in_psum", 8)
        mx_s = sig("max_ready", 8)
        pe_s = sig("exp_ready", 8)
        pn_s = sig("prob_ready", 8)
        pt_ps = sig("pt_in_psum", 8)
        pt_s = sig("pt_ready", 8)
        o_ps = sig("o_in_psum", 8)
        ohi_s = sig("o_hi_ready", 2)
        olo_s = sig("o_lo_ready", 2)
        g3_s = sig("gate_tanh", 24)
        mg_s = sig("merged", 8)
        mhi_s = sig("m_hi_ready", 8)
        mlo_s = sig("m_lo_ready", 8)
        rl_s = sig("relu_ready", 16)
        us_s = sig("u_squared", 16)
        uhi_s = sig("u_hi_ready", 16)
        ulo_s = sig("u_lo_ready", 16)
        dve_step = sem("dve_step")
        pool_step = sem("pool_step")

        block = ctx.enter_context(nc.Block())
        tiles_of = ((0, 1), (1, 0))
        MLP_BODY = 12


        def level_mask(d, i):
            return con("level", P, (d * len(LEVELS) + i) * P).unsqueeze(1).to_broadcast([P, 4, P])

        def incl_mask(d):
            return con("incl", 2 * P, d * 2 * P).unsqueeze(1).to_broadcast([P, 2, 2 * P])

        ident4 = ident.unsqueeze(1).to_broadcast([P, 4, P])

        @block.sync
        def _(sp):
            sp.dma_start(x[:, :, :], x_in.rearrange("(t p) d -> p t d", p=P)).then_inc(x_in_s, 16)
            sp.dma_start(cst[:, :], consts).then_inc(consts_in, 16)
            with sp.Fori(0, DEPTH) as l:
                sp.wait_ge(*lo_ready.after(l, 0))
                sp.dma_start(raw[:, 0, :], stream[l, 0]).then_inc(landed[0], 16)
                sp.wait_ge(*x_new.after(l, 0))
                sp.dma_start(par[:, :], params[l]).then_inc(pars_in, 16)
                sp.dma_start(raw[:, 1, :], stream[l, 1]).then_inc(landed[1], 16)
                sp.dma_start(lor[:, :, :], lora[l]).then_inc(lora_in, 16)
                sp.dma_start(gain[:, :], gains[l].partition_broadcast(P)).then_inc(gains_in, 16)
                with sp.Fori(1, CHUNKS // 2) as c:
                    for s in range(2):
                        sp.wait_ge(lo_ready.sem, l * UNITS + c * (2 * CHUNK) + CHUNK * (s - 1))
                        sp.dma_start(raw[:, s, :], stream[l, c * 2 + s]).then_inc(landed[s], 16)
                sp.wait_ge(*lo_ready.after(l, CHUNK * (CHUNKS - 2)))
                sp.dma_start(raw[:, 0, :], stream[l, CHUNKS - 1]).then_inc(landed[0], 16)
            sp.wait_ge(x_new.sem, DEPTH * x_new.per)
            sp.dma_start(out.rearrange("(t p) d -> p t d", p=P), x[:, :, :]).then_inc(out_s, 16)
            sp.wait_ge(out_s, 16)

        @block.gpsimd
        def _(pool):
            pool.memset(mhalf[:, :], -0.5).then_inc(half_s, 1)
            pool.wait_ge(half_s, 1)
            pool.wait_ge(consts_in, 16)
            with pool.Fori(0, DEPTH) as l:
                def lo(u, it=0):
                    s, c, k = u % RING, (u // CHUNK) % 2, u % CHUNK
                    pool.wait_ge(*hi_ready.after(l, it * MLP_BODY + u + 1))
                    pool.tensor_tensor(w_lo[:, s, :], raw[:, c, k * UNIT:(k + 1) * UNIT],
                                       w_hi[:, s, :].bitcast(F32), ALU.subtract).then_inc(lo_ready.sem, 1)

                def rsqrt(o, i, n):
                    return pool.tensor_tensor(o, i, mhalf[:, 0:n], ALU.pow)

                pool.wait_ge(*meansq.after(l, 1))
                rsqrt(rstd[:, :], mean2[:, :], 2).then_inc(rstd_s.sem, 1)
                for u in range(U_CV + RING):
                    lo(u)
                pool.wait_ge(*nrm_mx.after(l, 1))
                rsqrt(small[:, 1, :], small[:, 0, :], 16).then_inc(nrm_rs.sem, 1)
                step = 0
                for g in range(4):
                    for e in range(2):
                        v = xt[:, 4 * e:4 * e + 4, :]
                        pool.wait_ge(*bq_s.after(l, 4 * g + 3 + e))
                        if g:
                            pool.wait_ge(*u_ps.after(l, 2 * g))
                        pool.tensor_tensor(v, bq[:, 4 * e:4 * e + 4, 0, :], level_mask(1 - g // 2, 0),
                                           ALU.mult).then_inc(pool_step, 1)
                        step += 1
                        pool.wait_ge(pool_step, step)
                        pool.tensor_tensor(v, v, ident4, ALU.add).then_inc(xt_init.sem, 1)
                pool.wait_ge(*gn_var.after(l, 1))
                rsqrt(small[:, 3, :], small[:, 2, :], 16).then_inc(gn_rs.sem, 1)
                for u in range(U_CV + RING, U_GATE):
                    lo(u)
                pool.wait_ge(*qss_s.after(l, 1))
                rsqrt(a_st[:, 1, :], a_st[:, 0, :], 20).then_inc(qrs_s.sem, 1)
                for u in range(U_GATE, U_MLP + RING):
                    lo(u)
                pool.wait_ge(*meansq.after(l, 2))
                rsqrt(rstd[:, :], mean2[:, :], 2).then_inc(rstd_s.sem, 1)
                for u in range(U_MLP + RING, U_MLP + 2 + MLP_BODY):
                    lo(u)
                with pool.Fori(1, 5) as it:
                    for u in range(U_MLP + 2, U_MLP + 2 + MLP_BODY):
                        lo(u, it)
                for u in range(UNITS - 2, UNITS):
                    lo(u)
                pool.sem_clear(pool_step)

        @block.scalar
        def _(act):
            act.wait_ge(consts_in, 16)
            act.wait_ge(x_in_s, 16)
            with act.Fori(0, DEPTH) as l:
                def split(u, it=0):
                    s, c, k = u % RING, (u // CHUNK) % 2, u % CHUNK
                    if k == 0:
                        act.wait_ge(landed[c], (l * LANDS[c] + it * (MLP_BODY // CHUNK // 2)
                                                + (u // CHUNK // 2 + 1)) * 16)
                    act.wait_ge(*unit_used.after(l, it * MLP_BODY + u + 1 - RING if u >= RING else 0))
                    act.activation(w_hi[:, s, :], raw[:, c, k * UNIT:(k + 1) * UNIT],
                                   ACT.Copy).then_inc(hi_ready.sem, 1)

                def norm(n, xn):
                    act.wait_ge(*x_new.after(l, 4 * n))
                    for t in range(NT):
                        act.activation(xn[:, t, :], x[:, t, :], ACT.Square,
                                       accum_out=stat[:, t:t + 1]).then_inc(sumsq.sem, 1)
                    if n == 0:
                        for u in range(3):
                            split(u)
                    act.wait_ge(*rstd_s.after(l, n + 1))
                    for t in range(NT):
                        act.activation(xn[:, t, :], x[:, t, :], ACT.Identity,
                                       scale=rstd[:, t:t + 1]).then_inc(xn_s.sem, 1)
                    if n == 0:
                        act.wait_ge(pars_in, (l + 1) * 16)
                        for u in range(3, RING):
                            split(u)
                    for k in range(KT):
                        act.wait_ge(*ht_ps.after(l, KT * n + k + 1))
                        act.activation(h_hi[:, k, :], bank[k][:, 0:SEQ], ACT.Identity,
                                       scale=par_of(f"norm{n + 1}_g", k)).then_inc(hhi_s.sem, 1)

                norm(0, xn1)

                act.wait_ge(*derived.after(l, 1))
                for u in range(U_CV):
                    act.wait_ge(*unit_used.after(l, u + 1))
                    act.activation(z[:, u, :], bank[u % 4][:, 0:SEQ], ACT.Identity,
                                   scale=der[:, D_MU + u:D_MU + u + 1]).then_inc(rw_sc.sem, 1)
                    split(u + RING)
                act.wait_ge(*rw_sh.after(l, 15))
                act.activation(z[:, 12, :], z[:, 12, :], ACT.Tanh).then_inc(lora_act.sem, 1)
                act.activation(z[:, 14, :], z[:, 14, :], ACT.Tanh, scale=0.5).then_inc(lora_act.sem, 1)
                for t in range(NT):
                    act.wait_ge(*vt_ps.after(l, t + 1))
                    act.activation(v_tok[:, t, :], bank[5 + t][:, :], ACT.Copy).then_inc(vt_s.sem, 1)

                for d in range(2):
                    if d:
                        act.wait_ge(*st_ps.after(l, 4))
                        act.wait_ge(*y_ps.after(l, 2))
                    for part, th in enumerate((lw, a_t)):
                        if part and not d:
                            act.wait_ge(*rnt_ps.after(l, 1))
                            act.activation(rn_t[:, :], bank[7][0:8, 0:SEQ], ACT.Copy).then_inc(rnt_s.sem, 1)
                        for j in range(JT):
                            if j % 2 == 0:
                                act.wait_ge(*lora_ps.after(l, 4 * d + 2 * part + j // 2 + 1))
                            at = (D_W0, D_A0)[part] + JT * d + j
                            ins = act.activation(th[:, j, :], bank[2 * part + j // 2][:, (j % 2) * SEQ:(j % 2 + 1) * SEQ],
                                                 ACT.Tanh, scale=0.5, bias=der[:, at:at + 1])
                        ins.then_inc(lora_th.sem, 1)
                    act.wait_ge(*cum_s.after(l, d + 1))
                    act.activation(e_cum[:, :, :], cum[:, :, :], ACT.Exp).then_inc(exp_s.sem, 1)
                    act.activation(lw[:, :, :], lw[:, :, :], ACT.Exp).then_inc(exp_s.sem, 1)
                    act.activation(cum[:, :, :], cum[:, :, :], ACT.Exp, scale=-1.0).then_inc(exp_s.sem, 1)
                    for i, (o, t) in enumerate(((kh_tok, 0), (kh_tok, 1), (bh_tok, 0), (bh_tok, 1))):
                        act.wait_ge(*tok_ps.after(l, 4 * d + i + 1))
                        act.activation(o[:, t, :], bank[4 + i][:, :], ACT.Copy).then_inc(tok_s.sem, 1)
                    for i, t in enumerate(tiles_of[d]):
                        g = 2 * d + i
                        for ci, c in enumerate(tiles_of[d]):
                            n, q = 2 * g + ci, C * c
                            act.wait_ge(*r_ps.after(l, n + 1))
                            act.activation(r_b[q:q + C, :], bank[6][q:q + C, :], ACT.Copy).then_inc(r_s.sem, 1)
                            act.wait_ge(*u_ps.after(l, n + 1))
                            act.activation(u_b[q:q + C, :], bank[7][q:q + C, :], ACT.Copy,
                                           scale=-1.0).then_inc(u_s.sem, 1)
                        if d == 0:
                            act.wait_ge(*y_ps.after(l, g + 1))
                            act.activation(y_tok[:, t, :], bank[0][:, :], ACT.Copy).then_inc(y0_s.sem, 1)
                for j in range(JT):
                    if j % 2 == 0:
                        act.wait_ge(*yt_ps.after(l, j // 2 + 1))
                    ins = act.activation(e_cum[:, j, :], bank[j // 2][:, (j % 2) * SEQ:(j % 2 + 1) * SEQ], ACT.Identity,
                                         scale=par_of("ln_g", j), bias=par_of("ln_b", j))
                    if j % 2:
                        ins.then_inc(yl_s.sem, 1)
                act.wait_ge(*yo_s.after(l, 2))
                act.activation(y_hi[:, :, :], kh[:, :, :], ACT.Copy).then_inc(yhi_s.sem, 1)

                act.wait_ge(*ylo_s.after(l, 1))
                for i in range(JT):
                    b0 = 2 + 3 * (i % 2)
                    act.wait_ge(*unit_used.after(l, U_CV + 3 * i + 2))
                    act.activation(cc[:, i % 2, :], bank[b0 + 1][:, 0:SEQ], ACT.Copy).then_inc(cc_s.sem, 1)
                    for s in range(3):
                        split(U_CV + 3 * i + s + RING)
                    act.wait_ge(*cv_s.after(l, i + 1))
                    act.activation(yb_hi[:, i, :], cv[:, i % 2, :], ACT.Copy).then_inc(cvhi_s.sem, 1)

                for a in range(2):
                    for t in range(NT):
                        act.wait_ge(*(unit_used.after(l, U_AT + 3 * a + 3) if t else at_ps.after(l, a + 1)))
                        act.activation(qkv[:, t, a * 384:(a + 1) * 384], bank[2 * a + t][:, 0:384],
                                       ACT.Copy).then_inc(at_s.sem, 1)
                    for s in range(3):
                        split(U_AT + 3 * a + s + RING)
                for i in range(2):
                    act.wait_ge(*qt_ps.after(l, i + 1))
                    act.activation(q_t[:, 2 * i:2 * i + 2, :].rearrange("p a b -> p (a b)"), bank[4 + i][:, :],
                                   ACT.Copy, scale=HD ** -0.5).then_inc(qt_s.sem, 1)
                act.wait_ge(*qt_ps.after(l, 3))
                act.activation(k_t[:, :], bank[6][:, 0:SEQ], ACT.Copy).then_inc(qt_s.sem, 1)

                def exps(i):
                    b = i % 2 + 2 * (i // 2 % 2)
                    act.wait_ge(*mx_s.after(l, i + 1))
                    if i >= 2:
                        act.wait_ge(*pt_ps.after(l, i - 1))
                    for t in range(NT):
                        ins = act.activation(prob[:, i % 2, t, :], bank[b][:, t * SEQ:(t + 1) * SEQ], ACT.Exp,
                                             bias=nmx[:, i, t:t + 1], accum_out=rsum[:, i, t:t + 1])
                    ins.then_inc(pe_s.sem, 1)

                exps(0)
                exps(1)
                for i in range(H):
                    act.wait_ge(*pt_ps.after(l, i + 1))
                    if i >= 2:
                        act.wait_ge(*o_ps.after(l, i - 1))
                    act.activation(p_t[:, i % 2, :, :].rearrange("p a b -> p (a b)"), bank[4 + i % 2][:, :],
                                   ACT.Copy).then_inc(pt_s.sem, 1)
                    if i + 2 < H:
                        exps(i + 2)
                act.wait_ge(*o_ps.after(l, H))
                for b in range(2):
                    act.activation(yb_hi[:, JT + 2 * b:JT + 2 * b + 2, :].rearrange("p a b -> p (a b)"),
                                   bank[6 + b][:, :], ACT.Copy).then_inc(ohi_s.sem, 1)

                for i in range(4):
                    u0 = U_GATE + 9 * i
                    if i:
                        act.wait_ge(*mg_s.after(l, 2 * i))
                    for k in range(6):
                        g = 6 * i + k
                        act.wait_ge(*unit_used.after(l, u0 + k + 1))
                        act.activation(gth[:, k // 3, k % 3, :], bank[g % 4][:, 0:SEQ], ACT.Tanh,
                                       scale=0.5).then_inc(g3_s.sem, 1)
                        split(u0 + k + RING)
                    for k in range(6, 9):
                        split(u0 + k + RING)
                    for k in range(2):
                        act.wait_ge(*mg_s.after(l, 2 * i + k + 1))
                        act.activation(m_hi[:, 2 * i + k, :], gmul[:, k, 0, :], ACT.Copy,
                                       scale=0.5).then_inc(mhi_s.sem, 1)
                for k in range(KT):
                    split(U_OUT + k + RING)

                norm(1, xn2)

                def square(p, it=0):
                    s = p % 3
                    act.wait_ge(*unit_used.after(l, it * MLP_BODY + U_MLP + (4 * p if p else 2)))
                    act.activation(relu[:, s, :], bank[4 + s][:, :], ACT.Relu).then_inc(rl_s.sem, 1)

                def round_u(p, it=0):
                    s = p % 3
                    act.wait_ge(*us_s.after(l, 3 * it + p + 1))
                    act.activation(u_hi[:, s, :, :].rearrange("p a b -> p (a b)"), usq[:, s, :],
                                   ACT.Copy).then_inc(uhi_s.sem, 1)

                def pair(p, it=0):
                    u0 = U_MLP + 2 + 4 * (p - 1)
                    square(p, it)
                    for k in range(4):
                        if k == 2:
                            round_u(p, it)
                        if u0 + k + RING < UNITS:
                            split(u0 + k + RING, it)

                square(0)
                for k in range(2):
                    split(U_MLP + k + RING)
                round_u(0)
                for p in range(1, 4):
                    pair(p)
                with act.Fori(1, 4) as it:
                    for p in range(1, 4):
                        pair(p, it)
                for p in range(13, 16):
                    pair(p)

        @block.vector
        def _(dve):
            dve.wait_ge(consts_in, 16)
            with dve.Fori(0, DEPTH) as l:
                count = [0]

                def then(ins):
                    count[0] += 1
                    ins.then_inc(dve_step, 1)
                    dve.wait_ge(dve_step, count[0])

                def norm(n):
                    dve.wait_ge(*sumsq.after(l, 2 * n + 2))
                    dve.tensor_scalar(mean2[:, :], stat[:, :], 1.0 / D, EPS, ALU.mult, ALU.add).then_inc(meansq.sem, 1)
                    if n == 0:
                        derive()
                    for k in range(KT):
                        dve.wait_ge(*hhi_s.after(l, KT * n + k + 1))
                        dve.scalar_tensor_tensor(h_lo[:, k, :], bank[k][:, 0:SEQ], par_of(f"norm{n + 1}_g", k),
                                                 h_hi[:, k, :].bitcast(F32), ALU.mult,
                                                 ALU.subtract).then_inc(hlo_s.sem, 1)

                def derive():
                    dve.wait_ge(pars_in, (l + 1) * 16)
                    mp, mn = (par[:, PARAMS[k]:PARAMS[k] + 15] for k in ("mu_prev", "mu_next"))
                    mu = der[:, D_MU:D_MU + 15]
                    dve.tensor_scalar(der[:, D_W0:D_W0 + 16], par[:, PARAMS["w0"]:PARAMS["w0"] + 16], 0.5, None,
                                      ALU.mult)
                    dve.tensor_scalar(der[:, D_KA:D_KA + 4], par[:, PARAMS["k_a"]:PARAMS["k_a"] + 4], -1.0, 1.0,
                                      ALU.mult, ALU.add)
                    then(dve.tensor_tensor(mu, mp, mn, ALU.add))
                    dve.tensor_scalar(mu, mu, -1.0, 1.0, ALU.mult, ALU.add).then_inc(derived.sem, 1)

                norm(0)

                for u in range(U_CV):
                    ps = bank[u % 4]
                    dve.wait_ge(*rw_sc.after(l, u + 1))
                    then(dve.scalar_tensor_tensor(z[:, u, 1:SEQ], ps[:, 0:SEQ - 1], par_of("mu_prev", u),
                                                  z[:, u, 1:SEQ], ALU.mult, ALU.add))
                    dve.scalar_tensor_tensor(z[:, u, 0:SEQ - 1], ps[:, 1:SEQ], par_of("mu_next", u),
                                             z[:, u, 0:SEQ - 1], ALU.mult, ALU.add).then_inc(rw_sh.sem, 1)
                dve.wait_ge(*rw_sh.after(l, 15))
                for j in range(JT):
                    ins = dve.tensor_scalar(kk[:, j, :], z[:, 4 + j, :], par_of("k_k", j), None, ALU.mult)
                then(ins)
                dve.tensor_tensor(lw[:, :, :], kk[:, :, :], kk[:, :, :], ALU.mult).then_inc(kksq_s.sem, 1)
                dve.memset(state[:, :, :], 0.0).then_inc(st_zero.sem, 1)
                dve.wait_ge(*nrm_ps.after(l, 1))
                dve.tensor_scalar(small[:, 0, :], bank[4][:, 0:16], 1e-24, None, ALU.max).then_inc(nrm_mx.sem, 1)
                dve.wait_ge(*lora_act.after(l, 2))
                dve.tensor_scalar(z[:, 14, :], z[:, 14, :], 0.5, 0.5, ALU.mult, ALU.add).then_inc(gd_s.sem, 1)

                for d in range(2):
                    dve.wait_ge(*lora_th.after(l, 2 * d + 1))
                    then(dve.tensor_scalar(lw[:, :, :], lw[:, :, :], -DECAY / 2, -DECAY / 2, ALU.mult, ALU.add))
                    for j in range(JT):
                        reset = con("reset", SEQ, d * SEQ)
                        o, i = cum[:, j, :], lw[:, j, :]
                        if d:
                            reset, o, i = reset[:, ::-1], o[:, ::-1], i[:, ::-1]
                        ins = dve.tensor_tensor_scan(o, reset, i, 0.0, ALU.mult, ALU.add)
                    then(ins)
                    dve.tensor_tensor(lw[:, :, :], cum[:, :, :], lw[:, :, :], ALU.subtract).then_inc(cum_s.sem, 1)
                    dve.wait_ge(*lora_th.after(l, 2 * d + 2))
                    then(dve.tensor_scalar(a_t[:, :, :], a_t[:, :, :], 0.5, 0.5, ALU.mult, ALU.add))
                    for j in range(JT):
                        ins = dve.tensor_scalar(bh[:, j, :], a_t[:, j, :], par_of("k_a", j),
                                                der[:, D_KA + j:D_KA + j + 1], ALU.mult, ALU.add)
                    then(ins)
                    then(dve.tensor_tensor(bh[:, :, :], bh[:, :, :], z[:, 4:8, :], ALU.mult))
                    if d == 0:
                        dve.tensor_copy(ksum[:, :, :], bh[:, :, :])
                        for i in range(2):
                            dve.wait_ge(*kkn_ps.after(l, i + 1))
                            v = kk[:, 2 * i:2 * i + 2, :].rearrange("p a b -> p (a b)")
                            dve.tensor_tensor(v, v, bank[4 + i][:, :], ALU.mult).then_inc(kk_s.sem, 1)
                        dve.wait_ge(*kk_s.after(l, 2))
                    else:
                        dve.tensor_tensor(ksum[:, :, :], ksum[:, :, :], bh[:, :, :], ALU.add)
                    then(dve.tensor_tensor(a_t[:, :, :], kk[:, :, :], a_t[:, :, :], ALU.mult))
                    dve.wait_ge(*exp_s.after(l, 3 * d + 1))
                    dve.tensor_tensor(kr[:, :, 1, :], z[:, 0:4, :], e_cum[:, :, :], ALU.mult)
                    dve.wait_ge(*exp_s.after(l, 3 * d + 2))
                    dve.tensor_tensor(kr[:, :, 0, :], kk[:, :, :], lw[:, :, :], ALU.mult).then_inc(kr_s.sem, 1)
                    dve.wait_ge(*exp_s.after(l, 3 * d + 3))
                    dve.tensor_tensor(kh[:, :, :], bh[:, :, :], cum[:, :, :], ALU.mult).then_inc(khb_s.sem, 1)
                    dve.wait_ge(*khb_s.after(l, 2 * d + 1))
                    dve.tensor_tensor(bh[:, :, :], a_t[:, :, :], cum[:, :, :], ALU.mult).then_inc(khb_s.sem, 1)

                    if d:
                        dve.wait_ge(*y_ps.after(l, 2))
                        dve.memset(state[:, :, :], 0.0).then_inc(st_zero.sem, 1)
                    for i, t in enumerate(tiles_of[d]):
                        g = 2 * d + i
                        if g:
                            dve.wait_ge(*y_ps.after(l, g))
                        for m in range(4):
                            at = 4 * (m % 2) + 2 * (m // 2)
                            dve.wait_ge(*bq_ps.after(l, 4 * g + m + 1))
                            dve.tensor_tensor(bq[:, at:at + 2, :, :].rearrange("p a b c -> p a (b c)"),
                                              bank[m][:, :].rearrange("p (a b) -> p a b", a=2), incl_mask(d),
                                              ALU.mult).then_inc(bq_s.sem, 1)
                        for e in range(2):
                            v = xm[:, 4 * e:4 * e + 4, :]
                            dve.wait_ge(*a_ps.after(l, 2 * g + e + 1))
                            then(dve.tensor_tensor(v, bank[4 + e][:, :].rearrange("p (a b) -> p a b", a=4),
                                                   level_mask(d, 0), ALU.mult))
                            dve.tensor_tensor(v, v, ident4, ALU.add).then_inc(x_up.sem, 1)
                        for m in range(4):
                            at = 4 * (m % 2) + 2 * (m // 2)
                            dve.wait_ge(*kq_ps.after(l, 4 * g + m + 1))
                            dve.tensor_tensor(kq[:, at:at + 2, :, :].rearrange("p a b c -> p a (b c)"),
                                              bank[6 + m % 2][:, :].rearrange("p (a b) -> p a b", a=2), incl_mask(d),
                                              ALU.mult).then_inc(kq_s.sem, 1)
                        for li in range(5):
                            for e in range(2):
                                dve.wait_ge(*zl_ps.after(l, 10 * g + 2 * li + e + 1))
                                dve.tensor_tensor(zm[:, 4 * e:4 * e + 4, :],
                                                  bank[e][:, :].rearrange("p (a b) -> p a b", a=4),
                                                  level_mask(d, li + 1), ALU.mult).then_inc(zl_s.sem, 1)
                            for e in range(2):
                                if li < 4:
                                    v = xm[:, 4 * e:4 * e + 4, :].rearrange("p a b -> p (a b)")
                                    dve.wait_ge(*x_up.after(l, 10 * g + 2 * li + e + 1))
                                    dve.wait_ge(*xz_ps.after(l, 8 * g + 2 * li + e + 1))
                                    dve.tensor_tensor(v, v, bank[2 + e][:, :], ALU.add).then_inc(x_up.sem, 1)
                                v = xt[:, 4 * e:4 * e + 4, :].rearrange("p a b -> p (a b)")
                                if li:
                                    dve.wait_ge(*xt_up.after(l, 10 * g + 2 * li + e - 1))
                                dve.wait_ge(*zx_ps.after(l, 10 * g + 2 * li + e + 1))
                                dve.tensor_tensor(v, v, bank[4 + e][:, :], ALU.add).then_inc(xt_up.sem, 1)
                        for ci, c in enumerate(tiles_of[d]):
                            n = 2 * g + ci
                            last = t * P + c * C + (0 if d else C - 1)
                            dve.wait_ge(*st_ps.after(l, n + 1))
                            for e in range(2):
                                r = slice(HD * e, HD * (e + 1))
                                ins = dve.tensor_tensor(s_new[r, :, :], state[r, :, HD * e:HD * (e + 1)],
                                                        bank[1][r, 0:JT * HD].rearrange("p (a b) -> p a b", a=JT),
                                                        ALU.add)
                            then(ins)
                            for e in range(2):
                                r = slice(HD * e, HD * (e + 1))
                                ins = dve.tensor_tensor(state[r, :, HD * e:HD * (e + 1)], s_new[r, :, :],
                                                        e_cum[r, :, last:last + 1].to_broadcast([HD, JT, HD]), ALU.mult)
                            ins.then_inc(st_s.sem, 1)
                            dve.wait_ge(*st_s.after(l, n + 1))
                        if d:
                            dve.wait_ge(*y_ps.after(l, g + 1))
                            dve.tensor_tensor(y_tok[:, t, :], y_tok[:, t, :], bank[0][:, :],
                                              ALU.add).then_inc(y1_s.sem, 1)

                for j in range(JT):
                    ins = dve.scalar_tensor_tensor(cum[:, j, :], ksum[:, j, :], par_of("r_k", j), z[:, j, :],
                                                   ALU.mult, ALU.mult)
                ins.then_inc(bon_in.sem, 1)
                y3 = y_tok[:, :, :].rearrange("p t (h v) -> p (t h) v", v=HD)
                sq = lw[:, :, :].rearrange("p j (a v) -> p (j a) v", v=HD)
                spread = lambda i: small[:, i, :].unsqueeze(2).to_broadcast([P, 16, HD])
                dve.wait_ge(*y1_s.after(l, 2))
                then(dve.tensor_reduce(small[:, 0, :], y3, AX.X, ALU.add))
                then(dve.tensor_scalar(small[:, 0, :], small[:, 0, :], 1.0 / HD, None, ALU.mult))
                then(dve.tensor_tensor(y3, y3, spread(0), ALU.subtract))
                then(dve.tensor_tensor(sq, y3, y3, ALU.mult))
                then(dve.tensor_reduce(small[:, 2, :], sq, AX.X, ALU.add))
                dve.tensor_scalar(small[:, 2, :], small[:, 2, :], 1.0 / HD, LN_EPS, ALU.mult,
                                  ALU.add).then_inc(gn_var.sem, 1)
                dve.wait_ge(*gn_rs.after(l, 1))
                dve.tensor_tensor(y3, y3, spread(3), ALU.mult).then_inc(yn_s.sem, 1)
                for i in range(2):
                    js = slice(2 * i, 2 * i + 2)
                    flat = lambda t: t[:, js, :].rearrange("p a b -> p (a b)")
                    dve.wait_ge(*bon_ps.after(l, i + 1))
                    then(dve.tensor_tensor(flat(a_t), bank[4 + i][:, :], z[:, 8 + 2 * i:10 + 2 * i, :].rearrange(
                        "p a b -> p (a b)"), ALU.mult))
                    dve.wait_ge(*yl_s.after(l, i + 1))
                    then(dve.scalar_tensor_tensor(flat(e_cum), flat(a_t), 0.5, flat(e_cum), ALU.mult, ALU.add))
                    dve.wait_ge(*g_ps.after(l, i + 1))
                    dve.tensor_tensor(flat(kh), flat(e_cum), bank[6 + i][:, :], ALU.mult).then_inc(yo_s.sem, 1)
                dve.wait_ge(*yhi_s.after(l, 1))
                dve.tensor_tensor(y_lo[:, :, :], kh[:, :, :], y_hi[:, :, :].bitcast(F32),
                                  ALU.subtract).then_inc(ylo_s.sem, 1)
                dve.wait_ge(*ylo_s.after(l, 1))

                then(dve.memset(cz[:, :, 0:SEQ + 2:SEQ + 1], 0.0))
                for i in range(JT):
                    b0, s = 2 + 3 * (i % 2), i % 2
                    tap = lambda k: par_of("cv_w", 4 * k + i)
                    dve.wait_ge(*cc_s.after(l, i + 1))
                    dve.wait_ge(*unit_used.after(l, U_CV + 3 * i + 3))
                    then(dve.tensor_tensor(cz[:, s, 1:SEQ + 1], bank[b0 + 2][:, 0:SEQ], cc[:, s, :], ALU.mult))
                    then(dve.tensor_scalar(cv[:, s, :], cz[:, s, 0:SEQ], tap(0), par_of("cv_b", i), ALU.mult, ALU.add))
                    for k in (1, 2):
                        then(dve.scalar_tensor_tensor(cv[:, s, :], cz[:, s, k:SEQ + k], tap(k), cv[:, s, :],
                                                      ALU.mult, ALU.add))
                    dve.tensor_tensor(cv[:, s, :], cv[:, s, :], bank[b0][:, 0:SEQ], ALU.mult).then_inc(cv_s.sem, 1)
                    dve.wait_ge(*cvhi_s.after(l, i + 1))
                    dve.tensor_tensor(yb_lo[:, i, :], cv[:, s, :], yb_hi[:, i, :].bitcast(F32),
                                      ALU.subtract).then_inc(cvlo_s.sem, 1)

                NH = H + KV
                heads = lambda v: v.rearrange("p (h v) -> p h v", v=HD)
                dve.wait_ge(*at_s.after(l, 4))
                for t in range(NT):
                    ins = dve.tensor_tensor(q_sq[:, t, :], qkv[:, t, 0:NH * HD], qkv[:, t, 0:NH * HD], ALU.mult)
                then(ins)
                then(dve.tensor_reduce(a_st[:, 2, :], q_sq[:, :, :].rearrange("p t (h v) -> p (t h) v", v=HD),
                                       AX.X, ALU.add))
                dve.tensor_scalar(a_st[:, 0, :], a_st[:, 2, :], 1.0 / HD, EPS, ALU.mult, ALU.add).then_inc(qss_s.sem, 1)
                dve.wait_ge(*qrs_s.after(l, 1))
                dve.wait_ge(gains_in, (l + 1) * 16)
                for t in range(NT):
                    qn, q2, q3 = q_rt[:, t, :], q_sq[:, t, :], rot[:, t, :]
                    cos = con("rope_c", HD, t * HD).unsqueeze(1).to_broadcast([P, NH, HD])
                    sin = con("rope_s", HD, t * HD).rearrange("p (a b c) -> p a b c", a=2, b=2)
                    then(dve.tensor_tensor(heads(qn), heads(qkv[:, t, 0:NH * HD]),
                                           a_st[:, 1, t * NH:(t + 1) * NH].unsqueeze(2).to_broadcast([P, NH, HD]),
                                           ALU.mult))
                    then(dve.tensor_tensor(qn, qn, gain[:, :], ALU.mult))
                    dve.tensor_tensor(heads(q2), heads(qn), cos, ALU.mult)
                    for a in range(2):
                        for b in range(2):
                            pick = lambda v, b: v.rearrange("p (h a b c) -> p h a b c", a=2, b=2, c=16)[:, :, a, b, :]
                            ins = dve.tensor_tensor(pick(q3, b), pick(qn, 1 - b),
                                                    sin[:, a, b, :].unsqueeze(1).to_broadcast([P, NH, 16]), ALU.mult)
                    then(ins)
                    q4 = lambda v: v[:, 0:H * HD].rearrange("p (a m v) -> p a m v", a=KV, m=4)
                    dve.tensor_tensor(qn[:, 0:H * HD].rearrange("p (m a v) -> p a m v", a=KV, m=4), q4(q2), q4(q3),
                                      ALU.add)
                    dve.tensor_tensor(qn[:, H * HD:], q2[:, H * HD:], q3[:, H * HD:], ALU.add).then_inc(rope_s.sem, 1)

                def maxes(i):
                    b = i % 2 + 2 * (i // 2 % 2)
                    dve.wait_ge(*sc_ps.after(l, i + 1))
                    dve.tensor_reduce(nmx[:, i, :], bank[b][:, :].rearrange("p (t s) -> p t s", t=NT), AX.X, ALU.max,
                                      negate=True).then_inc(mx_s.sem, 1)

                for i in range(4):
                    maxes(i)
                for i in range(H):
                    dve.wait_ge(*pe_s.after(l, i + 1))
                    then(dve.reciprocal(rinv[:, i, :], rsum[:, i, :]))
                    for t in range(NT):
                        ins = dve.tensor_scalar(prob[:, i % 2, t, :], prob[:, i % 2, t, :], rinv[:, i, t:t + 1], None,
                                                ALU.mult)
                    ins.then_inc(pn_s.sem, 1)
                    if i + 4 < H:
                        maxes(i + 4)
                for b in range(2):
                    flat = lambda v: v[:, JT + 2 * b:JT + 2 * b + 2, :].rearrange("p a b -> p (a b)")
                    dve.wait_ge(*ohi_s.after(l, b + 1))
                    dve.tensor_tensor(flat(yb_lo), bank[6 + b][:, :], flat(yb_hi).bitcast(F32),
                                      ALU.subtract).then_inc(olo_s.sem, 1)

                for i in range(4):
                    dve.wait_ge(*unit_used.after(l, U_GATE + 9 * i + 9))
                    dve.wait_ge(*g3_s.after(l, 6 * i + 6))
                    if i:
                        dve.wait_ge(*mhi_s.after(l, 2 * i))
                        dve.wait_ge(*mlo_s.after(l, 2 * i))
                    for k in range(2):
                        flat = lambda v: v.rearrange("p a b -> p (a b)")
                        dve.scalar_tensor_tensor(flat(gmul[:, k, 0:2, :]), flat(gth[:, k, 0:2, :]), 1.0,
                                                 bank[4 + 2 * k][:, :], ALU.add, ALU.mult)
                        then(dve.scalar_tensor_tensor(gmul[:, k, 2, :], gth[:, k, 2, :], 1.0,
                                                      bank[5 + 2 * k][:, 0:SEQ], ALU.add, ALU.mult))
                        then(dve.tensor_tensor(gmul[:, k, 0, :], gmul[:, k, 0, :], gmul[:, k, 1, :], ALU.add))
                        dve.tensor_tensor(gmul[:, k, 0, :], gmul[:, k, 0, :], gmul[:, k, 2, :],
                                          ALU.add).then_inc(mg_s.sem, 1)
                    for k in range(2):
                        dve.wait_ge(*mhi_s.after(l, 2 * i + k + 1))
                        dve.scalar_tensor_tensor(m_lo[:, 2 * i + k, :], gmul[:, k, 0, :], 0.5,
                                                 m_hi[:, 2 * i + k, :].bitcast(F32), ALU.mult,
                                                 ALU.subtract).then_inc(mlo_s.sem, 1)

                def residual():
                    for t in range(NT):
                        for n in range(2):
                            v = x[:, t, n * 512:(n + 1) * 512]
                            dve.tensor_tensor(v, v, bank[2 * t + n][:, :], ALU.add).then_inc(x_new.sem, 1)

                dve.wait_ge(*unit_used.after(l, U_MLP))
                residual()
                norm(1)

                def square(p, it=0):
                    s = p % 3
                    dve.wait_ge(*rl_s.after(l, 3 * it + p + 1))
                    dve.tensor_tensor(usq[:, s, :], relu[:, s, :], bank[4 + s][:, :], ALU.mult).then_inc(us_s.sem, 1)
                    dve.wait_ge(*uhi_s.after(l, 3 * it + p + 1))
                    dve.tensor_tensor(u_lo[:, s, :, :].rearrange("p a b -> p (a b)"), usq[:, s, :],
                                      u_hi[:, s, :, :].rearrange("p a b -> p (a b)").bitcast(F32),
                                      ALU.subtract).then_inc(ulo_s.sem, 1)

                for p in range(4):
                    square(p)
                with dve.Fori(1, 4) as it:
                    for p in range(1, 4):
                        square(p, it)
                for p in range(13, 16):
                    square(p)
                dve.wait_ge(*unit_used.after(l, UNITS))
                dve.wait_ge(*x_new.after(l, 4))
                residual()
                dve.sem_clear(dve_step)

        @block.tensor
        def _(pe):
            pe.wait_ge(consts_in, 16)
            with pe.Fori(0, DEPTH) as l:
                def weights(u, it=0):
                    pe.wait_ge(*lo_ready.after(l, it * MLP_BODY + u + 1))

                def columns(o, s, tiles=KT, width=P, at=0, hi=h_hi, lo=h_lo, base=0, used=True):
                    for k in range(tiles):
                        c = slice(k * width + at, k * width + at + P)
                        pe.matmul(o, w_hi[:, s, c], hi[:, base + k, :], start=(k == 0), stop=False)
                        pe.matmul(o, w_hi[:, s, c], lo[:, base + k, :], start=False, stop=False)
                        ins = pe.matmul(o, w_lo[:, s, c], hi[:, base + k, :], start=False, stop=(k == tiles - 1))
                    if used:
                        ins.then_inc(unit_used.sem, 1)

                def norm(n, xn):
                    pe.wait_ge(*xn_s.after(l, 2 * n + 2))
                    for k in range(KT):
                        for t in range(NT):
                            ins = pe.transpose(bank[k][:, t * P:(t + 1) * P], xn[:, t, k * P:(k + 1) * P], ident)
                        ins.then_inc(ht_ps.sem, 1)

                norm(0, xn1)
                pe.wait_ge(*hlo_s.after(l, KT))
                for u in range(U_CV):
                    weights(u)
                    if u >= 4:
                        pe.wait_ge(*rw_sh.after(l, u - 3))
                    columns(bank[u % 4][:, 0:SEQ], u % RING)

                pe.wait_ge(*rw_sh.after(l, 12))
                for t in range(NT):
                    for j in range(JT):
                        ins = pe.transpose(bank[5 + t][:, j * P:(j + 1) * P], z[:, 8 + j, t * P:(t + 1) * P], ident)
                    ins.then_inc(vt_ps.sem, 1)
                pe.wait_ge(*kksq_s.after(l, 1))
                for t in range(NT):
                    for j in range(JT):
                        ins = pe.matmul(bank[4][:, t * H + 2 * j:t * H + 2 * j + 2], lw[:, j, t * P:(t + 1) * P],
                                        con("headsum", 2), start=True, stop=True)
                ins.then_inc(nrm_ps.sem, 1)

                def lora_products(d):
                    for part in range(2):
                        for j in range(JT):
                            ins = pe.matmul(bank[2 * part + j // 2][:, (j % 2) * SEQ:(j % 2 + 1) * SEQ],
                                            lor[HD * d:HD * (d + 1), part, j * P:(j + 1) * P],
                                            z[HD * d:HD * (d + 1), 12 + part, :], start=True, stop=True)
                            if j % 2:
                                ins.then_inc(lora_ps.sem, 1)

                for d in range(2):
                    if d == 0:
                        pe.wait_ge(lora_in, (l + 1) * 16)
                        pe.wait_ge(*lora_act.after(l, 1))
                        pe.wait_ge(*rw_sh.after(l, 15))
                    else:
                        pe.wait_ge(*y0_s.after(l, 2))
                        pe.wait_ge(*st_s.after(l, 4))
                    lora_products(d)
                    if d == 0:
                        pe.wait_ge(*nrm_rs.after(l, 1))
                        for t in range(NT):
                            ins = pe.transpose(bank[7][0:8, t * P:(t + 1) * P], small[:, 1, t * H:(t + 1) * H], ident)
                        ins.then_inc(rnt_ps.sem, 1)
                        pe.wait_ge(*rnt_s.after(l, 1))
                        pe.wait_ge(*vt_s.after(l, 2))
                        for j in range(JT):
                            ins = pe.matmul(bank[4 + j // 2][:, (j % 2) * SEQ:(j % 2 + 1) * SEQ],
                                            con("sel", P, j * P, rows=8), rn_t[:, :], start=True, stop=True)
                            if j % 2:
                                ins.then_inc(kkn_ps.sem, 1)
                    for i, src in enumerate((kh, bh)):
                        pe.wait_ge(*khb_s.after(l, 2 * d + i + 1))
                        for t in range(NT):
                            for j in range(JT):
                                ins = pe.transpose(bank[4 + 2 * i + t][:, j * P:(j + 1) * P],
                                                   src[:, j, t * P:(t + 1) * P], ident)
                            ins.then_inc(tok_ps.sem, 1)
                    for i, t in enumerate(tiles_of[d]):
                        g = 2 * d + i
                        tok = slice(t * P, (t + 1) * P)
                        pe.wait_ge(*kr_s.after(l, d + 1))
                        if i:
                            pe.wait_ge(*(y1_s.after(l, 1) if d else y0_s.after(l, 1)))
                            pe.wait_ge(*st_s.after(l, 2 * g))
                        for m in range(4):
                            e = slice(HD * (m % 2), HD * (m % 2 + 1))
                            for j in range(2):
                                jj = 2 * (m // 2) + j
                                ins = pe.matmul(bank[m][:, j * SEQ:(j + 1) * SEQ], bh[e, jj, tok], kr[e, jj, :, tok],
                                                start=True, stop=True)
                            ins.then_inc(bq_ps.sem, 1)
                        pe.wait_ge(*tok_s.after(l, 4 * d + 4))
                        for e in range(2):
                            r = slice(HD * e, HD * (e + 1))
                            for j in range(JT):
                                ins = pe.matmul(bank[4 + e][:, j * P:(j + 1) * P], kr[r, j, 0, tok], bh[r, j, tok],
                                                start=True, stop=True)
                            ins.then_inc(a_ps.sem, 1)
                        for m in range(4):
                            e = slice(HD * (m % 2), HD * (m % 2 + 1))
                            if m >= 2:
                                pe.wait_ge(*kq_s.after(l, 4 * g + m - 1))
                            for j in range(2):
                                jj = 2 * (m // 2) + j
                                ins = pe.matmul(bank[6 + m % 2][:, j * SEQ:(j + 1) * SEQ], kh[e, jj, tok],
                                                kr[e, jj, :, tok], start=True, stop=True)
                            ins.then_inc(kq_ps.sem, 1)
                        for li in range(5):
                            for e in range(2):
                                pe.wait_ge(*x_up.after(l, 10 * g + 2 * li + e + 1))
                                for j in range(JT):
                                    a = 4 * e + j
                                    ins = pe.matmul(bank[e][:, j * P:(j + 1) * P], bq[:, a, 0, :], xm[:, a, :],
                                                    start=True, stop=True)
                                ins.then_inc(zl_ps.sem, 1)
                            for e in range(2):
                                pe.wait_ge(*zl_s.after(l, 10 * g + 2 * li + e + 1))
                                if li:
                                    pe.wait_ge(*xt_up.after(l, 10 * g + 2 * li + e - 1))
                                else:
                                    pe.wait_ge(*xt_init.after(l, 2 * g + e + 1))
                                if li < 4:
                                    for j in range(JT):
                                        a = 4 * e + j
                                        ins = pe.matmul(bank[2 + e][:, j * P:(j + 1) * P], xt[:, a, :], zm[:, a, :],
                                                        start=True, stop=True)
                                    ins.then_inc(xz_ps.sem, 1)
                                for j in range(JT):
                                    a = 4 * e + j
                                    ins = pe.matmul(bank[4 + e][:, j * P:(j + 1) * P], zm[:, a, :], xt[:, a, :],
                                                    start=True, stop=True)
                                ins.then_inc(zx_ps.sem, 1)

                        def at(h):
                            return 4 * (h % 2) + h // 2

                        pe.wait_ge(*kq_s.after(l, 4 * g + 4))
                        for k, b in ((0, 6), (1, 0)):
                            for h in range(H):
                                pe.matmul(bank[b][:, h * HD:(h + 1) * HD], kq[:, at(h), k, :],
                                          v_tok[:, t, h * HD:(h + 1) * HD], start=(h == 0), stop=False,
                                          skip_group_check=True)
                        pe.wait_ge(*(st_s.after(l, 2 * g) if i else st_zero.after(l, d + 1)))
                        for ci, c in enumerate(tiles_of[d]):
                            n = 2 * g + ci
                            r = slice(C * c, C * (c + 1))
                            here = slice(t * P + C * c, t * P + C * (c + 1))
                            if ci:
                                pe.wait_ge(*st_s.after(l, n))
                            for k, b in ((0, 6), (1, 0)):
                                for j in range(JT):
                                    ins = pe.matmul(bank[b][r, j * P:(j + 1) * P], kr[:, j, k, here], state[:, j, :],
                                                    start=False, stop=(k == 0), skip_group_check=True)
                                if k == 0:
                                    ins.then_inc(r_ps.sem, 1)
                            for h in range(H):
                                e = slice(HD * (h % 2), HD * (h % 2 + 1))
                                v = slice(h * HD, (h + 1) * HD)
                                pe.matmul(bank[1][e, h // 2 * HD:(h // 2 + 1) * HD], kh_tok[r, t, v], v_tok[r, t, v],
                                          start=(h < 2), stop=False, skip_group_check=True)
                            pe.wait_ge(*xt_up.after(l, 10 * g + 10))
                            pe.wait_ge(*r_s.after(l, n + 1))
                            for h in range(H):
                                v = slice(h * HD, (h + 1) * HD)
                                ins = pe.matmul(bank[7][r, v], xt[:, at(h), r], r_b[:, v], start=True, stop=True)
                            ins.then_inc(u_ps.sem, 1)
                            pe.wait_ge(*u_s.after(l, n + 1))

                            def own(h):
                                v = slice(h * HD, (h + 1) * HD)
                                return pe.matmul(bank[0][r, v], bq[:, at(h), 1, r], u_b[:, v], start=False, stop=True,
                                                 skip_group_check=True)

                            own(0)
                            for h in range(H):
                                e = slice(HD * (h % 2), HD * (h % 2 + 1))
                                v = slice(h * HD, (h + 1) * HD)
                                ins = pe.matmul(bank[1][e, h // 2 * HD:(h // 2 + 1) * HD], bh_tok[r, t, v], u_b[r, v],
                                                start=False, stop=True, skip_group_check=True)
                            ins.then_inc(st_ps.sem, 1)
                            for h in range(1, H):
                                ins = own(h)
                        ins.then_inc(y_ps.sem, 1)

                pe.wait_ge(*bon_in.after(l, 1))
                for j in range(JT):
                    ins = pe.matmul(bank[4 + j // 2][:, (j % 2) * SEQ:(j % 2 + 1) * SEQ], con("ones", P), cum[:, j, :],
                                    start=True, stop=True)
                    if j % 2:
                        ins.then_inc(bon_ps.sem, 1)
                pe.wait_ge(*gd_s.after(l, 1))
                for j in range(JT):
                    ins = pe.matmul(bank[6 + j // 2][:, (j % 2) * SEQ:(j % 2 + 1) * SEQ], lor[:, 2, j * P:(j + 1) * P],
                                    z[:, 14, :], start=True, stop=True)
                    if j % 2:
                        ins.then_inc(g_ps.sem, 1)
                pe.wait_ge(*yn_s.after(l, 1))
                for j in range(JT):
                    for t in range(NT):
                        ins = pe.transpose(bank[j // 2][:, (j % 2) * SEQ + t * P:(j % 2) * SEQ + (t + 1) * P],
                                           y_tok[:, t, j * P:(j + 1) * P], ident)
                    if j % 2:
                        ins.then_inc(yt_ps.sem, 1)

                pe.wait_ge(*yo_s.after(l, 2))
                for i in range(JT):
                    if i >= 2:
                        pe.wait_ge(*cv_s.after(l, i - 1))
                    for s in range(3):
                        u = U_CV + 3 * i + s
                        weights(u)
                        columns(bank[2 + 3 * (i % 2) + s][:, 0:SEQ], u % RING)
                for a in range(2):
                    s0 = (U_AT + 3 * a) % RING
                    hi, lo = (w[:, s0:s0 + 3, :].rearrange("p a b -> p (a b)") for w in (w_hi, w_lo))
                    weights(U_AT + 3 * a + 2)
                    if a:
                        pe.wait_ge(*cv_s.after(l, 3))
                    for t in range(NT):
                        tok = slice(t * P, (t + 1) * P)
                        o = bank[2 * a + t][:, 0:384]
                        for k in range(KT):
                            c = slice(k * 384, (k + 1) * 384)
                            pe.matmul(o, h_hi[:, k, tok], hi[:, c], start=(k == 0), stop=False)
                            pe.matmul(o, h_hi[:, k, tok], lo[:, c], start=False, stop=False)
                            ins = pe.matmul(o, h_lo[:, k, tok], hi[:, c], start=False, stop=(k == KT - 1))
                        if t == 0:
                            ins.then_inc(at_ps.sem, 1)
                        else:
                            ins.then_inc(unit_used.sem, 3)
                pe.wait_ge(*rope_s.after(l, NT))
                for m in range(4):
                    for t in range(NT):
                        ins = pe.transpose(bank[4 + m // 2][:, (m % 2) * SEQ + t * P:(m % 2) * SEQ + (t + 1) * P],
                                           q_rt[:, t, m * P:(m + 1) * P], ident)
                    if m % 2:
                        ins.then_inc(qt_ps.sem, 1)
                for t in range(NT):
                    ins = pe.transpose(bank[6][:, t * P:(t + 1) * P], q_rt[:, t, H * HD:H * HD + P], ident)
                ins.then_inc(qt_ps.sem, 1)

                def scores(i):
                    m, e = i // 2, slice(HD * (i % 2), HD * (i % 2 + 1))
                    if i >= 4:
                        pe.wait_ge(*pe_s.after(l, i - 3))
                    for t in range(NT):
                        ins = pe.matmul(bank[i % 2 + 2 * (m % 2)][:, t * SEQ:(t + 1) * SEQ],
                                        q_t[e, m, t * P:(t + 1) * P], k_t[e, :], start=True, stop=True)
                    ins.then_inc(sc_ps.sem, 1)

                pe.wait_ge(*qt_s.after(l, 3))
                for i in range(4):
                    scores(i)
                for i in range(H):
                    m, e = i // 2, i % 2
                    pe.wait_ge(*pn_s.after(l, i + 1))
                    if i >= 2:
                        pe.wait_ge(*pt_s.after(l, i - 1))
                    for st in range(NT):
                        for t in range(NT):
                            ins = pe.transpose(bank[4 + i % 2][:, st * SEQ + t * P:st * SEQ + (t + 1) * P],
                                               prob[:, i % 2, t, st * P:(st + 1) * P], ident)
                    ins.then_inc(pt_ps.sem, 1)
                    if i + 4 < H:
                        scores(i + 4)
                    pe.wait_ge(*pt_s.after(l, i + 1))
                    h = m + 4 * e
                    o = bank[6 + h // 4][HD * (h % 2):HD * (h % 2 + 1), (h // 2 % 2) * SEQ:(h // 2 % 2 + 1) * SEQ]
                    for st in range(NT):
                        at = (H + KV + e) * HD
                        ins = pe.matmul(o, qkv[:, st, at:at + HD], p_t[:, i % 2, st, :], start=(st == 0),
                                        stop=(st == NT - 1))
                    ins.then_inc(o_ps.sem, 1)

                pe.wait_ge(*pe_s.after(l, H))
                for i in range(4):
                    u0 = U_GATE + 9 * i
                    for k in range(6):
                        g = 6 * i + k
                        weights(u0 + k)
                        if g >= 4:
                            pe.wait_ge(*g3_s.after(l, g - 3))
                        columns(bank[g % 4][:, 0:SEQ], (u0 + k) % RING)
                    if i:
                        pe.wait_ge(*mg_s.after(l, 2 * i))
                    else:
                        pe.wait_ge(*olo_s.after(l, 2))
                        pe.wait_ge(*cvlo_s.after(l, JT))
                    for b, (hi, lo, base) in enumerate(((y_hi, y_lo, 0), (yb_hi, yb_lo, 0), (yb_hi, yb_lo, JT))):
                        weights(u0 + 6 + b)
                        for k in range(2):
                            o = bank[4 + 2 * k + b // 2][:, (b % 2) * SEQ:(b % 2 + 1) * SEQ]
                            columns(o, (u0 + 6 + b) % RING, tiles=JT, width=2 * P, at=k * P, hi=hi, lo=lo, base=base,
                                    used=(k == 1))

                def rows(u, hi, lo, start, stop, it=0):
                    s = u % RING
                    weights(u, it)
                    for t in range(NT):
                        tok = slice(t * P, (t + 1) * P)
                        for i, (a, w) in enumerate(((hi, w_hi), (hi, w_lo), (lo, w_hi))):
                            for n in range(2):
                                ins = pe.matmul(bank[2 * t + n][:, :], a[:, tok], w[:, s, n * 512:(n + 1) * 512],
                                                start=start and i == 0, stop=stop and i == 2)
                    ins.then_inc(unit_used.sem, 1)

                pe.wait_ge(*g3_s.after(l, 24))
                pe.wait_ge(*mg_s.after(l, KT))
                for k in range(KT):
                    pe.wait_ge(*mlo_s.after(l, k + 1))
                    rows(U_OUT + k, m_hi[:, k, :], m_lo[:, k, :], k == 0, k == KT - 1)
                norm(1, xn2)
                pe.wait_ge(*hlo_s.after(l, 2 * KT))

                def up(p, it=0):
                    s = p % 3
                    u0 = U_MLP + (2 + 4 * (p - 1) if p else 0)
                    if p >= 3 or not isinstance(it, int):
                        pe.wait_ge(*us_s.after(l, 3 * it + p - 2))
                    for k in range(2):
                        weights(u0 + k, it)
                        columns(bank[4 + s][:, k * SEQ:(k + 1) * SEQ], (u0 + k) % RING)

                def down(p, it=0, start=False, stop=False):
                    s = p % 3
                    pe.wait_ge(*ulo_s.after(l, 3 * it + p + 1))
                    for k in range(2):
                        rows(U_MLP + 4 + 4 * p + k if p < 15 else UNITS - 2 + k, u_hi[:, s, k, :], u_lo[:, s, k, :],
                             start and k == 0, stop and k == 1, it)

                up(0)
                for p in range(1, 4):
                    up(p)
                    down(p - 1, start=(p == 1))
                with pe.Fori(1, 4) as it:
                    for p in range(1, 4):
                        up(p, it)
                        down(p - 1, it)
                for p in range(13, 16):
                    up(p)
                    down(p - 1)
                down(15, stop=True)


_INS = ("x", "stream", "params", "lora", "gains", "consts")


def constants():
    c = np.zeros((P, NCONST), np.float32)
    i, j = np.arange(P)[:, None], np.arange(P)[None, :]

    def put(name, at, v):
        c[:v.shape[0], CONST[name] + at:CONST[name] + at + v.shape[1]] = v

    put("ident", 0, i == j)
    put("ones", 0, i // HD == j // HD)
    put("headsum", 0, i // HD == np.arange(2)[None, :])
    for t in range(JT):
        put("sel", t * P, np.arange(8)[:, None] == 2 * t + j // HD)
    chunk = i // C == j // C
    for d in range(2):
        before = (i < j) if d == 0 else (i > j)
        put("incl", d * 2 * P, chunk & before)
        put("incl", d * 2 * P + P, chunk & (before | (i == j)))
        for n, b in enumerate(LEVELS):
            fill = (i // (2 * b) == j // (2 * b)) & (i // b % 2 == 1) & (j // b % 2 == 0)
            put("level", (d * len(LEVELS) + n) * P, -(fill if d == 0 else fill.T).astype(np.float32))
        tok = np.arange(SEQ)[None, :]
        put("reset", d * SEQ, np.repeat(tok % C != (0 if d == 0 else C - 1), P, 0))
    half = HD // 2
    inv = (np.float32(10000.0) ** (-np.arange(0, half, 2, dtype=np.float32) / np.float32(half))).astype(np.float32)
    for t in range(NT):
        tok = t * P + np.arange(P)
        for a, pos in enumerate((tok // GRID_W, tok % GRID_W)):
            ang = pos.astype(np.float32)[:, None] * inv
            cos, sin = np.cos(ang), np.sin(ang)
            put("rope_c", t * HD + a * half, np.concatenate([cos, cos], 1))
            put("rope_s", t * HD + a * half, np.concatenate([-sin, sin], 1))
    return c


def layout(inputs):
    f = {k: np.asarray(v) for k, v in inputs.items()}
    L = DEPTH
    w = f["w_in"].reshape(L, KT, P, -1)

    def cols(at):
        return w[..., at:at + P].transpose(0, 2, 1, 3).reshape(L, P, UNIT)

    rwc, cvc = 15 * P, 12 * P
    units = [cols(u * P) for u in range(15)]
    units += [cols(rwc + s * RW + i * P) for i in range(JT) for s in range(3)]
    for a in range(2):
        at = rwc + cvc + a * 3 * P
        v = w[..., at:at + 3 * P].transpose(0, 2, 1, 3).reshape(L, P, 3 * UNIT)
        units += [v[..., k * UNIT:(k + 1) * UNIT] for k in range(3)]
    gate = rwc + cvc + QKV
    br = f["w_branch"].reshape(L, 3, JT, P, 4, 2 * P)
    for i in range(4):
        units += [cols(gate + b * D + n * P) for n in (2 * i, 2 * i + 1) for b in range(3)]
        units += [br[:, b, :, :, i].transpose(0, 2, 1, 3).reshape(L, P, UNIT) for b in range(3)]
    units += [f["w_out"].reshape(L, KT, P, D)[:, k] for k in range(KT)]
    w1 = f["w_mlp1"].reshape(L, KT, P, FF // P, P)
    w2 = f["w_mlp2"].reshape(L, FF // P, P, D)
    up = [w1[:, :, :, n].transpose(0, 2, 1, 3).reshape(L, P, UNIT) for n in range(FF // P)]
    units += up[0:2]
    for p in range(1, 16):
        units += up[2 * p:2 * p + 2] + [w2[:, 2 * p - 2], w2[:, 2 * p - 1]]
    units += [w2[:, 30], w2[:, 31]]
    assert len(units) == UNITS
    stream = np.stack(units, 1).reshape(L, CHUNKS, CHUNK, P, UNIT).transpose(0, 1, 3, 2, 4).reshape(
        L, CHUNKS, P, CHUNK * UNIT)
    names = {"mu_prev": "rw_mu_prev", "mu_next": "rw_mu_next", "w0": "rw_w0", "a0": "rw_a0", "k_k": "rw_k_k",
             "k_a": "rw_k_a", "r_k": "rw_r_k", "ln_g": "rw_ln_g", "ln_b": "rw_ln_b"}
    params = np.concatenate([f[names.get(k, k)].reshape(L, -1, P).transpose(0, 2, 1) for k in PARAMS], 2)
    lora = np.stack([f["rw_w2"].reshape(L, P, RW), f["rw_a2"].reshape(L, P, RW), f["rw_g2"]], 2)
    gains = np.concatenate([f["at_q_g"]] * H + [f["at_k_g"]] * KV, 1)
    return {"x": f["x"].reshape(SEQ, D), "stream": stream, "params": params, "lora": lora, "gains": gains,
            "consts": constants()}


def kernel(**inputs):
    import concourse.bacc as _bacc
    from concourse.bass_utils import run_bass_kernel_spmd as _run

    nc = _bacc.Bacc("TRN2", target_bir_lowering=False, num_devices=1, dynamic_dma_scratch_size=1024)
    arrays, args = {}, []
    for name, a in layout(inputs).items():
        arrays[f"in_{name}"] = np.ascontiguousarray(a)
        args.append(nc.dram_tensor(f"in_{name}", a.shape, F32, kind="ExternalInput").ap())
    out = nc.dram_tensor("out_x", (SEQ, D), F32, kind="ExternalOutput").ap()
    build(nc, *args, out)
    r = _run(nc, [arrays], core_ids=[0])
    return r.results[0]["out_x"].reshape(1, SEQ, D)
```

```python
from contextlib import ExitStack

import numpy as np

import concourse.bass as bass
from concourse import mybir

F32 = mybir.dt.float32
F32R = mybir.dt.float32r
ALU = mybir.AluOpType
ACT = mybir.ActivationFunctionType
AX = mybir.AxisListType

P = 128
D = 1024
SEQ = 256
NT = SEQ // P
KT = D // P
DEPTH = 2
H = 8
HD = 64
RW = H * HD
JT = RW // P
C = 64
FF = 4 * D
EPS = 1e-6
LN_EPS = 64e-5
DECAY = float(np.exp(np.float32(-0.5)))
GRID_W = 64
KV = 2
QKV = (H + 2 * KV) * HD

UNIT = 8 * P
CHUNK = 3
U_RW = 0
U_AT = U_RW + 15
U_CV = (U_AT + 6, U_AT + 9, U_AT + 18, U_AT + 21)
U_GATE = (U_AT + 12, U_AT + 24, U_AT + 30, U_AT + 36)
U_BRANCH = U_AT + 42
U_OUT = U_BRANCH + 12
U_MLP = U_OUT + KT
UNITS = U_MLP + 64
CHUNKS = UNITS // CHUNK
RING = 6
LANDS = ((CHUNKS + 1) // 2, CHUNKS // 2)

PARAMS = {}
_at = 0
for _name, _n in (("norm1_g", KT), ("norm2_g", KT), ("mu_prev", 15), ("mu_next", 15), ("w0", 8), ("a0", 8),
                  ("k_k", 4), ("k_a", 4), ("r_k", 4), ("ln_g", 4), ("ln_b", 4), ("cv_w", 12), ("cv_b", 4)):
    PARAMS[_name] = _at
    _at += _n
NPAR = _at
D_MU, D_W0, D_A0, D_KA = 0, 15, 23, 31
NDER = 35

LEVELS = (1, 2, 4, 8, 16, 32)
CONST = {}
_at = 0
for _name, _n in (("ident", P), ("sel", P), ("rope_c", NT * HD), ("rope_s", NT * HD), ("reset", SEQ),
                  ("incl", 2 * 2 * P), ("first", 2 * P), ("level", 2 * 5 * C), ("headsum", 2)):
    CONST[_name] = _at
    _at += _n
NCONST = _at


class Signal:

    def __init__(self, sem, per, start=0):
        self.sem, self.per, self.start = sem, per, start

    def after(self, layer, n):
        return self.sem, layer * self.per + (self.start + n)


def build(nc, x_in, stream, params, lora, gains, consts, out):
    with ExitStack() as ctx:
        sem = lambda name: ctx.enter_context(nc.semaphore(name))
        sig = lambda name, per, start=0: Signal(sem(name), per, start)
        bank = [ctx.enter_context(nc.psum_tensor(f"bank{i}", [P, 512], F32)) for i in range(8)]

        place = [nc.sbuf_base + (-nc.sbuf_base) % 32]

        def sb(name, shape, dt=F32):
            size = 4 * int(np.prod(shape[1:]))
            t = nc.alloc_sbuf_tensor_at(name, shape, dt, offset=place[0])
            place[0] += size + (-size) % 32
            return t

        raw = sb("raw", [P, 2, CHUNK * UNIT])
        w_hi = sb("w_hi", [P, RING, UNIT], F32R)
        w_lo = sb("w_lo", [P, RING, UNIT], F32R)
        x = sb("x", [P, NT, D])
        h_hi = sb("h_hi", [P, KT, SEQ], F32R)
        h_lo = sb("h_lo", [P, KT, SEQ], F32R)
        y_at = place[0]
        y_hi = sb("y_hi", [P, JT, SEQ], F32R)
        y_lo = sb("y_lo", [P, JT, SEQ], F32R)
        qkv = sb("qkv", [P, NT, QKV])
        gth0 = sb("gth0", [P, 6, SEQ])
        cst = sb("cst", [P, NCONST])
        par = sb("par", [P, NPAR])
        der = sb("der", [P, NDER])
        lor = sb("lor", [P, 3, RW])
        gain = sb("gain", [P, (H + KV) * HD])
        stat = sb("stat", [P, 2])
        mean2 = sb("mean2", [P, 2])
        rstd = sb("rstd", [P, 2])
        mhalf = sb("mhalf", [P, 20])
        overlay = place[0]

        z = sb("z", [P, 15, SEQ])
        ksum = sb("ksum", [P, JT, SEQ])
        v_tok = sb("v_tok", [P, NT, RW])
        a_t = sb("a_t", [P, JT, SEQ])
        lw = sb("lw", [P, JT, SEQ])
        cum = sb("cum", [P, JT, SEQ])
        e_cum = sb("e_cum", [P, JT, SEQ])
        kr = sb("kr", [P, JT, 2, SEQ])
        kh = sb("kh", [P, JT, SEQ])
        gates_at = place[0]
        bh = sb("bh", [P, JT, SEQ])
        kh_tok = sb("kh_tok", [P, NT, RW])
        bh_tok = sb("bh_tok", [P, NT, RW])
        bq = sb("bq", [P, H, 2, P])
        kq = sb("kq", [P, H, 2, P])
        xt = sb("xt", [P, H, P])
        state = sb("state", [P, JT, P])
        s_new = sb("s_new", [P, JT, HD])
        small = sb("small", [P, 4, 16])
        cc = sb("cc", [P, SEQ])
        cz = sb("cz", [P, SEQ + 2])
        kk = nc.alloc_sbuf_tensor_at("kk", [P, JT, SEQ], F32, offset=y_at)
        y_tok = nc.alloc_sbuf_tensor_at("y_tok", [P, NT, RW], F32, offset=y_at + 4 * JT * SEQ)
        assert place[0] <= nc.sbuf_usable_end, (place[0], nc.sbuf_usable_end)
        xm = a_t[:, :, :].rearrange("p j (e s) -> p (j e) s", e=2)
        zm = cum[:, :, :].rearrange("p j (e s) -> p (j e) s", e=2)
        r_b = lw[:, 0:2, :].rearrange("p a b -> p (a b)")
        u_b = lw[:, 2:4, :].rearrange("p a b -> p (a b)")
        rn_t = kh[0:2, :, :].rearrange("p a b -> p (a b)")
        bonus_v = kq[:, 0:4, :, :].rearrange("p a b c -> p (a b c)")
        cv = z[:, 8:12, :]
        xn1 = z[:, 0:8, :].rearrange("p (t a) b -> p t (a b)", t=2)

        place[0] = overlay
        yb_hi = sb("yb_hi", [P, 2 * JT, SEQ], F32R)
        yb_lo = sb("yb_lo", [P, 2 * JT, SEQ], F32R)
        m_hi = sb("m_hi", [P, KT, SEQ], F32R)
        m_lo = sb("m_lo", [P, KT, SEQ], F32R)
        overlay3 = place[0]
        q_sq = sb("q_sq", [P, NT, (H + KV) * HD])
        q_rt = sb("q_rt", [P, NT, (H + KV) * HD])
        rot = sb("rot", [P, NT, (H + KV) * HD])
        assert place[0] <= gates_at
        place[0] = gates_at
        gth_rest = sb("gth_rest", [P, 18, SEQ])
        a_st = sb("a_st", [P, 3, 20])
        q_t = sb("q_t", [P, 4, SEQ])
        k_t = sb("k_t", [P, SEQ])
        prob = sb("prob", [P, 2, NT, SEQ])
        p_t = sb("p_t", [P, 2, NT, SEQ])
        nmx = sb("nmx", [P, 8, NT])
        rsum = sb("rsum", [P, 8, NT])
        rinv = sb("rinv", [P, 8, NT])
        gmul = sb("gmul", [P, 2, 3, SEQ])
        assert place[0] <= nc.sbuf_usable_end, (place[0], nc.sbuf_usable_end)
        place[0] = overlay3
        xn2 = sb("xn2", [P, NT, D])
        relu = sb("relu", [P, 3, 512])
        usq = sb("usq", [P, 3, 512])
        u_hi = sb("u_hi", [P, 3, 2, SEQ], F32R)
        u_lo = sb("u_lo", [P, 3, 2, SEQ], F32R)
        assert place[0] <= nc.sbuf_usable_end, (place[0], nc.sbuf_usable_end)

        def gates(i, k, n):
            return gth0[:, k:k + n, :] if i == 0 else gth_rest[:, 6 * i - 6 + k:6 * i - 6 + k + n, :]

        def gth(i, k):
            return gates(i, k, 1).rearrange("p a b -> p (a b)")

        def branch_ps(i, k, b, n):
            banks = (4, 5, 6) if i % 2 else (2, 3, 7)
            if b == 2:
                return bank[banks[2]][:, k * SEQ:(k + 1) * SEQ]
            return bank[banks[k]][:, b * SEQ:(b + n) * SEQ]

        def gate_bank(i, k):
            return 4 + k % 4 if i == 0 else 2 + k % 2

        def updates(n):
            return n - n // 4

        def con(name, n, at=0, rows=P):
            return cst[0:rows, CONST[name] + at:CONST[name] + at + n]

        def par_of(name, i):
            return par[:, PARAMS[name] + i:PARAMS[name] + i + 1]

        ident = con("ident", P)

        ident_in = sem("ident_in")
        consts_in = sem("consts_in")
        out_s = sem("out_written")
        half_s = sem("exponent_set")
        landed = [sem("landed0"), sem("landed1")]
        pars_in = sem("pars_in")
        lora_in = sem("lora_in")
        gains_in = sem("gains_in")
        hi_ready = sig("hi_ready", UNITS)
        lo_ready = sig("lo_ready", UNITS, 1)
        unit_used = sig("unit_used", UNITS, 1)
        derived = sig("derived", 1)
        x_new = sig("x_new", 8, 16)
        sumsq = sig("sumsq", 4)
        meansq = sig("meansq", 2)
        rstd_s = sig("rstd_ready", 2)
        xn_s = sig("xn_ready", 2)
        xn1_s = sig("xn1_ready", 2)
        ht_ps = sig("ht_in_psum", 16)
        hhi_s = sig("h_hi_ready", 16)
        hlo_s = sig("h_lo_ready", 16)
        rw_sc = sig("rw_scaled", 15)
        rw_sh = sig("rw_shifted", 15)
        lora_act = sig("lora_inputs_ready", 2)
        kksq_s = sig("kk_squared", 1)
        nrm_ps = sig("kk_norm_in_psum", 1)
        nrm_mx = sig("kk_norm_guarded", 1)
        nrm_rs = sig("kk_rnorm", 1)
        vt_ps = sig("v_tok_in_psum", 2)
        vt_s = sig("v_tok_ready", 2)
        rnt_ps = sig("rnorm_t_in_psum", 1)
        rnt_s = sig("rnorm_t_ready", 2)
        kkn_ps = sig("rnorm_spread_in_psum", 2)
        kk_s = sig("kk_ready", 2)
        lora_ps = sig("lora_in_psum", 8)
        lora_th = sig("lora_tanh", 4)
        cum_s = sig("cum_ready", 2)
        exp_s = sig("exps_ready", 6)
        kr_s = sig("kr_ready", 2)
        khb_s = sig("khat_bhat_ready", 4)
        tok_ps = sig("hat_tok_in_psum", 8)
        tok_s = sig("hat_tok_ready", 8)
        st_zero = sig("state_cleared", 2)
        bq_ps = sig("bq_in_psum", 16)
        bq_s = sig("bq_masked", 16)
        a_ps = sig("a_in_psum", 8)
        kq_ps = sig("kq_in_psum", 16)
        kq_s = sig("kq_masked", 16)
        x_up = sig("x_updated", 8 * 5)
        xt_ps = sig("xt_in_psum", 8 * 5)
        xt_s = sig("xt_ready", 8 * 5)
        xt_up = sig("xt_updated", 8)
        zl_ps = sig("z_in_psum", 8 * 5)
        zl_s = sig("z_ready", 8 * 5)
        xz_ps = sig("xz_in_psum", 8 * 4)
        zx_ps = sig("zx_in_psum", 8)
        r_ps = sig("rhs_in_psum", 8)
        r_s = sig("rhs_ready", 8)
        u_ps = sig("u_in_psum", 8)
        u_s = sig("u_ready", 8)
        st_ps = sig("state_in_psum", 6)
        st_s = sig("state_ready", 6)
        y_ps = sig("y_in_psum", 4)
        y0_s = sig("y_copied", 2)
        y1_s = sig("y_added", 2)
        gn_var = sig("gn_var", 1)
        gn_rs = sig("gn_rstd", 1)
        yn_s = sig("yn_ready", 1)
        yt_ps = sig("yt_in_psum", 2)
        bon_in = sig("bonus_in", 1)
        bon_ps = sig("bonus_sums_in_psum", 1)
        bv_s = sig("bonus_v_ready", 1)
        bt_ps = sig("bonus_v_t_in_psum", 2)
        gd_s = sig("gd_ready", 1)
        g_ps = sig("g_in_psum", 2)
        yl_s = sig("y_affine", 2)
        yo_s = sig("y_gated", 2)
        yhi_s = sig("y_hi_ready", 1)
        ylo_s = sig("y_lo_ready", 1)
        cc_s = sig("c_gate_ready", 4)
        cx_s = sig("cx_ready", 4)
        cv_s = sig("cv_ready", 4)
        cvhi_s = sig("cv_hi_ready", 1)
        cvlo_s = sig("cv_lo_ready", 1)
        at_ps = sig("qkv_in_psum", 2)
        at_s = sig("qkv_ready", 4)
        qss_s = sig("q_meansq", 1)
        qrs_s = sig("q_rstd", 1)
        rope_s = sig("roped", 2)
        qt_ps = sig("qt_in_psum", 3)
        qt_s = sig("qt_ready", 3)
        sc_ps = sig("scores_in_psum", 8)
        mx_s = sig("max_ready", 8)
        pe_s = sig("exp_ready", 8)
        pn_s = sig("prob_ready", 8)
        pt_ps = sig("pt_in_psum", 8)
        pt_s = sig("pt_ready", 8)
        o_ps = sig("o_in_psum", 8)
        ohi_s = sig("o_hi_ready", 2)
        olo_s = sig("o_lo_ready", 2)
        g3_s = sig("gate_tanh", 24)
        mg_s = sig("merged", 8)
        mhi_s = sig("m_hi_ready", 8)
        mlo_s = sig("m_lo_ready", 8)
        rl_s = sig("relu_ready", 16)
        us_s = sig("u_squared", 16)
        uhi_s = sig("u_hi_ready", 16)
        ulo_s = sig("u_lo_ready", 16)
        dve_step = sem("dve_step")

        block = ctx.enter_context(nc.Block())
        tiles_of = ((0, 1), (1, 0))
        MLP_BODY = 12


        def level_mask(d, i):
            return con("level", C, (d * 5 + i - 1) * C).unsqueeze(1).to_broadcast([P, 8, C])

        def first_mask(d):
            return con("first", P, d * P).unsqueeze(1).to_broadcast([P, 4, P])

        def by_chunk(v):
            return v.rearrange("p a (c t) -> p (a c) t", t=C)

        def incl_mask(d):
            return con("incl", 2 * P, d * 2 * P).unsqueeze(1).to_broadcast([P, 2, 2 * P])

        def ht_bank(n, k):
            return bank[(k + 4 * n) % 8]

        ident4 = ident.unsqueeze(1).to_broadcast([P, 4, P])

        @block.sync
        def _(sp):
            sp.dma_start(x[:, :, :], x_in.rearrange("(t p) d -> p t d", p=P)).then_inc(x_new.sem, 16)
            sp.dma_start(cst[:, 0:P], consts[:, 0:P]).then_inc(ident_in, 16)
            with sp.Fori(0, DEPTH) as l:
                sp.wait_ge(*lo_ready.after(l, 0))
                sp.dma_start(raw[:, 0, :], stream[l, 0]).then_inc(landed[0], 16)
                sp.wait_ge(*x_new.after(l, 0))
                sp.dma_start(par[:, :], params[l]).then_inc(pars_in, 16)
                sp.dma_start(raw[:, 1, :], stream[l, 1]).then_inc(landed[1], 16)
                sp.dma_start(cst[:, P:], consts[:, P:]).then_inc(consts_in, 16)
                sp.dma_start(lor[:, :, :], lora[l]).then_inc(lora_in, 16)
                sp.dma_start(gain[:, :], gains[l].partition_broadcast(P)).then_inc(gains_in, 16)
                with sp.Fori(1, CHUNKS // 2) as c:
                    for s in range(2):
                        sp.wait_ge(*lo_ready.after(l, c * (2 * CHUNK) + CHUNK * (s - 1)))
                        sp.dma_start(raw[:, s, :], stream[l, c * 2 + s]).then_inc(landed[s], 16)
                sp.wait_ge(*lo_ready.after(l, CHUNK * (CHUNKS - 2)))
                sp.dma_start(raw[:, 0, :], stream[l, CHUNKS - 1]).then_inc(landed[0], 16)
            sp.wait_ge(*x_new.after(DEPTH, 0))
            sp.dma_start(out.rearrange("(t p) d -> p t d", p=P), x[:, :, :]).then_inc(out_s, 16)
            sp.wait_ge(out_s, 16)

        @block.gpsimd
        def _(pool):
            pool.sem_inc(lo_ready.sem, 1)
            pool.memset(mhalf[:, :], -0.5).then_inc(half_s, 1)
            pool.wait_ge(half_s, 1)
            with pool.Fori(0, DEPTH) as l:
                def lo(u, it=0):
                    s, c, k = u % RING, (u // CHUNK) % 2, u % CHUNK
                    pool.wait_ge(*hi_ready.after(l, it * MLP_BODY + u + 1))
                    pool.tensor_tensor(w_lo[:, s, :], raw[:, c, k * UNIT:(k + 1) * UNIT],
                                       w_hi[:, s, :].bitcast(F32), ALU.subtract).then_inc(lo_ready.sem, 1)

                def rsqrt(o, i, n):
                    return pool.tensor_tensor(o, i, mhalf[:, 0:n], ALU.pow)

                pool.wait_ge(*meansq.after(l, 1))
                rsqrt(rstd[:, :], mean2[:, :], 2).then_inc(rstd_s.sem, 1)
                for u in range(U_AT + RING):
                    lo(u)
                pool.wait_ge(*nrm_mx.after(l, 1))
                rsqrt(small[:, 1, :], small[:, 0, :], 16).then_inc(nrm_rs.sem, 1)
                for u in range(U_CV[0], U_GATE[1] + 6):
                    lo(u)
                pool.wait_ge(*gn_var.after(l, 1))
                rsqrt(small[:, 3, :], small[:, 2, :], 16).then_inc(gn_rs.sem, 1)
                for u in range(U_GATE[2], U_GATE[3]):
                    lo(u)
                pool.wait_ge(*qss_s.after(l, 1))
                rsqrt(a_st[:, 1, :], a_st[:, 0, :], 20).then_inc(qrs_s.sem, 1)
                for u in range(U_GATE[3], U_MLP + RING):
                    lo(u)
                pool.wait_ge(*meansq.after(l, 2))
                rsqrt(rstd[:, :], mean2[:, :], 2).then_inc(rstd_s.sem, 1)
                for u in range(U_MLP + RING, U_MLP + 2 + MLP_BODY):
                    lo(u)
                with pool.Fori(1, 5) as it:
                    for u in range(U_MLP + 2, U_MLP + 2 + MLP_BODY):
                        lo(u, it)
                for u in range(UNITS - 2, UNITS):
                    lo(u)

        @block.scalar
        def _(act):
            with act.Fori(0, DEPTH) as l:
                def split(u, it=0):
                    s, c, k = u % RING, (u // CHUNK) % 2, u % CHUNK
                    if k == 0:
                        act.wait_ge(landed[c], (l * LANDS[c] + it * (MLP_BODY // CHUNK // 2)
                                                + (u // CHUNK // 2 + 1)) * 16)
                    act.wait_ge(*unit_used.after(l, it * MLP_BODY + u + 1 - RING if u >= RING else 0))
                    act.activation(w_hi[:, s, :], raw[:, c, k * UNIT:(k + 1) * UNIT],
                                   ACT.Copy).then_inc(hi_ready.sem, 1)

                def norm(n, xn):
                    for t in range(NT):
                        act.wait_ge(*x_new.after(l, 2 * n * (t + 1)))
                        act.activation(xn[:, t, :], x[:, t, :], ACT.Square,
                                       accum_out=stat[:, t:t + 1]).then_inc(sumsq.sem, 1)
                    if n == 0:
                        for u in range(3):
                            split(u)
                    act.wait_ge(*rstd_s.after(l, n + 1))
                    act.activation(xn[:, 0, :], x[:, 0, :], ACT.Identity, scale=rstd[:, 0:1]).then_inc(xn_s.sem, 1)
                    if n == 0:
                        act.wait_ge(pars_in, (l + 1) * 16)
                        for u in range(3, RING):
                            split(u)
                    for k in range(KT):
                        act.wait_ge(*ht_ps.after(l, KT * n + k + 1))
                        act.activation(h_hi[:, k, :], ht_bank(n, k)[:, 0:SEQ], ACT.Identity,
                                       scale=par_of(f"norm{n + 1}_g", k)).then_inc(hhi_s.sem, 1)

                norm(0, xn1)

                act.wait_ge(*derived.after(l, 1))
                def attention_inputs(a):
                    for t in range(NT):
                        act.wait_ge(*(unit_used.after(l, U_AT + 3 * a + 3) if t else at_ps.after(l, a + 1)))
                        act.activation(qkv[:, t, a * 384:(a + 1) * 384], bank[6 + t][:, 0:384],
                                       ACT.Copy).then_inc(at_s.sem, 1)

                def gate(i, k):
                    act.wait_ge(*unit_used.after(l, U_GATE[i] + k + 1))
                    act.activation(gth(i, k), bank[gate_bank(i, k)][:, 0:SEQ], ACT.Tanh,
                                   scale=0.5).then_inc(g3_s.sem, 1)

                def split3(u):
                    for k in range(3):
                        split(u + k)

                for u in range(U_AT):
                    act.wait_ge(*unit_used.after(l, u + 1))
                    act.activation(z[:, u, :], bank[u % 4][:, 0:SEQ], ACT.Identity,
                                   scale=der[:, D_MU + u:D_MU + u + 1]).then_inc(rw_sc.sem, 1)
                    split(u + RING)
                act.wait_ge(*rw_sh.after(l, 15))
                act.activation(z[:, 12, :], z[:, 12, :], ACT.Tanh).then_inc(lora_act.sem, 1)
                act.activation(z[:, 14, :], z[:, 14, :], ACT.Tanh, scale=0.5).then_inc(lora_act.sem, 1)
                attention_inputs(0)
                for t in range(NT):
                    act.wait_ge(*vt_ps.after(l, t + 1))
                    act.activation(v_tok[:, t, :], bank[5 + t][:, :], ACT.Copy).then_inc(vt_s.sem, 1)
                split3(U_CV[0])

                for d in range(2):
                    if d:
                        act.wait_ge(*y_ps.after(l, 2))
                    for part, th in enumerate((lw, a_t)):
                        if part and not d:
                            act.wait_ge(*rnt_ps.after(l, 1))
                            for b in range(2):
                                act.activation(rn_t[:, b * 512:(b + 1) * 512], bank[6 + b][0:2, :],
                                               ACT.Copy).then_inc(rnt_s.sem, 1)
                        for j in range(JT):
                            if j % 2 == 0:
                                act.wait_ge(*lora_ps.after(l, 4 * d + 2 * part + j // 2 + 1))
                            at = (D_W0, D_A0)[part] + JT * d + j
                            ins = act.activation(th[:, j, :], bank[2 * part + j // 2][:, (j % 2) * SEQ:(j % 2 + 1) * SEQ],
                                                 ACT.Tanh, scale=0.5, bias=der[:, at:at + 1])
                        ins.then_inc(lora_th.sem, 1)
                    if d:
                        for k in range(2):
                            gate(0, k)
                    act.wait_ge(*cum_s.after(l, d + 1))
                    act.activation(e_cum[:, :, :], cum[:, :, :], ACT.Exp).then_inc(exp_s.sem, 1)
                    act.activation(lw[:, :, :], lw[:, :, :], ACT.Exp).then_inc(exp_s.sem, 1)
                    act.activation(cum[:, :, :], cum[:, :, :], ACT.Exp, scale=-1.0).then_inc(exp_s.sem, 1)
                    if d:
                        for k in range(2, 6):
                            gate(0, k)
                    else:
                        attention_inputs(1)
                        split3(U_CV[1])
                    for i, (o, t) in enumerate(((kh_tok, 0), (kh_tok, 1), (bh_tok, 0), (bh_tok, 1))):
                        act.wait_ge(*tok_ps.after(l, 4 * d + i + 1))
                        act.activation(o[:, t, :], bank[4 + i][:, :], ACT.Copy).then_inc(tok_s.sem, 1)
                    if d:
                        split3(U_CV[2])
                        split3(U_CV[3])
                    for i, t in enumerate(tiles_of[d]):
                        g = 2 * d + i
                        for li in range(5):
                            for e in range(2):
                                act.wait_ge(*xt_ps.after(l, 10 * g + 2 * li + e + 1))
                                act.activation(xt[:, 4 * e:4 * e + 4, :].rearrange("p a b -> p (a b)"),
                                               bank[4 + e][:, :], ACT.Copy).then_inc(xt_s.sem, 1)
                        for ci, c in enumerate(tiles_of[d]):
                            n, q = 2 * g + ci, C * c
                            act.wait_ge(*r_ps.after(l, n + 1))
                            act.activation(r_b[q:q + C, :], bank[6][q:q + C, :], ACT.Copy).then_inc(r_s.sem, 1)
                            act.wait_ge(*u_ps.after(l, n + 1))
                            act.activation(u_b[q:q + C, :], bank[7][q:q + C, :], ACT.Copy,
                                           scale=-1.0).then_inc(u_s.sem, 1)
                            if ci == 0:
                                act.wait_ge(*unit_used.after(l, U_CV[g] + 1))
                                if g:
                                    act.wait_ge(*cv_s.after(l, g))
                                act.activation(cc[:, :], bank[2][:, 0:SEQ], ACT.Copy).then_inc(cc_s.sem, 1)
                        if d == 0:
                            act.wait_ge(*y_ps.after(l, g + 1))
                            act.activation(y_tok[:, t, :], bank[0][:, :], ACT.Copy).then_inc(y0_s.sem, 1)
                        split3((U_GATE[0], U_GATE[0] + 3, U_GATE[1], U_GATE[1] + 3)[g])
                for k in range(6):
                    gate(1, k)
                    split(U_GATE[2] + k)
                act.wait_ge(*cv_s.after(l, JT))
                act.wait_ge(*bon_in.after(l, 1))
                act.activation(yb_hi[:, 0:JT, :], cv, ACT.Copy).then_inc(cvhi_s.sem, 1)
                for j in range(JT):
                    if j % 2 == 0:
                        act.wait_ge(*yt_ps.after(l, j // 2 + 1))
                    ins = act.activation(e_cum[:, j, :], bank[j // 2][:, (j % 2) * SEQ:(j % 2 + 1) * SEQ], ACT.Identity,
                                         scale=par_of("ln_g", j), bias=par_of("ln_b", j))
                    if j % 2:
                        ins.then_inc(yl_s.sem, 1)
                act.wait_ge(*yo_s.after(l, 2))
                act.activation(y_hi[:, :, :], kh[:, :, :], ACT.Copy).then_inc(yhi_s.sem, 1)

                for k in range(6):
                    gate(2, k)
                    split(U_GATE[3] + k)

                for i in range(2):
                    act.wait_ge(*qt_ps.after(l, i + 1))
                    act.activation(q_t[:, 2 * i:2 * i + 2, :].rearrange("p a b -> p (a b)"), bank[4 + i][:, :],
                                   ACT.Copy, scale=HD ** -0.5).then_inc(qt_s.sem, 1)
                act.wait_ge(*qt_ps.after(l, 3))
                act.activation(k_t[:, :], bank[6][:, 0:SEQ], ACT.Copy).then_inc(qt_s.sem, 1)

                def exps(i):
                    b = i % 2
                    act.wait_ge(*mx_s.after(l, i + 1))
                    if i >= 2:
                        act.wait_ge(*pt_ps.after(l, i - 1))
                    for t in range(NT):
                        ins = act.activation(prob[:, i % 2, t, :], bank[b][:, t * SEQ:(t + 1) * SEQ], ACT.Exp,
                                             bias=nmx[:, i, t:t + 1], accum_out=rsum[:, i, t:t + 1])
                    ins.then_inc(pe_s.sem, 1)

                exps(0)
                exps(1)
                for i in range(H):
                    act.wait_ge(*pt_ps.after(l, i + 1))
                    if i >= 2:
                        act.wait_ge(*o_ps.after(l, i - 1))
                    act.activation(p_t[:, i % 2, :, :].rearrange("p a b -> p (a b)"), bank[4 + i % 2][:, :],
                                   ACT.Copy).then_inc(pt_s.sem, 1)
                    if i + 2 < H:
                        exps(i + 2)
                    if i < 6:
                        gate(3, i)
                    split(U_BRANCH + i)
                act.wait_ge(*o_ps.after(l, H))
                for b in range(2):
                    act.activation(yb_hi[:, JT + 2 * b:JT + 2 * b + 2, :].rearrange("p a b -> p (a b)"),
                                   bank[6 + b][:, :], ACT.Copy).then_inc(ohi_s.sem, 1)

                for i in range(4):
                    for k in range(0 if i else 2, 3):
                        split(U_BRANCH + RING + 3 * i + k)
                    for k in range(2):
                        act.wait_ge(*mg_s.after(l, 2 * i + k + 1))
                        act.activation(m_hi[:, 2 * i + k, :], gmul[:, k, 0, :], ACT.Copy,
                                       scale=0.5).then_inc(mhi_s.sem, 1)
                for k in range(KT):
                    split(U_OUT + k + RING)

                norm(1, xn2)

                def square(p, it=0):
                    s = p % 3
                    act.wait_ge(*unit_used.after(l, it * MLP_BODY + U_MLP + (4 * p if p else 2)))
                    act.activation(relu[:, s, :], bank[4 + s][:, :], ACT.Relu).then_inc(rl_s.sem, 1)

                def round_u(p, it=0):
                    s = p % 3
                    act.wait_ge(*us_s.after(l, 3 * it + p + 1))
                    act.activation(u_hi[:, s, :, :].rearrange("p a b -> p (a b)"), usq[:, s, :],
                                   ACT.Copy).then_inc(uhi_s.sem, 1)

                def pair(p, it=0):
                    u0 = U_MLP + 2 + 4 * (p - 1)
                    square(p, it)
                    for k in range(4):
                        if k == 2:
                            round_u(p, it)
                        if u0 + k + RING < UNITS:
                            split(u0 + k + RING, it)

                square(0)
                for k in range(2):
                    split(U_MLP + k + RING)
                round_u(0)
                for p in range(1, 4):
                    pair(p)
                with act.Fori(1, 4) as it:
                    for p in range(1, 4):
                        pair(p, it)
                for p in range(13, 16):
                    pair(p)

        @block.vector
        def _(dve):
            with dve.Fori(0, DEPTH) as l:
                count = [0]

                def then(ins):
                    count[0] += 1
                    ins.then_inc(dve_step, 1)
                    dve.wait_ge(dve_step, count[0])

                def norm(n, xn):
                    dve.wait_ge(*sumsq.after(l, 2 * n + 2))
                    dve.tensor_scalar(mean2[:, :], stat[:, :], 1.0 / D, EPS, ALU.mult, ALU.add).then_inc(meansq.sem, 1)
                    dve.wait_ge(*rstd_s.after(l, n + 1))
                    dve.tensor_scalar(xn[:, 1, :], x[:, 1, :], rstd[:, 1:2], None, ALU.mult).then_inc(xn1_s.sem, 1)
                    if n == 0:
                        derive()
                    for k in range(KT):
                        dve.wait_ge(*hhi_s.after(l, KT * n + k + 1))
                        dve.scalar_tensor_tensor(h_lo[:, k, :], ht_bank(n, k)[:, 0:SEQ], par_of(f"norm{n + 1}_g", k),
                                                 h_hi[:, k, :].bitcast(F32), ALU.mult,
                                                 ALU.subtract).then_inc(hlo_s.sem, 1)

                def derive():
                    dve.wait_ge(pars_in, (l + 1) * 16)
                    mp, mn = (par[:, PARAMS[k]:PARAMS[k] + 15] for k in ("mu_prev", "mu_next"))
                    mu = der[:, D_MU:D_MU + 15]
                    dve.tensor_scalar(der[:, D_W0:D_W0 + 16], par[:, PARAMS["w0"]:PARAMS["w0"] + 16], 0.5, None,
                                      ALU.mult)
                    dve.tensor_scalar(der[:, D_KA:D_KA + 4], par[:, PARAMS["k_a"]:PARAMS["k_a"] + 4], -1.0, 1.0,
                                      ALU.mult, ALU.add)
                    then(dve.tensor_tensor(mu, mp, mn, ALU.add))
                    dve.tensor_scalar(mu, mu, -1.0, 1.0, ALU.mult, ALU.add).then_inc(derived.sem, 1)

                norm(0, xn1)

                for u in range(U_AT):
                    ps = bank[u % 4]
                    dve.wait_ge(*rw_sc.after(l, u + 1))
                    then(dve.scalar_tensor_tensor(z[:, u, 1:SEQ], ps[:, 0:SEQ - 1], par_of("mu_prev", u),
                                                  z[:, u, 1:SEQ], ALU.mult, ALU.add))
                    dve.scalar_tensor_tensor(z[:, u, 0:SEQ - 1], ps[:, 1:SEQ], par_of("mu_next", u),
                                             z[:, u, 0:SEQ - 1], ALU.mult, ALU.add).then_inc(rw_sh.sem, 1)
                dve.wait_ge(*rw_sh.after(l, 15))
                def convolve(i):
                    tap = lambda k: par_of("cv_w", 4 * k + i)
                    dve.wait_ge(*cc_s.after(l, i + 1))
                    dve.wait_ge(*unit_used.after(l, U_CV[i] + 2))
                    dve.tensor_tensor(cz[:, 1:SEQ + 1], bank[3][:, 0:SEQ], cc[:, :], ALU.mult).then_inc(cx_s.sem, 1)
                    dve.wait_ge(*cx_s.after(l, i + 1))
                    then(dve.tensor_scalar(cv[:, i, :], cz[:, 0:SEQ], tap(0), par_of("cv_b", i), ALU.mult, ALU.add))
                    for k in (1, 2):
                        then(dve.scalar_tensor_tensor(cv[:, i, :], cz[:, k:SEQ + k], tap(k), cv[:, i, :],
                                                      ALU.mult, ALU.add))

                def centre(t):
                    y3 = y_tok[:, t, :].rearrange("p (h v) -> p h v", v=HD)
                    sq = kh[:, 2 * t:2 * t + 2, :].rearrange("p j (a v) -> p (j a) v", v=HD)
                    mean = small[:, 0, t * H:(t + 1) * H]
                    then(dve.tensor_reduce(mean, y3, AX.X, ALU.add))
                    then(dve.tensor_scalar(mean, mean, 1.0 / HD, None, ALU.mult))
                    then(dve.tensor_tensor(y3, y3, mean.unsqueeze(2).to_broadcast([P, H, HD]), ALU.subtract))
                    then(dve.tensor_tensor(sq, y3, y3, ALU.mult))
                    then(dve.tensor_reduce(small[:, 2, t * H:(t + 1) * H], sq, AX.X, ALU.add))

                dve.wait_ge(consts_in, (l + 1) * 16)
                for j in range(JT):
                    ins = dve.tensor_scalar(kk[:, j, :], z[:, 4 + j, :], par_of("k_k", j), None, ALU.mult)
                then(ins)
                dve.tensor_tensor(lw[:, :, :], kk[:, :, :], kk[:, :, :], ALU.mult).then_inc(kksq_s.sem, 1)
                dve.memset(cz[:, 0:SEQ + 2:SEQ + 1], 0.0)
                dve.memset(state[:, :, :], 0.0).then_inc(st_zero.sem, 1)
                dve.wait_ge(*nrm_ps.after(l, 1))
                dve.tensor_scalar(small[:, 0, :], bank[4][:, 0:16], 1e-24, None, ALU.max).then_inc(nrm_mx.sem, 1)
                dve.wait_ge(*lora_act.after(l, 2))
                dve.tensor_scalar(z[:, 14, :], z[:, 14, :], 0.5, 0.5, ALU.mult, ALU.add).then_inc(gd_s.sem, 1)

                for d in range(2):
                    dve.wait_ge(*lora_th.after(l, 2 * d + 1))
                    then(dve.tensor_scalar(lw[:, :, :], lw[:, :, :], -DECAY / 2, -DECAY / 2, ALU.mult, ALU.add))
                    for j in range(JT):
                        o, i = cum[:, j, :], lw[:, j, :]
                        if d:
                            o, i = o[:, ::-1], i[:, ::-1]
                        ins = dve.tensor_tensor_scan(o, con("reset", SEQ), i, 0.0, ALU.mult, ALU.add)
                    then(ins)
                    dve.tensor_tensor(lw[:, :, :], cum[:, :, :], lw[:, :, :], ALU.subtract).then_inc(cum_s.sem, 1)
                    dve.wait_ge(*lora_th.after(l, 2 * d + 2))
                    then(dve.tensor_scalar(a_t[:, :, :], a_t[:, :, :], 0.5, 0.5, ALU.mult, ALU.add))
                    for j in range(JT):
                        ins = dve.tensor_scalar(bh[:, j, :], a_t[:, j, :], par_of("k_a", j),
                                                der[:, D_KA + j:D_KA + j + 1], ALU.mult, ALU.add)
                    then(ins)
                    then(dve.tensor_tensor(bh[:, :, :], bh[:, :, :], z[:, 4:8, :], ALU.mult))
                    if d == 0:
                        dve.tensor_copy(ksum[:, :, :], bh[:, :, :])
                        for i in range(2):
                            dve.wait_ge(*kkn_ps.after(l, i + 1))
                            v = kk[:, 2 * i:2 * i + 2, :].rearrange("p a b -> p (a b)")
                            dve.tensor_tensor(v, v, bank[4 + i][:, :], ALU.mult).then_inc(kk_s.sem, 1)
                        dve.wait_ge(*kk_s.after(l, 2))
                    else:
                        dve.tensor_tensor(ksum[:, :, :], ksum[:, :, :], bh[:, :, :], ALU.add)
                    then(dve.tensor_tensor(a_t[:, :, :], kk[:, :, :], a_t[:, :, :], ALU.mult))
                    dve.wait_ge(*exp_s.after(l, 3 * d + 1))
                    dve.tensor_tensor(kr[:, :, 1, :], z[:, 0:4, :], e_cum[:, :, :], ALU.mult)
                    dve.wait_ge(*exp_s.after(l, 3 * d + 2))
                    dve.tensor_tensor(kr[:, :, 0, :], kk[:, :, :], lw[:, :, :], ALU.mult).then_inc(kr_s.sem, 1)
                    dve.wait_ge(*exp_s.after(l, 3 * d + 3))
                    dve.tensor_tensor(kh[:, :, :], bh[:, :, :], cum[:, :, :], ALU.mult).then_inc(khb_s.sem, 1)
                    dve.wait_ge(*khb_s.after(l, 2 * d + 1))
                    dve.tensor_tensor(bh[:, :, :], a_t[:, :, :], cum[:, :, :], ALU.mult).then_inc(khb_s.sem, 1)

                    if d:
                        dve.wait_ge(*y_ps.after(l, 2))
                        dve.memset(state[:, :, :], 0.0).then_inc(st_zero.sem, 1)
                    for i, t in enumerate(tiles_of[d]):
                        g = 2 * d + i
                        if g:
                            dve.wait_ge(*y_ps.after(l, g))
                        for m in range(4):
                            at = 4 * (m % 2) + 2 * (m // 2)
                            dve.wait_ge(*bq_ps.after(l, 4 * g + m + 1))
                            dve.tensor_tensor(bq[:, at:at + 2, :, :].rearrange("p a b c -> p a (b c)"),
                                              bank[m][:, :].rearrange("p (a b) -> p a b", a=2), incl_mask(d),
                                              ALU.mult).then_inc(bq_s.sem, 1)
                        for e in range(2):
                            v = xm[:, 4 * e:4 * e + 4, :]
                            dve.wait_ge(*a_ps.after(l, 2 * g + e + 1))
                            then(dve.tensor_tensor(v, bank[4 + e][:, :].rearrange("p (a b) -> p a b", a=4),
                                                   first_mask(d), ALU.mult))
                            dve.tensor_tensor(v, v, ident4, ALU.add).then_inc(x_up.sem, 1)
                        for m in range(4):
                            at = 4 * (m % 2) + 2 * (m // 2)
                            dve.wait_ge(*kq_ps.after(l, 4 * g + m + 1))
                            dve.tensor_tensor(kq[:, at:at + 2, :, :].rearrange("p a b c -> p a (b c)"),
                                              bank[6 + m % 2][:, :].rearrange("p (a b) -> p a b", a=2), incl_mask(d),
                                              ALU.mult).then_inc(kq_s.sem, 1)
                        for li in range(5):
                            for e in range(2):
                                dve.wait_ge(*zl_ps.after(l, 10 * g + 2 * li + e + 1))
                                dve.tensor_tensor(by_chunk(zm[:, 4 * e:4 * e + 4, :]),
                                                  bank[e][:, :].rearrange("p (a b) -> p a b", a=8),
                                                  level_mask(d, li + 1), ALU.mult).then_inc(zl_s.sem, 1)
                            for e in range(2):
                                if li < 4:
                                    v = xm[:, 4 * e:4 * e + 4, :].rearrange("p a b -> p (a b)")
                                    dve.wait_ge(*x_up.after(l, 10 * g + 2 * li + e + 1))
                                    dve.wait_ge(*xz_ps.after(l, 8 * g + 2 * li + e + 1))
                                    dve.tensor_tensor(v, v, bank[2 + e][:, :], ALU.add).then_inc(x_up.sem, 1)
                                else:
                                    v = xt[:, 4 * e:4 * e + 4, :].rearrange("p a b -> p (a b)")
                                    dve.wait_ge(*xt_s.after(l, 10 * g + 8 + e + 1))
                                    dve.wait_ge(*zx_ps.after(l, 2 * g + e + 1))
                                    dve.tensor_tensor(v, v, bank[4 + e][:, :], ALU.add).then_inc(xt_up.sem, 1)
                        for ci, c in enumerate(tiles_of[d]):
                            n = 2 * g + ci
                            last = t * P + c * C + (0 if d else C - 1)
                            if g == 3 and ci == 0:
                                dve.wait_ge(*u_ps.after(l, n + 1))
                                for j in range(JT):
                                    ins = dve.scalar_tensor_tensor(cum[:, j, :], ksum[:, j, :], par_of("r_k", j),
                                                                   z[:, j, :], ALU.mult, ALU.mult)
                                ins.then_inc(bon_in.sem, 1)
                                centre(t + 1)
                            if ci:
                                convolve(g)
                            if i and ci:
                                continue
                            dve.wait_ge(*st_ps.after(l, updates(n) + 1))
                            for e in range(2):
                                r = slice(HD * e, HD * (e + 1))
                                ins = dve.tensor_tensor(s_new[r, :, :], state[r, :, HD * e:HD * (e + 1)],
                                                        bank[1][r, 0:JT * HD].rearrange("p (a b) -> p a b", a=JT),
                                                        ALU.add)
                            then(ins)
                            for e in range(2):
                                r = slice(HD * e, HD * (e + 1))
                                ins = dve.tensor_tensor(state[r, :, HD * e:HD * (e + 1)], s_new[r, :, :],
                                                        e_cum[r, :, last:last + 1].to_broadcast([HD, JT, HD]), ALU.mult)
                            ins.then_inc(st_s.sem, 1)
                            dve.wait_ge(*st_s.after(l, updates(n) + 1))
                        if d:
                            dve.wait_ge(*y_ps.after(l, g + 1))
                            dve.tensor_tensor(y_tok[:, t, :], y_tok[:, t, :], bank[0][:, :],
                                              ALU.add).then_inc(y1_s.sem, 1)

                        if g == 3:
                            dve.wait_ge(*y1_s.after(l, 2))
                            centre(t)
                            dve.tensor_scalar(small[:, 2, :], small[:, 2, :], 1.0 / HD, LN_EPS, ALU.mult,
                                              ALU.add).then_inc(gn_var.sem, 1)
                        dve.wait_ge(*unit_used.after(l, U_CV[g] + 3))
                        dve.tensor_tensor(cv[:, g, :], cv[:, g, :], bank[4][:, 0:SEQ], ALU.mult).then_inc(cv_s.sem, 1)

                y3 = y_tok[:, :, :].rearrange("p t (h v) -> p (t h) v", v=HD)
                spread = lambda i: small[:, i, :].unsqueeze(2).to_broadcast([P, 16, HD])
                dve.wait_ge(*bon_ps.after(l, 1))
                dve.tensor_tensor(bonus_v.rearrange("p (h v) -> p h v", v=HD),
                                  v_tok[:, :, :].rearrange("p t (h v) -> p (t h) v", v=HD),
                                  bank[5][:, 0:16].unsqueeze(2).to_broadcast([P, 16, HD]),
                                  ALU.mult).then_inc(bv_s.sem, 1)
                dve.wait_ge(*gn_rs.after(l, 1))
                dve.tensor_tensor(y3, y3, spread(3), ALU.mult).then_inc(yn_s.sem, 1)
                for i in range(2):
                    js = slice(2 * i, 2 * i + 2)
                    flat = lambda t: t[:, js, :].rearrange("p a b -> p (a b)")
                    dve.wait_ge(*bt_ps.after(l, i + 1))
                    dve.wait_ge(*yl_s.after(l, i + 1))
                    then(dve.scalar_tensor_tensor(flat(e_cum), bank[4 + i][:, :], 0.5, flat(e_cum), ALU.mult, ALU.add))
                    dve.wait_ge(*g_ps.after(l, i + 1))
                    dve.tensor_tensor(flat(kh), flat(e_cum), bank[6 + i][:, :], ALU.mult).then_inc(yo_s.sem, 1)
                dve.wait_ge(*yhi_s.after(l, 1))
                dve.tensor_tensor(y_lo[:, :, :], kh[:, :, :], y_hi[:, :, :].bitcast(F32),
                                  ALU.subtract).then_inc(ylo_s.sem, 1)
                dve.wait_ge(*ylo_s.after(l, 1))

                dve.wait_ge(*cvhi_s.after(l, 1))
                dve.tensor_tensor(yb_lo[:, 0:JT, :], cv, yb_hi[:, 0:JT, :].bitcast(F32),
                                  ALU.subtract).then_inc(cvlo_s.sem, 1)

                NH = H + KV
                heads = lambda v: v.rearrange("p (h v) -> p h v", v=HD)
                dve.wait_ge(*at_s.after(l, 4))
                for t in range(NT):
                    ins = dve.tensor_tensor(q_sq[:, t, :], qkv[:, t, 0:NH * HD], qkv[:, t, 0:NH * HD], ALU.mult)
                then(ins)
                then(dve.tensor_reduce(a_st[:, 2, :], q_sq[:, :, :].rearrange("p t (h v) -> p (t h) v", v=HD),
                                       AX.X, ALU.add))
                dve.tensor_scalar(a_st[:, 0, :], a_st[:, 2, :], 1.0 / HD, EPS, ALU.mult, ALU.add).then_inc(qss_s.sem, 1)
                dve.wait_ge(*qrs_s.after(l, 1))
                dve.wait_ge(gains_in, (l + 1) * 16)
                for t in range(NT):
                    qn, q2, q3 = q_rt[:, t, :], q_sq[:, t, :], rot[:, t, :]
                    cos = con("rope_c", HD, t * HD).unsqueeze(1).to_broadcast([P, NH, HD])
                    sin = con("rope_s", HD, t * HD).rearrange("p (a b c) -> p a b c", a=2, b=2)
                    then(dve.tensor_tensor(heads(qn), heads(qkv[:, t, 0:NH * HD]),
                                           a_st[:, 1, t * NH:(t + 1) * NH].unsqueeze(2).to_broadcast([P, NH, HD]),
                                           ALU.mult))
                    then(dve.tensor_tensor(qn, qn, gain[:, :], ALU.mult))
                    dve.tensor_tensor(heads(q2), heads(qn), cos, ALU.mult)
                    for a in range(2):
                        for b in range(2):
                            pick = lambda v, b: v.rearrange("p (h a b c) -> p h a b c", a=2, b=2, c=16)[:, :, a, b, :]
                            ins = dve.tensor_tensor(pick(q3, b), pick(qn, 1 - b),
                                                    sin[:, a, b, :].unsqueeze(1).to_broadcast([P, NH, 16]), ALU.mult)
                    then(ins)
                    q4 = lambda v: v[:, 0:H * HD].rearrange("p (a m v) -> p a m v", a=KV, m=4)
                    dve.tensor_tensor(qn[:, 0:H * HD].rearrange("p (m a v) -> p a m v", a=KV, m=4), q4(q2), q4(q3),
                                      ALU.add)
                    dve.tensor_tensor(qn[:, H * HD:], q2[:, H * HD:], q3[:, H * HD:], ALU.add).then_inc(rope_s.sem, 1)

                def maxes(i):
                    b = i % 2
                    dve.wait_ge(*sc_ps.after(l, i + 1))
                    dve.tensor_reduce(nmx[:, i, :], bank[b][:, :].rearrange("p (t s) -> p t s", t=NT), AX.X, ALU.max,
                                      negate=True).then_inc(mx_s.sem, 1)

                for i in range(2):
                    maxes(i)
                for i in range(H):
                    dve.wait_ge(*pe_s.after(l, i + 1))
                    then(dve.reciprocal(rinv[:, i, :], rsum[:, i, :]))
                    for t in range(NT):
                        ins = dve.tensor_scalar(prob[:, i % 2, t, :], prob[:, i % 2, t, :], rinv[:, i, t:t + 1], None,
                                                ALU.mult)
                    ins.then_inc(pn_s.sem, 1)
                    if i + 2 < H:
                        maxes(i + 2)
                for b in range(2):
                    flat = lambda v: v[:, JT + 2 * b:JT + 2 * b + 2, :].rearrange("p a b -> p (a b)")
                    dve.wait_ge(*ohi_s.after(l, b + 1))
                    dve.tensor_tensor(flat(yb_lo), bank[6 + b][:, :], flat(yb_hi).bitcast(F32),
                                      ALU.subtract).then_inc(olo_s.sem, 1)

                for i in range(4):
                    dve.wait_ge(*unit_used.after(l, U_BRANCH + 3 * i + 3))
                    dve.wait_ge(*g3_s.after(l, 6 * i + 6))
                    if i:
                        dve.wait_ge(*mhi_s.after(l, 2 * i))
                        dve.wait_ge(*mlo_s.after(l, 2 * i))
                    for k in range(2):
                        flat = lambda v: v.rearrange("p a b -> p (a b)")
                        dve.scalar_tensor_tensor(flat(gmul[:, k, 0:2, :]), flat(gates(i, 3 * k, 2)), 1.0,
                                                 branch_ps(i, k, 0, 2), ALU.add, ALU.mult)
                        then(dve.scalar_tensor_tensor(gmul[:, k, 2, :], gth(i, 3 * k + 2), 1.0,
                                                      branch_ps(i, k, 2, 1), ALU.add, ALU.mult))
                        then(dve.tensor_tensor(gmul[:, k, 0, :], gmul[:, k, 0, :], gmul[:, k, 1, :], ALU.add))
                        dve.tensor_tensor(gmul[:, k, 0, :], gmul[:, k, 0, :], gmul[:, k, 2, :],
                                          ALU.add).then_inc(mg_s.sem, 1)
                    for k in range(2):
                        dve.wait_ge(*mhi_s.after(l, 2 * i + k + 1))
                        dve.scalar_tensor_tensor(m_lo[:, 2 * i + k, :], gmul[:, k, 0, :], 0.5,
                                                 m_hi[:, 2 * i + k, :].bitcast(F32), ALU.mult,
                                                 ALU.subtract).then_inc(mlo_s.sem, 1)

                def residual():
                    for t in range(NT):
                        for n in range(2):
                            v = x[:, t, n * 512:(n + 1) * 512]
                            dve.tensor_tensor(v, v, bank[2 * t + n][:, :], ALU.add).then_inc(x_new.sem, 1)

                dve.wait_ge(*unit_used.after(l, U_MLP))
                residual()
                norm(1, xn2)

                def square(p, it=0):
                    s = p % 3
                    dve.wait_ge(*rl_s.after(l, 3 * it + p + 1))
                    dve.tensor_tensor(usq[:, s, :], relu[:, s, :], bank[4 + s][:, :], ALU.mult).then_inc(us_s.sem, 1)
                    dve.wait_ge(*uhi_s.after(l, 3 * it + p + 1))
                    dve.tensor_tensor(u_lo[:, s, :, :].rearrange("p a b -> p (a b)"), usq[:, s, :],
                                      u_hi[:, s, :, :].rearrange("p a b -> p (a b)").bitcast(F32),
                                      ALU.subtract).then_inc(ulo_s.sem, 1)

                for p in range(4):
                    square(p)
                with dve.Fori(1, 4) as it:
                    for p in range(1, 4):
                        square(p, it)
                for p in range(13, 16):
                    square(p)
                dve.wait_ge(*unit_used.after(l, UNITS))
                dve.wait_ge(*x_new.after(l, 4))
                residual()
                dve.sem_clear(dve_step)

        @block.tensor
        def _(pe):
            pe.sem_inc(unit_used.sem, 1)
            pe.wait_ge(ident_in, 16)
            with pe.Fori(0, DEPTH) as l:
                def weights(u, it=0):
                    pe.wait_ge(*lo_ready.after(l, it * MLP_BODY + u + 1))

                def columns(o, s, tiles=KT, width=P, at=0, hi=h_hi, lo=h_lo, base=0, used=True,
                            arriving=None):
                    for k in range(tiles):
                        if arriving is not None:
                            pe.wait_ge(*hlo_s.after(l, arriving + k + 1))
                        c = slice(k * width + at, k * width + at + P)
                        pe.matmul(o, w_hi[:, s, c], hi[:, base + k, :], start=(k == 0), stop=False)
                        pe.matmul(o, w_hi[:, s, c], lo[:, base + k, :], start=False, stop=False)
                        ins = pe.matmul(o, w_lo[:, s, c], hi[:, base + k, :], start=False, stop=(k == tiles - 1))
                    if used:
                        ins.then_inc(unit_used.sem, 1)

                def norm(n, xn):
                    for t, ready in enumerate((xn_s, xn1_s)):
                        pe.wait_ge(*ready.after(l, n + 1))
                        for k in range(KT):
                            ins = pe.transpose(ht_bank(n, k)[:, t * P:(t + 1) * P], xn[:, t, k * P:(k + 1) * P], ident)
                            if t:
                                ins.then_inc(ht_ps.sem, 1)

                norm(0, xn1)
                for u in range(U_AT):
                    weights(u)
                    if u >= 4:
                        pe.wait_ge(*rw_sh.after(l, u - 3))
                    columns(bank[u % 4][:, 0:SEQ], u % RING, arriving=None if u else 0)

                def attention_inputs(a):
                    s0 = (U_AT + 3 * a) % RING
                    hi, lo = (w[:, s0:s0 + 3, :].rearrange("p a b -> p (a b)") for w in (w_hi, w_lo))
                    weights(U_AT + 3 * a + 2)
                    for t in range(NT):
                        tok = slice(t * P, (t + 1) * P)
                        o = bank[6 + t][:, 0:384]
                        for k in range(KT):
                            c = slice(k * 384, (k + 1) * 384)
                            pe.matmul(o, h_hi[:, k, tok], hi[:, c], start=(k == 0), stop=False)
                            pe.matmul(o, h_hi[:, k, tok], lo[:, c], start=False, stop=False)
                            ins = pe.matmul(o, h_lo[:, k, tok], hi[:, c], start=False, stop=(k == KT - 1))
                        if t == 0:
                            ins.then_inc(at_ps.sem, 1)
                        else:
                            ins.then_inc(unit_used.sem, 3)

                def gate(i, k):
                    g = 6 * i + k
                    weights(U_GATE[i] + k)
                    if i:
                        pe.wait_ge(*g3_s.after(l, g - 1))
                    elif k >= 4:
                        pe.wait_ge(*g3_s.after(l, g - 3))
                    columns(bank[gate_bank(i, k)][:, 0:SEQ], (U_GATE[i] + k) % RING)

                def convolution_half(i, n):
                    u, k0 = U_CV[i] + n // 2, KT // 2 * (n % 2)
                    s = u % RING
                    if k0 == 0:
                        weights(u)
                    o = bank[2 + n // 2][:, 0:SEQ]
                    for k in range(k0, k0 + KT // 2):
                        c = slice(k * P, (k + 1) * P)
                        pe.matmul(o, w_hi[:, s, c], h_hi[:, k, :], start=(k == 0), stop=False)
                        pe.matmul(o, w_hi[:, s, c], h_lo[:, k, :], start=False, stop=False)
                        ins = pe.matmul(o, w_lo[:, s, c], h_hi[:, k, :], start=False, stop=(k == KT - 1))
                    if k0:
                        ins.then_inc(unit_used.sem, 1)

                attention_inputs(0)
                pe.wait_ge(*rw_sh.after(l, 12))
                for t in range(NT):
                    if t:
                        pe.wait_ge(*at_s.after(l, 1))
                    for j in range(JT):
                        ins = pe.transpose(bank[5 + t][:, j * P:(j + 1) * P], z[:, 8 + j, t * P:(t + 1) * P], ident)
                    ins.then_inc(vt_ps.sem, 1)
                pe.wait_ge(consts_in, (l + 1) * 16)
                pe.wait_ge(*kksq_s.after(l, 1))
                for t in range(NT):
                    for j in range(JT):
                        ins = pe.matmul(bank[4][:, t * H + 2 * j:t * H + 2 * j + 2], lw[:, j, t * P:(t + 1) * P],
                                        con("headsum", 2), start=True, stop=True)
                ins.then_inc(nrm_ps.sem, 1)

                def lora_products(d):
                    for part in range(2):
                        for j in range(JT):
                            ins = pe.matmul(bank[2 * part + j // 2][:, (j % 2) * SEQ:(j % 2 + 1) * SEQ],
                                            lor[HD * d:HD * (d + 1), part, j * P:(j + 1) * P],
                                            z[HD * d:HD * (d + 1), 12 + part, :], start=True, stop=True)
                            if j % 2:
                                ins.then_inc(lora_ps.sem, 1)

                for d in range(2):
                    if d == 0:
                        pe.wait_ge(lora_in, (l + 1) * 16)
                        pe.wait_ge(*lora_act.after(l, 1))
                        pe.wait_ge(*rw_sh.after(l, 15))
                    else:
                        pe.wait_ge(*y0_s.after(l, 2))
                        pe.wait_ge(*st_s.after(l, updates(4)))
                        pe.wait_ge(*cv_s.after(l, 2))
                    lora_products(d)
                    if d == 0:
                        pe.wait_ge(*nrm_rs.after(l, 1))
                        pe.wait_ge(*vt_s.after(l, 2))
                        pe.wait_ge(*at_s.after(l, 2))
                        for j in range(JT):
                            for t in range(NT):
                                ins = pe.transpose(bank[6 + j // 2][0:2, (j % 2) * SEQ + t * P:(j % 2) * SEQ + (t + 1) * P],
                                                   small[:, 1, t * H + 2 * j:t * H + 2 * j + 2], ident)
                        ins.then_inc(rnt_ps.sem, 1)
                        pe.wait_ge(*rnt_s.after(l, 2))
                        for j in range(JT):
                            ins = pe.matmul(bank[4 + j // 2][:, (j % 2) * SEQ:(j % 2 + 1) * SEQ],
                                            con("sel", P, rows=2), rn_t[:, j * SEQ:(j + 1) * SEQ], start=True, stop=True)
                            if j % 2:
                                ins.then_inc(kkn_ps.sem, 1)
                        attention_inputs(1)
                    else:
                        for k in range(6):
                            gate(0, k)
                    for i, src in enumerate((kh, bh)):
                        pe.wait_ge(*khb_s.after(l, 2 * d + i + 1))
                        if i == 0:
                            pe.wait_ge(*(g3_s.after(l, 6) if d else at_s.after(l, 4)))
                        for t in range(NT):
                            for j in range(JT):
                                ins = pe.transpose(bank[4 + 2 * i + t][:, j * P:(j + 1) * P],
                                                   src[:, j, t * P:(t + 1) * P], ident)
                            ins.then_inc(tok_ps.sem, 1)
                    for i, t in enumerate(tiles_of[d]):
                        g = 2 * d + i
                        tok = slice(t * P, (t + 1) * P)
                        pe.wait_ge(*kr_s.after(l, d + 1))
                        if i:
                            pe.wait_ge(*(y1_s.after(l, 1) if d else y0_s.after(l, 1)))
                            pe.wait_ge(*st_s.after(l, updates(2 * g)))
                            pe.wait_ge(*cv_s.after(l, g))
                        for m in range(4):
                            e = slice(HD * (m % 2), HD * (m % 2 + 1))
                            for j in range(2):
                                jj = 2 * (m // 2) + j
                                ins = pe.matmul(bank[m][:, j * SEQ:(j + 1) * SEQ], bh[e, jj, tok], kr[e, jj, :, tok],
                                                start=True, stop=True)
                            ins.then_inc(bq_ps.sem, 1)
                        pe.wait_ge(*tok_s.after(l, 4 * d + 4))
                        for e in range(2):
                            r = slice(HD * e, HD * (e + 1))
                            for j in range(JT):
                                ins = pe.matmul(bank[4 + e][:, j * P:(j + 1) * P], kr[r, j, 0, tok], bh[r, j, tok],
                                                start=True, stop=True)
                            ins.then_inc(a_ps.sem, 1)
                        for m in range(4):
                            e = slice(HD * (m % 2), HD * (m % 2 + 1))
                            if m >= 2:
                                pe.wait_ge(*kq_s.after(l, 4 * g + m - 1))
                            for j in range(2):
                                jj = 2 * (m // 2) + j
                                ins = pe.matmul(bank[6 + m % 2][:, j * SEQ:(j + 1) * SEQ], kh[e, jj, tok],
                                                kr[e, jj, :, tok], start=True, stop=True)
                            ins.then_inc(kq_ps.sem, 1)
                        for li in range(5):
                            for e in range(2):
                                pe.wait_ge(*x_up.after(l, 10 * g + 2 * li + e + 1))
                                for j in range(JT):
                                    a = 4 * e + j
                                    ins = pe.matmul(bank[e][:, j * P:(j + 1) * P], bq[:, a, 0, :], xm[:, a, :],
                                                    start=True, stop=True)
                                ins.then_inc(zl_ps.sem, 1)
                            for e in range(2):
                                for j in range(JT):
                                    ins = pe.transpose(bank[4 + e][:, j * P:(j + 1) * P], xm[:, 4 * e + j, :], ident)
                                ins.then_inc(xt_ps.sem, 1)
                            for e in range(2):
                                pe.wait_ge(*zl_s.after(l, 10 * g + 2 * li + e + 1))
                                pe.wait_ge(*xt_s.after(l, 10 * g + 2 * li + e + 1))
                                for j in range(JT):
                                    a = 4 * e + j
                                    o = bank[(2 if li < 4 else 4) + e][:, j * P:(j + 1) * P]
                                    if li < 4:
                                        ins = pe.matmul(o, xt[:, a, :], zm[:, a, :], start=True, stop=True)
                                    else:
                                        ins = pe.matmul(o, zm[:, a, :], xt[:, a, :], start=True, stop=True)
                                ins.then_inc(xz_ps.sem if li < 4 else zx_ps.sem, 1)

                        def at(h):
                            return 4 * (h % 2) + h // 2

                        pe.wait_ge(*kq_s.after(l, 4 * g + 4))
                        for k, b in ((0, 6), (1, 0)):
                            for h in range(H):
                                pe.matmul(bank[b][:, h * HD:(h + 1) * HD], kq[:, at(h), k, :],
                                          v_tok[:, t, h * HD:(h + 1) * HD], start=(h == 0), stop=False,
                                          skip_group_check=True)
                        pe.wait_ge(*(st_s.after(l, updates(2 * g)) if i else st_zero.after(l, d + 1)))
                        for ci, c in enumerate(tiles_of[d]):
                            n = 2 * g + ci
                            r = slice(C * c, C * (c + 1))
                            here = slice(t * P + C * c, t * P + C * (c + 1))
                            if ci:
                                pe.wait_ge(*st_s.after(l, updates(n)))
                            for k, b in ((0, 6), (1, 0)):
                                for j in range(JT):
                                    ins = pe.matmul(bank[b][r, j * P:(j + 1) * P], kr[:, j, k, here], state[:, j, :],
                                                    start=False, stop=(k == 0), skip_group_check=True)
                                if k == 0:
                                    ins.then_inc(r_ps.sem, 1)
                            last = i == 1 and ci == 1
                            for h in range(0 if last else H):
                                e = slice(HD * (h % 2), HD * (h % 2 + 1))
                                v = slice(h * HD, (h + 1) * HD)
                                pe.matmul(bank[1][e, h // 2 * HD:(h // 2 + 1) * HD], kh_tok[r, t, v], v_tok[r, t, v],
                                          start=(h < 2), stop=False, skip_group_check=True)
                            convolution_half(g, 3 * ci)
                            pe.wait_ge(*xt_up.after(l, 2 * g + 2))
                            pe.wait_ge(*r_s.after(l, n + 1))
                            for h in range(H):
                                v = slice(h * HD, (h + 1) * HD)
                                ins = pe.matmul(bank[7][r, v], xt[:, at(h), r], r_b[:, v], start=True, stop=True)
                            ins.then_inc(u_ps.sem, 1)
                            convolution_half(g, 3 * ci + 1)
                            pe.wait_ge(*u_s.after(l, n + 1))

                            def own(h):
                                v = slice(h * HD, (h + 1) * HD)
                                return pe.matmul(bank[0][r, v], bq[:, at(h), 1, r], u_b[:, v], start=False, stop=True,
                                                 skip_group_check=True)

                            own(0)
                            for h in range(0 if last else H):
                                e = slice(HD * (h % 2), HD * (h % 2 + 1))
                                v = slice(h * HD, (h + 1) * HD)
                                ins = pe.matmul(bank[1][e, h // 2 * HD:(h // 2 + 1) * HD], bh_tok[r, t, v], u_b[r, v],
                                                start=False, stop=True, skip_group_check=True)
                            if not last:
                                ins.then_inc(st_ps.sem, 1)
                            for h in range(1, H):
                                ins = own(h)
                            if ci:
                                ins.then_inc(y_ps.sem, 1)
                            convolution_half(g, 3 * ci + 2)

                pe.wait_ge(*bon_in.after(l, 1))
                for t in range(NT):
                    for j in range(JT):
                        ins = pe.matmul(bank[5][:, t * H + 2 * j:t * H + 2 * j + 2], cum[:, j, t * P:(t + 1) * P],
                                        con("headsum", 2), start=True, stop=True)
                ins.then_inc(bon_ps.sem, 1)
                pe.wait_ge(*gd_s.after(l, 1))
                for j in range(JT):
                    ins = pe.matmul(bank[6 + j // 2][:, (j % 2) * SEQ:(j % 2 + 1) * SEQ], lor[:, 2, j * P:(j + 1) * P],
                                    z[:, 14, :], start=True, stop=True)
                    if j % 2:
                        ins.then_inc(g_ps.sem, 1)
                pe.wait_ge(*cx_s.after(l, JT))
                for k in range(5):
                    gate(1, k)

                def to_channels(src, b, done):
                    for j in range(JT):
                        for t in range(NT):
                            ins = pe.transpose(bank[b + j // 2][:, (j % 2) * SEQ + t * P:(j % 2) * SEQ + (t + 1) * P],
                                               src(t)[:, j * P:(j + 1) * P], ident)
                        if j % 2:
                            ins.then_inc(done.sem, 1)

                pe.wait_ge(*cv_s.after(l, JT))
                pe.wait_ge(*bv_s.after(l, 1))
                to_channels(lambda t: bonus_v[:, t * RW:(t + 1) * RW], 4, bt_ps)
                gate(1, 5)
                pe.wait_ge(*yn_s.after(l, 1))
                to_channels(lambda t: y_tok[:, t, :], 0, yt_ps)
                for k in range(6):
                    gate(2, k)

                pe.wait_ge(*yo_s.after(l, 2))
                pe.wait_ge(*rope_s.after(l, NT))
                for m in range(4):
                    for t in range(NT):
                        ins = pe.transpose(bank[4 + m // 2][:, (m % 2) * SEQ + t * P:(m % 2) * SEQ + (t + 1) * P],
                                           q_rt[:, t, m * P:(m + 1) * P], ident)
                    if m % 2:
                        ins.then_inc(qt_ps.sem, 1)
                for t in range(NT):
                    ins = pe.transpose(bank[6][:, t * P:(t + 1) * P], q_rt[:, t, H * HD:H * HD + P], ident)
                ins.then_inc(qt_ps.sem, 1)

                def scores(i):
                    m, e = i // 2, slice(HD * (i % 2), HD * (i % 2 + 1))
                    if i >= 2:
                        pe.wait_ge(*pe_s.after(l, i - 1))
                    for t in range(NT):
                        ins = pe.matmul(bank[i % 2][:, t * SEQ:(t + 1) * SEQ],
                                        q_t[e, m, t * P:(t + 1) * P], k_t[e, :], start=True, stop=True)
                    ins.then_inc(sc_ps.sem, 1)

                def branch(i, b):
                    hi, lo, base = ((y_hi, y_lo, 0), (yb_hi, yb_lo, 0), (yb_hi, yb_lo, JT))[b]
                    weights(U_BRANCH + 3 * i + b)
                    for k in range(2):
                        columns(branch_ps(i, k, b, 1), (U_BRANCH + 3 * i + b) % RING, tiles=JT, width=2 * P, at=k * P,
                                hi=hi, lo=lo, base=base, used=(k == 1))

                pe.wait_ge(*qt_s.after(l, 3))
                for i in range(2):
                    scores(i)
                for i in range(H):
                    m, e = i // 2, i % 2
                    pe.wait_ge(*pn_s.after(l, i + 1))
                    if i >= 2:
                        pe.wait_ge(*pt_s.after(l, i - 1))
                    for st in range(NT):
                        for t in range(NT):
                            ins = pe.transpose(bank[4 + i % 2][:, st * SEQ + t * P:st * SEQ + (t + 1) * P],
                                               prob[:, i % 2, t, st * P:(st + 1) * P], ident)
                    ins.then_inc(pt_ps.sem, 1)
                    if i + 2 < H:
                        scores(i + 2)
                    if i < 6:
                        gate(3, i)
                    elif i == 6:
                        pe.wait_ge(*g3_s.after(l, 24))
                        pe.wait_ge(*ylo_s.after(l, 1))
                        branch(0, 0)
                    else:
                        pe.wait_ge(*cvlo_s.after(l, 1))
                        branch(0, 1)
                    pe.wait_ge(*pt_s.after(l, i + 1))
                    h = m + 4 * e
                    o = bank[6 + h // 4][HD * (h % 2):HD * (h % 2 + 1), (h // 2 % 2) * SEQ:(h // 2 % 2 + 1) * SEQ]
                    for st in range(NT):
                        at = (H + KV + e) * HD
                        ins = pe.matmul(o, qkv[:, st, at:at + HD], p_t[:, i % 2, st, :], start=(st == 0),
                                        stop=(st == NT - 1))
                    ins.then_inc(o_ps.sem, 1)

                pe.wait_ge(*olo_s.after(l, 2))
                branch(0, 2)
                for i in range(1, 4):
                    if i >= 2:
                        pe.wait_ge(*mg_s.after(l, 2 * (i - 1)))
                    for b in range(3):
                        branch(i, b)

                def rows(u, hi, lo, start, stop, it=0):
                    s = u % RING
                    weights(u, it)
                    for t in range(NT):
                        tok = slice(t * P, (t + 1) * P)
                        for i, (a, w) in enumerate(((hi, w_hi), (hi, w_lo), (lo, w_hi))):
                            for n in range(2):
                                ins = pe.matmul(bank[2 * t + n][:, :], a[:, tok], w[:, s, n * 512:(n + 1) * 512],
                                                start=start and i == 0, stop=stop and i == 2)
                    ins.then_inc(unit_used.sem, 1)

                pe.wait_ge(*mg_s.after(l, 6))
                for k in range(KT):
                    pe.wait_ge(*mlo_s.after(l, k + 1))
                    rows(U_OUT + k, m_hi[:, k, :], m_lo[:, k, :], k == 0, k == KT - 1)
                norm(1, xn2)

                def up(p, it=0):
                    s = p % 3
                    u0 = U_MLP + (2 + 4 * (p - 1) if p else 0)
                    if p >= 3 or not isinstance(it, int):
                        pe.wait_ge(*us_s.after(l, 3 * it + p - 2))
                    for k in range(2):
                        weights(u0 + k, it)
                        columns(bank[4 + s][:, k * SEQ:(k + 1) * SEQ], (u0 + k) % RING,
                                arriving=None if p or k else KT)

                def down(p, it=0, start=False, stop=False):
                    s = p % 3
                    pe.wait_ge(*ulo_s.after(l, 3 * it + p + 1))
                    for k in range(2):
                        rows(U_MLP + 4 + 4 * p + k if p < 15 else UNITS - 2 + k, u_hi[:, s, k, :], u_lo[:, s, k, :],
                             start and k == 0, stop and k == 1, it)

                up(0)
                for p in range(1, 4):
                    up(p)
                    down(p - 1, start=(p == 1))
                with pe.Fori(1, 4) as it:
                    for p in range(1, 4):
                        up(p, it)
                        down(p - 1, it)
                for p in range(13, 16):
                    up(p)
                    down(p - 1)
                down(15, stop=True)


_INS = ("x", "stream", "params", "lora", "gains", "consts")


def constants():
    c = np.zeros((P, NCONST), np.float32)
    i, j = np.arange(P)[:, None], np.arange(P)[None, :]

    def put(name, at, v):
        c[:v.shape[0], CONST[name] + at:CONST[name] + at + v.shape[1]] = v

    put("ident", 0, i == j)
    put("headsum", 0, i // HD == np.arange(2)[None, :])
    put("sel", 0, np.arange(2)[:, None] == j // HD)
    chunk = i // C == j // C
    for d in range(2):
        before = (i < j) if d == 0 else (i > j)
        put("incl", d * 2 * P, chunk & before)
        put("incl", d * 2 * P + P, chunk & (before | (i == j)))
        for n, b in enumerate(LEVELS):
            fill = (i // (2 * b) == j // (2 * b)) & (i // b % 2 == 1) & (j // b % 2 == 0)
            fill = -(fill if d == 0 else fill.T).astype(np.float32)
            if n == 0:
                put("first", d * P, fill)
            else:
                put("level", (d * 5 + n - 1) * C, fill[:, 0:C] + fill[:, C:P])
    put("reset", 0, np.repeat(np.arange(SEQ)[None, :] % C != 0, P, 0))
    half = HD // 2
    inv = (np.float32(10000.0) ** (-np.arange(0, half, 2, dtype=np.float32) / np.float32(half))).astype(np.float32)
    for t in range(NT):
        tok = t * P + np.arange(P)
        for a, pos in enumerate((tok // GRID_W, tok % GRID_W)):
            ang = pos.astype(np.float32)[:, None] * inv
            cos, sin = np.cos(ang), np.sin(ang)
            put("rope_c", t * HD + a * half, np.concatenate([cos, cos], 1))
            put("rope_s", t * HD + a * half, np.concatenate([-sin, sin], 1))
    return c


def layout(inputs):
    f = {k: np.asarray(v) for k, v in inputs.items()}
    L = DEPTH
    w = f["w_in"].reshape(L, KT, P, -1)

    def cols(at):
        return w[..., at:at + P].transpose(0, 2, 1, 3).reshape(L, P, UNIT)

    rwc, cvc = 15 * P, 12 * P
    units = [cols(u * P) for u in range(15)]
    for a in range(2):
        at = rwc + cvc + a * 3 * P
        v = w[..., at:at + 3 * P].transpose(0, 2, 1, 3).reshape(L, P, 3 * UNIT)
        units += [v[..., k * UNIT:(k + 1) * UNIT] for k in range(3)]
    conv = [[cols(rwc + s * RW + i * P) for s in (1, 2, 0)] for i in range(JT)]
    gate = rwc + cvc + QKV
    gates = [[cols(gate + b * D + n * P) for n in (2 * i, 2 * i + 1) for b in range(3)] for i in range(4)]
    units += conv[0] + conv[1] + gates[0] + conv[2] + conv[3] + gates[1] + gates[2] + gates[3]
    br = f["w_branch"].reshape(L, 3, JT, P, 4, 2 * P)
    units += [br[:, b, :, :, i].transpose(0, 2, 1, 3).reshape(L, P, UNIT) for i in range(4) for b in range(3)]
    units += [f["w_out"].reshape(L, KT, P, D)[:, k] for k in range(KT)]
    w1 = f["w_mlp1"].reshape(L, KT, P, FF // P, P)
    w2 = f["w_mlp2"].reshape(L, FF // P, P, D)
    up = [w1[:, :, :, n].transpose(0, 2, 1, 3).reshape(L, P, UNIT) for n in range(FF // P)]
    units += up[0:2]
    for p in range(1, 16):
        units += up[2 * p:2 * p + 2] + [w2[:, 2 * p - 2], w2[:, 2 * p - 1]]
    units += [w2[:, 30], w2[:, 31]]
    assert len(units) == UNITS
    stream = np.stack(units, 1).reshape(L, CHUNKS, CHUNK, P, UNIT).transpose(0, 1, 3, 2, 4).reshape(
        L, CHUNKS, P, CHUNK * UNIT)
    names = {"mu_prev": "rw_mu_prev", "mu_next": "rw_mu_next", "w0": "rw_w0", "a0": "rw_a0", "k_k": "rw_k_k",
             "k_a": "rw_k_a", "r_k": "rw_r_k", "ln_g": "rw_ln_g", "ln_b": "rw_ln_b"}
    params = np.concatenate([f[names.get(k, k)].reshape(L, -1, P).transpose(0, 2, 1) for k in PARAMS], 2)
    lora = np.stack([f["rw_w2"].reshape(L, P, RW), f["rw_a2"].reshape(L, P, RW), f["rw_g2"]], 2)
    gains = np.concatenate([f["at_q_g"]] * H + [f["at_k_g"]] * KV, 1)
    return {"x": f["x"].reshape(SEQ, D), "stream": stream, "params": params, "lora": lora, "gains": gains,
            "consts": constants()}


def kernel(**inputs):
    import concourse.bacc as _bacc
    from concourse.bass_utils import run_bass_kernel_spmd as _run

    nc = _bacc.Bacc("TRN2", target_bir_lowering=False, num_devices=1, dynamic_dma_scratch_size=1024)
    arrays, args = {}, []
    for name, a in layout(inputs).items():
        arrays[f"in_{name}"] = np.ascontiguousarray(a)
        args.append(nc.dram_tensor(f"in_{name}", a.shape, F32, kind="ExternalInput").ap())
    out = nc.dram_tensor("out_x", (SEQ, D), F32, kind="ExternalOutput").ap()
    build(nc, *args, out)
    r = _run(nc, [arrays], core_ids=[0])
    return r.results[0]["out_x"].reshape(1, SEQ, D)
```

```python
from contextlib import ExitStack

import numpy as np

from concourse import mybir

F32 = mybir.dt.float32
F32R = mybir.dt.float32r
ALU = mybir.AluOpType
ACT = mybir.ActivationFunctionType
AX = mybir.AxisListType

P = 128
D = 1024
SEQ = 256
NT = SEQ // P
KT = D // P
DEPTH = 2
H = 8
HD = 64
RW = H * HD
JT = RW // P
C = 64
FF = 4 * D
EPS = 1e-6
LN_EPS = 64e-5
DECAY = float(np.exp(np.float32(-0.5)))
GRID_W = 64
KV = 2
QKV = (H + 2 * KV) * HD

UNIT = 8 * P
U_RW = 0
U_AT = U_RW + 15
U_CV = (U_AT + 9, U_AT + 12, U_AT + 21, U_AT + 24)
GATES = 24
U_GATE = [U_AT + (6 if g < 3 else 12 if g < 9 else 18) + g for g in range(GATES)]
U_BRANCH = U_AT + 42
U_OUT = U_BRANCH + 12
U_MLP = U_OUT + KT
UNITS = U_MLP + 64
RING = 6
TURNS = UNITS // RING
REST = UNITS % RING

PARAMS = {}
_at = 0
for _name, _n in (("norm1_g", KT), ("norm2_g", KT), ("mu_prev", 15), ("mu_next", 15), ("w0", 8), ("a0", 8),
                  ("k_k", 4), ("k_a", 4), ("r_k", 4), ("ln_g", 4), ("ln_b", 4), ("cv_w", 12), ("cv_b", 4)):
    PARAMS[_name] = _at
    _at += _n
NPAR = _at
D_MU, D_W0, D_A0, D_KA, D_KB = 0, 15, 23, 31, 35
NDER = 39

LEVELS = (1, 2, 4, 8, 16, 32)
CONST = {}
_at = 0
for _name, _n in (("ident", P), ("sel", P), ("rope_c", NT * HD), ("rope_s", NT * HD), ("reset", SEQ),
                  ("incl", 2 * 2 * P), ("first", 2 * P), ("level", 2 * 5 * C), ("headsum", 2)):
    CONST[_name] = _at
    _at += _n
NCONST = _at


class Signal:

    def __init__(self, sem, per, start=0):
        self.sem, self.per, self.start = sem, per, start

    def after(self, layer, n):
        return self.sem, layer * self.per + (self.start + n)


def build(nc, x_in, stream, params, lora, gains, consts, out):
    with ExitStack() as ctx:
        sem = lambda name: ctx.enter_context(nc.semaphore(name))
        sig = lambda name, per, start=0: Signal(sem(name), per, start)
        bank = [ctx.enter_context(nc.psum_tensor(f"bank{i}", [P, 512], F32)) for i in range(8)]

        place = [nc.sbuf_base + (-nc.sbuf_base) % 32]

        def sb(name, shape, dt=F32):
            size = 4 * int(np.prod(shape[1:]))
            t = nc.alloc_sbuf_tensor_at(name, shape, dt, offset=place[0])
            place[0] += size + (-size) % 32
            return t

        raw = sb("raw", [P, RING, UNIT])
        w_hi = sb("w_hi", [P, RING, UNIT], F32R)
        w_lo = sb("w_lo", [P, RING, UNIT], F32R)
        x = sb("x", [P, NT, D])
        h_hi = sb("h_hi", [P, KT, SEQ], F32R)
        h_lo = sb("h_lo", [P, KT, SEQ], F32R)
        y_at = place[0]
        y_hi = sb("y_hi", [P, JT, SEQ], F32R)
        y_lo = sb("y_lo", [P, JT, SEQ], F32R)
        qkv = sb("qkv", [P, NT, QKV])
        a_st = sb("a_st", [P, 3, 20])
        gth_first = sb("gth_first", [P, 9, SEQ])
        cst = sb("cst", [P, NCONST])
        par = sb("par", [P, NPAR])
        der = sb("der", [P, NDER])
        lor = sb("lor", [P, 3, RW])
        gain = sb("gain", [P, 2 * HD])
        stat = sb("stat", [P, NT, 2])
        sum2 = sb("sum2", [P, 2])
        mean2 = sb("mean2", [P, 2])
        rstd = sb("rstd", [P, 2])
        mhalf = sb("mhalf", [P, 20])
        overlay = place[0]

        z = sb("z", [P, 15, SEQ])
        ksum = sb("ksum", [P, JT, SEQ])
        v_tok = sb("v_tok", [P, NT, RW])
        a_t = sb("a_t", [P, JT, SEQ])
        lw = sb("lw", [P, JT, SEQ])
        cum = sb("cum", [P, JT, SEQ])
        e_cum = sb("e_cum", [P, JT, SEQ])
        kr = sb("kr", [P, JT, NT, 4, C])
        kh = sb("kh", [P, JT, SEQ])
        gates_at = place[0]
        bh = sb("bh", [P, JT, SEQ])
        kh_tok = sb("kh_tok", [P, NT, RW])
        bh_tok = sb("bh_tok", [P, NT, RW])
        bq = sb("bq", [P, H, 4, C])
        kq = sb("kq", [P, H, 4, C])
        xt = sb("xt", [P, H, P])
        state = sb("state", [P, JT, P])
        small = sb("small", [P, 4, 16])
        cc = sb("cc", [P, SEQ])
        cz = sb("cz", [P, SEQ + 2])
        kk = nc.alloc_sbuf_tensor_at("kk", [P, JT, SEQ], F32, offset=y_at)
        y_tok = nc.alloc_sbuf_tensor_at("y_tok", [P, NT, RW], F32, offset=y_at + 4 * JT * SEQ)
        assert place[0] <= nc.sbuf_usable_end, (place[0], nc.sbuf_usable_end)
        xm = a_t[:, :, :].rearrange("p j (e s) -> p (j e) s", e=2)
        zm = cum[:, :, :].rearrange("p j (e s) -> p (j e) s", e=2)
        r_b = lw[:, 0:2, :].rearrange("p a b -> p (a b)")
        u_b = lw[:, 2:4, :].rearrange("p a b -> p (a b)")
        kk_sq = e_cum
        y_flat = y_tok[:, :, :].rearrange("p t c -> p (t c)")
        rn_t = kh[0:2, :, :].rearrange("p a b -> p (a b)")
        bonus_v = kq[:, 0:4, :, :].rearrange("p a b c -> p (a b c)")
        cv = z[:, 8:12, :]
        xn1 = z[:, 0:8, :].rearrange("p (t a) b -> p t (a b)", t=2)

        place[0] = overlay
        yb_hi = sb("yb_hi", [P, 2 * JT, SEQ], F32R)
        yb_lo = sb("yb_lo", [P, 2 * JT, SEQ], F32R)
        m_hi = sb("m_hi", [P, KT, SEQ], F32R)
        twice = nc.alloc_sbuf_tensor_at("twice", [P, KT, SEQ], F32, offset=place[0])
        m_lo = sb("m_lo", [P, KT, SEQ], F32R)
        overlay3 = place[0]
        q_cos = sb("q_cos", [P, NT, (H + KV) * HD])
        q_rt = sb("q_rt", [P, NT, (H + KV) * HD])
        rot = sb("rot", [P, NT, (H + KV) * HD])
        assert place[0] <= gates_at
        place[0] = gates_at
        gth_rest = sb("gth_rest", [P, GATES - 9, SEQ])
        q_t = sb("q_t", [P, 4, SEQ])
        k_t = sb("k_t", [P, SEQ])
        prob = sb("prob", [P, 2, NT, SEQ])
        p_t = sb("p_t", [P, 2, NT, SEQ])
        nmx = sb("nmx", [P, 8, NT])
        rsum = sb("rsum", [P, 8, NT])
        rinv = sb("rinv", [P, 8, NT])
        gmul = sb("gmul", [P, 2, 2, SEQ])
        assert place[0] <= nc.sbuf_usable_end, (place[0], nc.sbuf_usable_end)
        place[0] = overlay3
        xn2 = sb("xn2", [P, NT, D])
        relu = sb("relu", [P, 3, 512])
        usq = sb("usq", [P, 3, 512])
        u_hi = sb("u_hi", [P, 3, 2, SEQ], F32R)
        u_lo = sb("u_lo", [P, 3, 2, SEQ], F32R)
        assert place[0] <= nc.sbuf_usable_end, (place[0], nc.sbuf_usable_end)

        def gates(g, n):
            return gth_first[:, g:g + n, :] if g < 9 else gth_rest[:, g - 9:g - 9 + n, :]

        def gate_bank(g):
            return g if g < 3 else 4 + (g - 3) % 4 if g < 9 else 2 + g % 2

        def updates(n):
            return n - n // 4

        def con(name, n, at=0, rows=P):
            return cst[0:rows, CONST[name] + at:CONST[name] + at + n]

        def par_of(name, i):
            return par[:, PARAMS[name] + i:PARAMS[name] + i + 1]

        ident = con("ident", P)

        ident_in = sem("ident_in")
        consts_in = sem("consts_in")
        out_s = sem("out_written")
        half_s = sem("exponent_set")
        landed = [sem(f"landed{i}") for i in range(RING)]
        pars_in = sem("pars_in")
        lora_in = sem("lora_in")
        gains_in = sem("gains_in")
        hi_ready = sig("hi_ready", UNITS)
        lo_ready = sig("lo_ready", UNITS, 3)
        unit_used = sig("unit_used", UNITS, 6)
        derived = sig("derived", 1)
        x_new = sig("x_new", 8, 4)
        x_loaded = sem("x_loaded")
        sums_s = sig("update_summed", 4)
        sumsq = sig("sumsq", 8)
        meansq = sig("meansq", 4)
        rstd_s = sig("rstd_ready", 4)
        xn_s = sig("xn_ready", 2)
        xn1_s = sig("xn1_ready", 2)
        ht_ps = sig("ht_in_psum", 16)
        hhi_s = sig("h_hi_ready", 16)
        hlo_s = sig("h_lo_ready", 16)
        rw_sc = sig("rw_scaled", 15)
        rw_sh = sig("rw_shifted", 15)
        lora_act = sig("lora_inputs_ready", 2)
        kksq_s = sig("kk_squared", 1)
        nrm_ps = sig("kk_norm_in_psum", 1)
        nrm_mx = sig("kk_norm_guarded", 1)
        nrm_rs = sig("kk_rnorm", 1)
        vt_ps = sig("v_tok_in_psum", 2)
        vt_s = sig("v_tok_ready", 2)
        rnt_ps = sig("rnorm_t_in_psum", 1)
        rnt_s = sig("rnorm_t_ready", 2)
        kkn_ps = sig("rnorm_spread_in_psum", 2)
        kk_s = sig("kk_ready", 2)
        lora_ps = sig("lora_in_psum", 8)
        lora_th = sig("lora_tanh", 4)
        fk_s = sig("k_factor_ready", 2)
        cum_s = sig("cum_ready", 2)
        exp_s = sig("exps_ready", 6)
        kr_s = sig("kr_ready", 2)
        khb_s = sig("khat_bhat_ready", 4)
        tok_ps = sig("hat_tok_in_psum", 8)
        tok_s = sig("hat_tok_ready", 8)
        st_zero = sig("state_cleared", 2)
        bq_ps = sig("bq_in_psum", 16)
        bq_s = sig("bq_masked", 16)
        kq_ps = sig("kq_in_psum", 16)
        kq_s = sig("kq_masked", 16)
        xi_s = sig("xt_started", 8)
        x_up = sig("x_updated", 8 * 4)
        xt_ps = sig("xt_in_psum", 8 * 5)
        xt_s = sig("xt_ready", 8 * 5)
        xt_up = sig("xt_updated", 8)
        zl_ps = sig("z_in_psum", 8 * 5)
        zl_s = sig("z_ready", 8 * 5)
        xz_ps = sig("xz_in_psum", 8 * 4)
        zx_ps = sig("zx_in_psum", 8)
        r_ps = sig("rhs_in_psum", 8)
        r_s = sig("rhs_ready", 8)
        u_ps = sig("u_in_psum", 8)
        u_s = sig("u_ready", 8)
        st_ps = sig("state_in_psum", 6)
        st_s = sig("state_ready", 6)
        y_ps = sig("y_in_psum", 4)
        y0_s = sig("y_copied", 2)
        y1_s = sig("y_added", 2)
        gn_var = sig("gn_var", 1)
        gn_rs = sig("gn_rstd", 1)
        yn_s = sig("yn_ready", 1)
        yt_ps = sig("yt_in_psum", 2)
        bon_in = sig("bonus_in", 1)
        bon_ps = sig("bonus_sums_in_psum", 1)
        bv_s = sig("bonus_v_ready", 1)
        bt_ps = sig("bonus_v_t_in_psum", 2)
        gd_s = sig("gd_ready", 1)
        g_ps = sig("g_in_psum", 2)
        yl_s = sig("y_affine", 2)
        yo_s = sig("y_gated", 2)
        yhi_s = sig("y_hi_ready", 1)
        ylo_s = sig("y_lo_ready", 1)
        cc_s = sig("c_gate_ready", 4)
        cx_s = sig("cx_ready", 4)
        cv_s = sig("cv_ready", 4)
        cvhi_s = sig("cv_hi_ready", 1)
        cvlo_s = sig("cv_lo_ready", 1)
        at_ps = sig("qkv_in_psum", 2)
        at_s = sig("qkv_ready", 4)
        qsq_s = sig("q_cosuared", 3)
        qss_s = sig("q_meansq", 1)
        qrs_s = sig("q_rstd", 1)
        qn_s = sig("q_normalised", 1)
        rope_s = sig("roped", 2)
        qt_ps = sig("qt_in_psum", 3)
        qt_s = sig("qt_ready", 3)
        sc_ps = sig("scores_in_psum", 8)
        mx_s = sig("max_ready", 8)
        pe_s = sig("exp_ready", 8)
        pn_s = sig("prob_ready", 8)
        pt_ps = sig("pt_in_psum", 8)
        pt_s = sig("pt_ready", 8)
        o_ps = sig("o_in_psum", 8)
        ohi_s = sig("o_hi_ready", 2)
        olo_s = sig("o_lo_ready", 2)
        g3_s = sig("gate_tanh", 24)
        part_s = sig("two_branches_merged", 8)
        mg_s = sig("merged", 8)
        mhi_s = sig("m_hi_ready", 8)
        mlo_s = sig("m_lo_ready", 8)
        rl_s = sig("relu_ready", 16)
        us_s = sig("u_squared", 16)
        uhi_s = sig("u_hi_ready", 16)
        ulo_s = sig("u_lo_ready", 16)
        dve_step = sem("dve_step")

        block = ctx.enter_context(nc.Block())
        chunk_bank = (bank[6], bank[0])
        rows_of = (slice(0, C), slice(C, P))
        HATS_ORDER = (2, 0, 3, 1)
        tiles_of = ((0, 1), (1, 0))
        MLP_BODY = 12


        def level_mask(d, i):
            return con("level", C, (d * 5 + i - 1) * C).unsqueeze(1).to_broadcast([P, 8, C])

        def first_mask(d):
            return con("first", P, d * P).unsqueeze(1).to_broadcast([P, 4, P])

        def k_part(v):
            return v[:, :, 1:3, :].rearrange("p a b q -> p a (b q)")

        def by_chunk(v):
            return v.rearrange("p a (c t) -> p (a c) t", t=C)

        def incl_mask(d):
            return con("incl", 2 * P, d * 2 * P).unsqueeze(1).to_broadcast([P, 2, 2 * P])

        def ht_bank(n, k):
            return bank[(k + 4 * n) % 8]

        ident4 = ident.unsqueeze(1).to_broadcast([P, 4, P])

        @block.sync
        def _(sp):
            sp.dma_start(x[:, :, :], x_in.rearrange("(t p) d -> p t d", p=P)).then_inc(x_loaded, 16)
            sp.dma_start(cst[:, 0:P], consts[:, 0:P]).then_inc(ident_in, 16)
            with sp.Fori(0, DEPTH) as l:
                def load(u, at):
                    sp.wait_ge(*lo_ready.after(l, at + 1))
                    sp.dma_start(raw[:, u % RING, :], stream[l, u]).then_inc(landed[u % RING], 16)

                for u in range(REST):
                    load(u, u - REST)
                sp.wait_ge(*x_new.after(l, 0))
                sp.dma_start(par[:, :], params[l]).then_inc(pars_in, 16)
                for u in range(REST, RING):
                    load(u, u - RING)
                sp.dma_start(cst[:, P:], consts[:, P:]).then_inc(consts_in, 16)
                sp.dma_start(lor[:, :, :], lora[l]).then_inc(lora_in, 16)
                sp.dma_start(gain[:, :], gains[l].partition_broadcast(P)).then_inc(gains_in, 16)
                with sp.Fori(1, TURNS) as c:
                    for s in range(RING):
                        sp.wait_ge(*lo_ready.after(l, c * RING + (s - RING + 1)))
                        sp.dma_start(raw[:, s, :], stream[l, c * RING + s]).then_inc(landed[s], 16)
                for u in range(RING * TURNS, UNITS):
                    load(u, u - RING)
            sp.wait_ge(*x_new.after(DEPTH, 0))
            sp.dma_start(out.rearrange("(t p) d -> p t d", p=P), x[:, :, :]).then_inc(out_s, 16)
            sp.wait_ge(out_s, 16)

        @block.gpsimd
        def _(pool):
            pool.sem_inc(lo_ready.sem, 3)
            pool.memset(mhalf[:, :], -0.5).then_inc(half_s, 1)
            pool.wait_ge(half_s, 1)
            with pool.Fori(0, DEPTH) as l:
                def lo(u, it=0):
                    s = u % RING
                    pool.wait_ge(*hi_ready.after(l, it * MLP_BODY + u + 1))
                    pool.tensor_tensor(w_lo[:, s, :], raw[:, s, :],
                                       w_hi[:, s, :].bitcast(F32), ALU.subtract).then_inc(lo_ready.sem, 1)

                def rsqrt(o, i, n):
                    return pool.tensor_tensor(o, i, mhalf[:, 0:n], ALU.pow)

                def rsqrt_rows(n):
                    for t in range(NT):
                        pool.wait_ge(*meansq.after(l, 2 * n + t + 1))
                        rsqrt(rstd[:, t:t + 1], mean2[:, t:t + 1], 1).then_inc(rstd_s.sem, 1)

                rsqrt_rows(0)
                for u in range(U_AT + RING):
                    lo(u)
                pool.wait_ge(*nrm_mx.after(l, 1))
                rsqrt(small[:, 1, :], small[:, 0, :], 16).then_inc(nrm_rs.sem, 1)
                for u in range(U_GATE[0], U_CV[1] + 3):
                    lo(u)
                pool.wait_ge(*at_s.after(l, 4))
                split_at = 2 * RW - (H + KV) * HD
                for o, v in ((y_flat[:, 0:(H + KV) * HD], qkv[:, 0, 0:(H + KV) * HD]),
                             (y_flat[:, (H + KV) * HD:], qkv[:, 1, 0:split_at]),
                             (cc[:, :], qkv[:, 1, split_at:(H + KV) * HD])):
                    pool.tensor_tensor(o, v, v, ALU.mult).then_inc(qsq_s.sem, 1)
                pool.wait_ge(*qss_s.after(l, 1))
                rsqrt(a_st[:, 1, :], a_st[:, 0, :], 20).then_inc(qrs_s.sem, 1)
                for u in range(U_GATE[3], U_GATE[13]):
                    lo(u)
                pool.wait_ge(*gn_var.after(l, 1))
                rsqrt(small[:, 3, :], small[:, 2, :], 16).then_inc(gn_rs.sem, 1)
                for u in range(U_GATE[13], U_MLP + RING - 2):
                    lo(u)
                rsqrt_rows(1)
                for u in range(U_MLP + RING - 2, U_MLP + 2 + MLP_BODY):
                    lo(u)
                with pool.Fori(1, 5) as it:
                    for u in range(U_MLP + 2, U_MLP + 2 + MLP_BODY):
                        lo(u, it)
                for u in range(UNITS - 2, UNITS):
                    lo(u)

        @block.scalar
        def _(act):
            with act.Fori(0, DEPTH) as l:
                def split(u, it=0):
                    s = u % RING
                    loads = TURNS + (1 if s < REST else 0)
                    act.wait_ge(landed[s], (l * loads + it * (MLP_BODY // RING) + (u // RING + 1)) * 16)
                    before = u - (RING if u >= RING else REST if u < REST else REST + RING)
                    act.wait_ge(*unit_used.after(l, it * MLP_BODY + (before + 1)))
                    act.activation(w_hi[:, s, :], raw[:, s, :],
                                   ACT.Copy).then_inc(hi_ready.sem, 1)

                def norm(n, xn):
                    for t in range(NT):
                        for i in range(2):
                            half = slice(i * 512, (i + 1) * 512)
                            act.wait_ge(*x_new.after(l, 4 * n - 3 + 2 * t + i))
                            act.activation(xn[:, t, half], x[:, t, half], ACT.Square,
                                           accum_out=stat[:, t, i:i + 1]).then_inc(sumsq.sem, 1)
                        if n == 0 and t == 0:
                            split(0)
                    act.wait_ge(*rstd_s.after(l, 2 * n + 1))
                    act.activation(xn[:, 0, :], x[:, 0, :], ACT.Identity, scale=rstd[:, 0:1]).then_inc(xn_s.sem, 1)
                    if n == 0:
                        split(1)
                        act.wait_ge(pars_in, (l + 1) * 16)
                    for k in range(KT):
                        act.wait_ge(*ht_ps.after(l, KT * n + k + 1))
                        act.activation(h_hi[:, k, :], ht_bank(n, k)[:, 0:SEQ], ACT.Identity,
                                       scale=par_of(f"norm{n + 1}_g", k)).then_inc(hhi_s.sem, 1)
                        if n == 0 and k == 3:
                            split(2)
                    if n:
                        for u in range(2):
                            split(U_MLP + RING - 2 + u)

                norm(0, xn1)
                for u in range(3, RING):
                    split(u)

                act.wait_ge(*derived.after(l, 1))
                def attention_inputs(a):
                    for t in range(NT):
                        act.wait_ge(*(unit_used.after(l, U_AT + 3 * a + 3) if t else at_ps.after(l, a + 1)))
                        act.activation(qkv[:, t, a * 384:(a + 1) * 384], bank[6 + t][:, 0:384],
                                       ACT.Copy).then_inc(at_s.sem, 1)

                def gate(g):
                    act.wait_ge(*unit_used.after(l, U_GATE[g] + 1))
                    act.activation(gates(g, 1).rearrange("p a b -> p (a b)"), bank[gate_bank(g)][:, 0:SEQ], ACT.Tanh,
                                   scale=0.5).then_inc(g3_s.sem, 1)

                def split3(u):
                    for k in range(3):
                        split(u + k)

                for u in range(U_AT):
                    act.wait_ge(*unit_used.after(l, u + 1))
                    act.activation(z[:, u, :], bank[u % 4][:, 0:SEQ], ACT.Identity,
                                   scale=der[:, D_MU + u:D_MU + u + 1]).then_inc(rw_sc.sem, 1)
                    split(u + RING)
                act.wait_ge(*rw_sh.after(l, 15))
                act.activation(z[:, 12, :], z[:, 12, :], ACT.Tanh).then_inc(lora_act.sem, 1)
                act.activation(z[:, 14, :], z[:, 14, :], ACT.Tanh, scale=0.5).then_inc(lora_act.sem, 1)
                attention_inputs(0)
                for t in range(NT):
                    act.wait_ge(*vt_ps.after(l, t + 1))
                    act.activation(v_tok[:, t, :], bank[4 + t][:, :], ACT.Copy).then_inc(vt_s.sem, 1)

                for d in range(2):
                    if d:
                        act.wait_ge(*y_ps.after(l, 2))
                    for part, th in enumerate((lw, a_t)):
                        for j in range(JT):
                            if j % 2 == 0:
                                act.wait_ge(*lora_ps.after(l, 4 * d + 2 * part + j // 2 + 1))
                            at = (D_W0, D_A0)[part] + JT * d + j
                            ps = bank[2 * part + j // 2]
                            ins = act.activation(th[:, j, :], ps[:, (j % 2) * SEQ:(j % 2 + 1) * SEQ], ACT.Tanh,
                                                 scale=0.5, bias=der[:, at:at + 1])
                        ins.then_inc(lora_th.sem, 1)
                    act.wait_ge(*lora_th.after(l, 2 * d + 2))
                    for j in range(JT):
                        ins = act.activation(bh[:, j, :], a_t[:, j, :], ACT.Identity,
                                             scale=der[:, D_KA + j:D_KA + j + 1], bias=der[:, D_KB + j:D_KB + j + 1])
                    ins.then_inc(fk_s.sem, 1)
                    if d == 0:
                        act.wait_ge(*rnt_ps.after(l, 1))
                        for b in range(2):
                            act.activation(rn_t[:, b * 512:(b + 1) * 512], bank[4 + b][0:2, :],
                                           ACT.Copy).then_inc(rnt_s.sem, 1)
                        split3(U_GATE[0])
                    if d:
                        gate(3)
                        gate(4)
                    act.wait_ge(*cum_s.after(l, d + 1))
                    act.activation(e_cum[:, :, :], cum[:, :, :], ACT.Exp).then_inc(exp_s.sem, 1)
                    act.activation(lw[:, :, :], lw[:, :, :], ACT.Exp).then_inc(exp_s.sem, 1)
                    act.activation(cum[:, :, :], cum[:, :, :], ACT.Exp, scale=-1.0).then_inc(exp_s.sem, 1)
                    if d:
                        for k in range(5, 9):
                            gate(k)
                    else:
                        attention_inputs(1)
                        split3(U_CV[0])
                        for k in range(3):
                            gate(k)
                    for i, (o, t) in enumerate(((kh_tok, 0), (kh_tok, 1), (bh_tok, 0), (bh_tok, 1))):
                        act.wait_ge(*tok_ps.after(l, 4 * d + i + 1))
                        act.activation(o[:, t, :], bank[4 + i][:, :], ACT.Copy).then_inc(tok_s.sem, 1)
                    for k in range(2) if d else (1,):
                        split3(U_CV[2 * d + k])
                    for i, t in enumerate(tiles_of[d]):
                        g = 2 * d + i
                        for li in range(5):
                            for e in range(2):
                                act.wait_ge(*xt_ps.after(l, 10 * g + 2 * li + e + 1))
                                o = (xt if li else xm)[:, 4 * e:4 * e + 4, :].rearrange("p a b -> p (a b)")
                                act.activation(o, bank[4 + e][:, :], ACT.Copy).then_inc(xt_s.sem, 1)
                        for ci, c in enumerate(tiles_of[d]):
                            n, q = 2 * g + ci, C * c
                            act.wait_ge(*r_ps.after(l, n + 1))
                            act.activation(r_b[q:q + C, :], chunk_bank[c][rows_of[1 - c], :],
                                           ACT.Copy).then_inc(r_s.sem, 1)
                            act.wait_ge(*u_ps.after(l, n + 1))
                            act.activation(u_b[q:q + C, :], bank[7][q:q + C, :], ACT.Copy,
                                           scale=-1.0).then_inc(u_s.sem, 1)
                            if ci == 0:
                                act.wait_ge(*unit_used.after(l, U_CV[g] + 1))
                                act.wait_ge(*(cv_s.after(l, g) if g else qss_s.after(l, 1)))
                                act.activation(cc[:, :], bank[2][:, 0:SEQ], ACT.Copy).then_inc(cc_s.sem, 1)
                        if d == 0:
                            act.wait_ge(*y_ps.after(l, g + 1))
                            for c in tiles_of[d]:
                                r = rows_of[c]
                                ins = act.activation(y_tok[r, t, :], chunk_bank[c][r, :], ACT.Copy)
                            ins.then_inc(y0_s.sem, 1)
                        split3(U_CV[g] + RING)
                for k in range(9, 17):
                    gate(k)
                    split(U_GATE[k] + RING)
                act.wait_ge(*cv_s.after(l, JT))
                act.wait_ge(*bon_in.after(l, 1))
                act.activation(yb_hi[:, 0:JT, :], cv, ACT.Copy).then_inc(cvhi_s.sem, 1)
                for j in range(JT):
                    if j % 2 == 0:
                        act.wait_ge(*yt_ps.after(l, j // 2 + 1))
                    ins = act.activation(e_cum[:, j, :], bank[j // 2][:, (j % 2) * SEQ:(j % 2 + 1) * SEQ], ACT.Identity,
                                         scale=par_of("ln_g", j), bias=par_of("ln_b", j))
                    if j % 2:
                        ins.then_inc(yl_s.sem, 1)
                act.wait_ge(*yo_s.after(l, 2))
                act.activation(y_hi[:, :, :], kh[:, :, :], ACT.Copy).then_inc(yhi_s.sem, 1)

                for k in range(17, 21):
                    gate(k)
                    split(U_GATE[k] + RING)

                for i in range(2):
                    act.wait_ge(*qt_ps.after(l, i + 1))
                    act.activation(q_t[:, 2 * i:2 * i + 2, :].rearrange("p a b -> p (a b)"), bank[4 + i][:, :],
                                   ACT.Copy, scale=HD ** -0.5).then_inc(qt_s.sem, 1)
                act.wait_ge(*qt_ps.after(l, 3))
                act.activation(k_t[:, :], bank[6][:, 0:SEQ], ACT.Copy).then_inc(qt_s.sem, 1)

                def exps(i):
                    b = i % 2
                    act.wait_ge(*mx_s.after(l, i + 1))
                    if i >= 2:
                        act.wait_ge(*pt_ps.after(l, i - 1))
                    for t in range(NT):
                        ins = act.activation(prob[:, i % 2, t, :], bank[b][:, t * SEQ:(t + 1) * SEQ], ACT.Exp,
                                             bias=nmx[:, i, t:t + 1], accum_out=rsum[:, i, t:t + 1])
                    ins.then_inc(pe_s.sem, 1)

                gate(21)
                split(U_GATE[21] + RING)
                exps(0)
                exps(1)
                gate(22)
                split(U_GATE[22] + RING)
                for i in range(H):
                    act.wait_ge(*pt_ps.after(l, i + 1))
                    if i >= 2:
                        act.wait_ge(*o_ps.after(l, i - 1))
                    act.activation(p_t[:, i % 2, :, :].rearrange("p a b -> p (a b)"), bank[4 + i % 2][:, :],
                                   ACT.Copy).then_inc(pt_s.sem, 1)
                    if i + 2 < H:
                        exps(i + 2)
                    if i == 0:
                        gate(23)
                    split(U_GATE[23] + RING + i)
                act.wait_ge(*o_ps.after(l, H))
                for b in range(2):
                    act.activation(yb_hi[:, JT + 2 * b:JT + 2 * b + 2, :].rearrange("p a b -> p (a b)"),
                                   bank[6 + b][:, :], ACT.Copy).then_inc(ohi_s.sem, 1)

                split(U_BRANCH + RING + 7)
                for i in range(4):
                    split(U_BRANCH + RING + 8 + i)
                    for k in range(2):
                        act.wait_ge(*mg_s.after(l, 2 * i + k + 1))
                        act.activation(m_hi[:, 2 * i + k, :], twice[:, 2 * i + k, :], ACT.Copy,
                                       scale=0.5).then_inc(mhi_s.sem, 1)
                for k in range(KT - 2):
                    split(U_OUT + k + RING)

                norm(1, xn2)

                def square(p, it=0):
                    s = p % 3
                    act.wait_ge(*unit_used.after(l, it * MLP_BODY + U_MLP + (4 * p if p else 2)))
                    act.activation(relu[:, s, :], bank[4 + s][:, :], ACT.Relu).then_inc(rl_s.sem, 1)

                def round_u(p, it=0):
                    s = p % 3
                    act.wait_ge(*us_s.after(l, 3 * it + p + 1))
                    act.activation(u_hi[:, s, :, :].rearrange("p a b -> p (a b)"), usq[:, s, :],
                                   ACT.Copy).then_inc(uhi_s.sem, 1)

                def pair(p, it=0):
                    u0 = U_MLP + 2 + 4 * (p - 1)
                    square(p, it)
                    for k in range(4):
                        if k == 2:
                            round_u(p, it)
                        if u0 + k + RING < UNITS:
                            split(u0 + k + RING, it)

                square(0)
                for k in range(2):
                    split(U_MLP + k + RING)
                round_u(0)
                for p in range(1, 4):
                    pair(p)
                with act.Fori(1, 4) as it:
                    for p in range(1, 4):
                        pair(p, it)
                for p in range(13, 16):
                    pair(p)

        @block.vector
        def _(dve):
            dve.wait_ge(x_loaded, 16)
            dve.sem_inc(x_new.sem, 4)
            with dve.Fori(0, DEPTH) as l:
                count = [0]

                def then(ins):
                    count[0] += 1
                    ins.then_inc(dve_step, 1)
                    dve.wait_ge(dve_step, count[0])

                def norm(n, xn):
                    for t in range(NT):
                        dve.wait_ge(*sumsq.after(l, 4 * n + 2 * t + 2))
                        then(dve.tensor_tensor(sum2[:, t:t + 1], stat[:, t, 0:1], stat[:, t, 1:2], ALU.add))
                        dve.tensor_scalar(mean2[:, t:t + 1], sum2[:, t:t + 1], 1.0 / D, EPS, ALU.mult,
                                          ALU.add).then_inc(meansq.sem, 1)
                    dve.wait_ge(*rstd_s.after(l, 2 * n + 2))
                    dve.tensor_scalar(xn[:, 1, :], x[:, 1, :], rstd[:, 1:2], None, ALU.mult).then_inc(xn1_s.sem, 1)
                    if n == 0:
                        derive()
                    for k in range(KT):
                        dve.wait_ge(*hhi_s.after(l, KT * n + k + 1))
                        dve.scalar_tensor_tensor(h_lo[:, k, :], ht_bank(n, k)[:, 0:SEQ], par_of(f"norm{n + 1}_g", k),
                                                 h_hi[:, k, :].bitcast(F32), ALU.mult,
                                                 ALU.subtract).then_inc(hlo_s.sem, 1)

                def derive():
                    dve.wait_ge(pars_in, (l + 1) * 16)
                    mp, mn = (par[:, PARAMS[k]:PARAMS[k] + 15] for k in ("mu_prev", "mu_next"))
                    mu = der[:, D_MU:D_MU + 15]
                    dve.tensor_scalar(der[:, D_W0:D_W0 + 16], par[:, PARAMS["w0"]:PARAMS["w0"] + 16], 0.5, None,
                                      ALU.mult)
                    ka = par[:, PARAMS["k_a"]:PARAMS["k_a"] + 4]
                    dve.tensor_scalar(der[:, D_KA:D_KA + 4], ka, 0.5, None, ALU.mult)
                    dve.tensor_scalar(der[:, D_KB:D_KB + 4], ka, -0.5, 1.0, ALU.mult, ALU.add)
                    then(dve.tensor_tensor(mu, mp, mn, ALU.add))
                    dve.tensor_scalar(mu, mu, -1.0, 1.0, ALU.mult, ALU.add).then_inc(derived.sem, 1)

                norm(0, xn1)

                NH = H + KV
                for u in range(U_AT):
                    ps = bank[u % 4]
                    dve.wait_ge(*rw_sc.after(l, u + 1))
                    then(dve.scalar_tensor_tensor(z[:, u, 1:SEQ], ps[:, 0:SEQ - 1], par_of("mu_prev", u),
                                                  z[:, u, 1:SEQ], ALU.mult, ALU.add))
                    dve.scalar_tensor_tensor(z[:, u, 0:SEQ - 1], ps[:, 1:SEQ], par_of("mu_next", u),
                                             z[:, u, 0:SEQ - 1], ALU.mult, ALU.add).then_inc(rw_sh.sem, 1)
                dve.wait_ge(*rw_sh.after(l, 15))
                def convolve(i):
                    tap = lambda k: par_of("cv_w", 4 * k + i)
                    dve.wait_ge(*cc_s.after(l, i + 1))
                    dve.wait_ge(*unit_used.after(l, U_CV[i] + 2))
                    dve.tensor_tensor(cz[:, 1:SEQ + 1], bank[3][:, 0:SEQ], cc[:, :], ALU.mult).then_inc(cx_s.sem, 1)
                    dve.wait_ge(*cx_s.after(l, i + 1))
                    then(dve.tensor_scalar(cv[:, i, :], cz[:, 0:SEQ], tap(0), par_of("cv_b", i), ALU.mult, ALU.add))
                    for k in (1, 2):
                        then(dve.scalar_tensor_tensor(cv[:, i, :], cz[:, k:SEQ + k], tap(k), cv[:, i, :],
                                                      ALU.mult, ALU.add))

                def centre(t):
                    y3 = y_tok[:, t, :].rearrange("p (h v) -> p h v", v=HD)
                    sq = kh[:, 2 * t:2 * t + 2, :].rearrange("p j (a v) -> p (j a) v", v=HD)
                    mean = small[:, 0, t * H:(t + 1) * H]
                    then(dve.tensor_reduce(mean, y3, AX.X, ALU.add))
                    then(dve.tensor_scalar(mean, mean, 1.0 / HD, None, ALU.mult))
                    then(dve.tensor_tensor(y3, y3, mean.unsqueeze(2).to_broadcast([P, H, HD]), ALU.subtract))
                    then(dve.tensor_tensor(sq, y3, y3, ALU.mult))
                    then(dve.tensor_reduce(small[:, 2, t * H:(t + 1) * H], sq, AX.X, ALU.add))

                dve.wait_ge(consts_in, (l + 1) * 16)
                for j in range(JT):
                    ins = dve.tensor_scalar(kk[:, j, :], z[:, 4 + j, :], par_of("k_k", j), None, ALU.mult)
                then(ins)
                dve.tensor_tensor(kk_sq[:, :, :], kk[:, :, :], kk[:, :, :], ALU.mult).then_inc(kksq_s.sem, 1)
                dve.memset(cz[:, 0:SEQ + 2:SEQ + 1], 0.0)
                dve.memset(state[:, :, :], 0.0).then_inc(st_zero.sem, 1)
                dve.wait_ge(*nrm_ps.after(l, 1))
                dve.tensor_scalar(small[:, 0, :], bank[7][:, 0:16], 1e-24, None, ALU.max).then_inc(nrm_mx.sem, 1)
                dve.wait_ge(*lora_act.after(l, 2))
                dve.tensor_scalar(z[:, 14, :], z[:, 14, :], 0.5, 0.5, ALU.mult, ALU.add).then_inc(gd_s.sem, 1)

                for d in range(2):
                    dve.wait_ge(*lora_th.after(l, 2 * d + 1))
                    then(dve.tensor_scalar(lw[:, :, :], lw[:, :, :], -DECAY / 2, -DECAY / 2, ALU.mult, ALU.add))
                    for j in range(JT):
                        o, i = cum[:, j, :], lw[:, j, :]
                        if d:
                            o, i = o[:, ::-1], i[:, ::-1]
                        ins = dve.tensor_tensor_scan(o, con("reset", SEQ), i, 0.0, ALU.mult, ALU.add)
                    then(ins)
                    dve.tensor_tensor(lw[:, :, :], cum[:, :, :], lw[:, :, :], ALU.subtract).then_inc(cum_s.sem, 1)
                    dve.wait_ge(*fk_s.after(l, d + 1))
                    kd = bh if d else ksum
                    then(dve.tensor_tensor(kd[:, :, :], bh[:, :, :], z[:, 4:8, :], ALU.mult))
                    if d == 0:
                        for i in range(2):
                            dve.wait_ge(*kkn_ps.after(l, i + 1))
                            v = kk[:, 2 * i:2 * i + 2, :].rearrange("p a b -> p (a b)")
                            dve.tensor_tensor(v, v, bank[4 + i][:, :], ALU.mult).then_inc(kk_s.sem, 1)
                        dve.wait_ge(*kk_s.after(l, 2))
                    else:
                        dve.tensor_tensor(ksum[:, :, :], ksum[:, :, :], bh[:, :, :], ALU.add)
                    then(dve.scalar_tensor_tensor(a_t[:, :, :], a_t[:, :, :], 1.0, kk[:, :, :], ALU.add, ALU.mult))
                    dve.wait_ge(*exp_s.after(l, 3 * d + 1))
                    chunks = lambda v: v.rearrange("p j (t c q) -> p (j t) c q", t=NT, c=2)
                    blocks = kr[:, :, :, :, :].rearrange("p j t b q -> p (j t) b q")
                    dve.tensor_tensor(blocks[:, :, ::3, :], chunks(z[:, 0:4, :]), chunks(e_cum[:, :, :]), ALU.mult)
                    dve.wait_ge(*exp_s.after(l, 3 * d + 2))
                    dve.tensor_tensor(blocks[:, :, 1:3, :], chunks(kk[:, :, :]), chunks(lw[:, :, :]),
                                      ALU.mult).then_inc(kr_s.sem, 1)
                    dve.wait_ge(*exp_s.after(l, 3 * d + 3))
                    dve.tensor_tensor(kh[:, :, :], kd[:, :, :], cum[:, :, :], ALU.mult).then_inc(khb_s.sem, 1)
                    dve.wait_ge(*khb_s.after(l, 2 * d + 1))
                    dve.scalar_tensor_tensor(bh[:, :, :], a_t[:, :, :], 0.5, cum[:, :, :], ALU.mult,
                                             ALU.mult).then_inc(khb_s.sem, 1)

                    if d:
                        dve.wait_ge(*y_ps.after(l, 2))
                        dve.memset(state[:, :, :], 0.0).then_inc(st_zero.sem, 1)
                    for i, t in enumerate(tiles_of[d]):
                        g = 2 * d + i
                        if g:
                            dve.wait_ge(*y_ps.after(l, g))
                        def mask_hats(o, m, ps, done):
                            at = 4 * (m % 2) + 2 * (m // 2)
                            dve.tensor_tensor(o[:, at:at + 2, :, :].rearrange("p a b c -> p a (b c)"),
                                              ps[:, :].rearrange("p (a b) -> p a b", a=2), incl_mask(d),
                                              ALU.mult).then_inc(done.sem, 1)

                        for k, m in enumerate(HATS_ORDER):
                            dve.wait_ge(*bq_ps.after(l, 4 * g + k + 1))
                            mask_hats(bq, m, bank[m], bq_s)
                            if k % 2:
                                e = m % 2
                                v = xt[:, 4 * e:4 * e + 4, :]
                                dve.wait_ge(*bq_s.after(l, 4 * g + k + 1))
                                then(dve.tensor_tensor(v, k_part(bq[:, 4 * e:4 * e + 4, :, :]), first_mask(1 - d),
                                                       ALU.mult))
                                dve.tensor_tensor(v, v, ident4, ALU.add).then_inc(xi_s.sem, 1)
                        for li in range(5):
                            for e in range(2):
                                dve.wait_ge(*zl_ps.after(l, 10 * g + 2 * li + e + 1))
                                dve.tensor_tensor(by_chunk(zm[:, 4 * e:4 * e + 4, :]),
                                                  bank[e][:, :].rearrange("p (a b) -> p a b", a=8),
                                                  level_mask(d, li + 1), ALU.mult).then_inc(zl_s.sem, 1)
                                if li < 4 and e == (li > 0):
                                    m, b, n = ((2, 3, 3), (0, 6, 1), (1, 7, 2), (3, 6, 4))[li]
                                    dve.wait_ge(*kq_ps.after(l, 4 * g + n))
                                    mask_hats(kq, m, bank[b], kq_s)
                            for e in range(2):
                                if li < 4:
                                    v = xm[:, 4 * e:4 * e + 4, :].rearrange("p a b -> p (a b)")
                                    if li:
                                        dve.wait_ge(*x_up.after(l, 8 * g + 2 * li + e - 1))
                                    else:
                                        dve.wait_ge(*xt_s.after(l, 10 * g + e + 1))
                                    dve.wait_ge(*xz_ps.after(l, 8 * g + 2 * li + e + 1))
                                    dve.tensor_tensor(v, v, bank[2 + e][:, :], ALU.add).then_inc(x_up.sem, 1)
                                else:
                                    v = xt[:, 4 * e:4 * e + 4, :].rearrange("p a b -> p (a b)")
                                    dve.wait_ge(*xt_s.after(l, 10 * g + 8 + e + 1))
                                    dve.wait_ge(*zx_ps.after(l, 2 * g + e + 1))
                                    dve.tensor_tensor(v, v, bank[4 + e][:, :], ALU.add).then_inc(xt_up.sem, 1)
                        if g == 0:
                            for k, (src, lo, hi) in enumerate(((y_flat, 0, 16), (cc, 16, 20))):
                                dve.wait_ge(*qsq_s.after(l, k + 2))
                                ins = dve.tensor_reduce(a_st[:, 2, lo:hi], src.rearrange("p (a v) -> p a v", v=HD),
                                                        AX.X, ALU.add)
                            then(ins)
                            dve.tensor_scalar(a_st[:, 0, :], a_st[:, 2, :], 1.0 / HD, EPS, ALU.mult,
                                              ALU.add).then_inc(qss_s.sem, 1)
                        if g == 1:
                            dve.wait_ge(*qrs_s.after(l, 1))
                            dve.wait_ge(gains_in, (l + 1) * 16)
                            heads = lambda t, a, b: qkv[:, t, a * HD:b * HD].rearrange("p (h v) -> p h v", v=HD)
                            for t2 in range(NT):
                                v = heads(t2, 0, NH)
                                rnorm = a_st[:, 1, t2 * NH:(t2 + 1) * NH].unsqueeze(2)
                                ins = dve.tensor_tensor(v, v, rnorm.to_broadcast([P, NH, HD]), ALU.mult)
                            then(ins)
                            for t2 in range(NT):
                                for a, b, m in ((0, H, 0), (H, NH, 1)):
                                    v = heads(t2, a, b)
                                    g_row = gain[:, m * HD:(m + 1) * HD].unsqueeze(1)
                                    ins = dve.tensor_tensor(v, v, g_row.to_broadcast([P, b - a, HD]), ALU.mult)
                            ins.then_inc(qn_s.sem, 1)
                        if g == 3:
                            for j in range(JT):
                                ins = dve.scalar_tensor_tensor(cum[:, j, :], ksum[:, j, :], par_of("r_k", j),
                                                               z[:, j, :], ALU.mult, ALU.mult)
                            ins.then_inc(bon_in.sem, 1)
                            centre(t + 1)
                        for ci, c in enumerate(tiles_of[d]):
                            n = 2 * g + ci
                            last = t * P + c * C + (0 if d else C - 1)
                            if ci:
                                convolve(g)
                            if i and ci:
                                continue
                            dve.wait_ge(*st_ps.after(l, updates(n) + 1))
                            for e in range(2):
                                r = slice(HD * e, HD * (e + 1))
                                v = state[r, :, HD * e:HD * (e + 1)]
                                ins = dve.tensor_tensor(v, v,
                                                        bank[1][r, :].rearrange("p (a b) -> p a b", a=JT)[
                                                            :, :, HD * e:HD * (e + 1)],
                                                        ALU.add)
                            then(ins)
                            for e in range(2):
                                r = slice(HD * e, HD * (e + 1))
                                v = state[r, :, HD * e:HD * (e + 1)]
                                ins = dve.tensor_tensor(v, v,
                                                        e_cum[r, :, last:last + 1].to_broadcast([HD, JT, HD]), ALU.mult)
                            ins.then_inc(st_s.sem, 1)
                            dve.wait_ge(*st_s.after(l, updates(n) + 1))
                        if d:
                            dve.wait_ge(*y_ps.after(l, g + 1))
                            for c in tiles_of[d]:
                                r = rows_of[c]
                                ins = dve.tensor_tensor(y_tok[r, t, :], y_tok[r, t, :], chunk_bank[c][r, :], ALU.add)
                            ins.then_inc(y1_s.sem, 1)

                        if g == 3:
                            dve.wait_ge(*y1_s.after(l, 2))
                            centre(t)
                            dve.tensor_scalar(small[:, 2, :], small[:, 2, :], 1.0 / HD, LN_EPS, ALU.mult,
                                              ALU.add).then_inc(gn_var.sem, 1)
                        dve.wait_ge(*unit_used.after(l, U_CV[g] + 3))
                        dve.tensor_tensor(cv[:, g, :], cv[:, g, :], bank[4][:, 0:SEQ], ALU.mult).then_inc(cv_s.sem, 1)

                y3 = y_tok[:, :, :].rearrange("p t (h v) -> p (t h) v", v=HD)
                spread = lambda i: small[:, i, :].unsqueeze(2).to_broadcast([P, 16, HD])
                dve.wait_ge(*bon_ps.after(l, 1))
                dve.tensor_tensor(bonus_v.rearrange("p (h v) -> p h v", v=HD),
                                  v_tok[:, :, :].rearrange("p t (h v) -> p (t h) v", v=HD),
                                  bank[5][:, 0:16].unsqueeze(2).to_broadcast([P, 16, HD]),
                                  ALU.mult).then_inc(bv_s.sem, 1)
                dve.wait_ge(*gn_rs.after(l, 1))
                dve.tensor_tensor(y3, y3, spread(3), ALU.mult).then_inc(yn_s.sem, 1)
                for i in range(2):
                    js = slice(2 * i, 2 * i + 2)
                    flat = lambda t: t[:, js, :].rearrange("p a b -> p (a b)")
                    dve.wait_ge(*bt_ps.after(l, i + 1))
                    dve.wait_ge(*yl_s.after(l, i + 1))
                    then(dve.scalar_tensor_tensor(flat(e_cum), bank[4 + i][:, :], 0.5, flat(e_cum), ALU.mult, ALU.add))
                    dve.wait_ge(*g_ps.after(l, i + 1))
                    dve.tensor_tensor(flat(kh), flat(e_cum), bank[6 + i][:, :], ALU.mult).then_inc(yo_s.sem, 1)

                heads = lambda v: v.rearrange("p (h v) -> p h v", v=HD)
                dve.wait_ge(*qn_s.after(l, 1))
                for t in range(NT):
                    qn, q2, q3, o = qkv[:, t, 0:NH * HD], q_cos[:, t, :], rot[:, t, :], q_rt[:, t, :]
                    cos = con("rope_c", HD, t * HD).unsqueeze(1).to_broadcast([P, NH, HD])
                    sin = con("rope_s", HD, t * HD).rearrange("p (a b c) -> p a b c", a=2, b=2)
                    dve.tensor_tensor(heads(q2), heads(qn), cos, ALU.mult)
                    for a in range(2):
                        for b in range(2):
                            pick = lambda v, b: v.rearrange("p (h a b c) -> p h a b c", a=2, b=2, c=16)[:, :, a, b, :]
                            ins = dve.tensor_tensor(pick(q3, b), pick(qn, 1 - b),
                                                    sin[:, a, b, :].unsqueeze(1).to_broadcast([P, NH, 16]), ALU.mult)
                    then(ins)
                    q4 = lambda v: v[:, 0:H * HD].rearrange("p (a m v) -> p a m v", a=KV, m=4)
                    dve.tensor_tensor(o[:, 0:H * HD].rearrange("p (m a v) -> p a m v", a=KV, m=4), q4(q2), q4(q3),
                                      ALU.add)
                    dve.tensor_tensor(o[:, H * HD:], q2[:, H * HD:], q3[:, H * HD:], ALU.add).then_inc(rope_s.sem, 1)

                dve.wait_ge(*yhi_s.after(l, 1))
                dve.tensor_tensor(y_lo[:, :, :], kh[:, :, :], y_hi[:, :, :].bitcast(F32),
                                  ALU.subtract).then_inc(ylo_s.sem, 1)
                dve.wait_ge(*cvhi_s.after(l, 1))
                dve.tensor_tensor(yb_lo[:, 0:JT, :], cv, yb_hi[:, 0:JT, :].bitcast(F32),
                                  ALU.subtract).then_inc(cvlo_s.sem, 1)

                def maxes(i):
                    b = i % 2
                    dve.wait_ge(*sc_ps.after(l, i + 1))
                    dve.tensor_reduce(nmx[:, i, :], bank[b][:, :].rearrange("p (t s) -> p t s", t=NT), AX.X, ALU.max,
                                      negate=True).then_inc(mx_s.sem, 1)

                def merge_two(i):
                    dve.wait_ge(*unit_used.after(l, U_BRANCH + 2 * i + 2))
                    if i == 0:
                        dve.wait_ge(*g3_s.after(l, 24))
                    for k in range(2):
                        flat = lambda v: v.rearrange("p a b -> p (a b)")
                        then(dve.scalar_tensor_tensor(flat(gmul[:, k, :, :]), flat(gates(6 * i + 3 * k, 2)), 1.0,
                                                      bank[2 + k][:, :], ALU.add, ALU.mult))
                        dve.tensor_tensor(twice[:, 2 * i + k, :], gmul[:, k, 0, :], gmul[:, k, 1, :],
                                          ALU.add).then_inc(part_s.sem, 1)

                for i in range(2):
                    maxes(i)
                def normalise(i):
                    dve.wait_ge(*pe_s.after(l, i + 1))
                    then(dve.reciprocal(rinv[:, i, :], rsum[:, i, :]))
                    for t in range(NT):
                        ins = dve.tensor_scalar(prob[:, i % 2, t, :], prob[:, i % 2, t, :], rinv[:, i, t:t + 1], None,
                                                ALU.mult)
                    ins.then_inc(pn_s.sem, 1)

                for i in range(H):
                    if i < 3 or i % 2 == 0:
                        normalise(i)
                    if i + 2 < H:
                        maxes(i + 2)
                    if i >= 2 and i % 2 == 0:
                        normalise(i + 1)
                        merge_two(i // 2 - 1)
                for b in range(2):
                    flat = lambda v: v[:, JT + 2 * b:JT + 2 * b + 2, :].rearrange("p a b -> p (a b)")
                    dve.wait_ge(*ohi_s.after(l, b + 1))
                    dve.tensor_tensor(flat(yb_lo), bank[6 + b][:, :], flat(yb_hi).bitcast(F32),
                                      ALU.subtract).then_inc(olo_s.sem, 1)

                merge_two(3)
                dve.wait_ge(*part_s.after(l, KT))
                for i in range(4):
                    dve.wait_ge(*unit_used.after(l, U_BRANCH + KT + i + 1))
                    for k in range(2):
                        th = gates(6 * i + 3 * k + 2, 1).rearrange("p a b -> p (a b)")
                        then(dve.scalar_tensor_tensor(gmul[:, k, 0, :], th, 1.0,
                                                      bank[4 + i][:, k * SEQ:(k + 1) * SEQ], ALU.add, ALU.mult))
                        v = twice[:, 2 * i + k, :]
                        dve.tensor_tensor(v, v, gmul[:, k, 0, :], ALU.add).then_inc(mg_s.sem, 1)
                    for k in range(2):
                        dve.wait_ge(*mhi_s.after(l, 2 * i + k + 1))
                        dve.scalar_tensor_tensor(m_lo[:, 2 * i + k, :], twice[:, 2 * i + k, :], 0.5,
                                                 m_hi[:, 2 * i + k, :].bitcast(F32), ALU.mult,
                                                 ALU.subtract).then_inc(mlo_s.sem, 1)

                def residual(n, last):
                    for t in range(NT):
                        for i in range(2):
                            if i == 0:
                                dve.wait_ge(*sums_s.after(l, 2 * n - 1 + t))
                            elif t:
                                dve.wait_ge(*unit_used.after(l, last))
                            v = x[:, t, i * 512:(i + 1) * 512]
                            dve.tensor_tensor(v, v, bank[2 * t + i][:, :], ALU.add).then_inc(x_new.sem, 1)

                residual(1, U_MLP)
                norm(1, xn2)

                def square(p, it=0):
                    s = p % 3
                    dve.wait_ge(*rl_s.after(l, 3 * it + p + 1))
                    dve.tensor_tensor(usq[:, s, :], relu[:, s, :], bank[4 + s][:, :], ALU.mult).then_inc(us_s.sem, 1)
                    dve.wait_ge(*uhi_s.after(l, 3 * it + p + 1))
                    dve.tensor_tensor(u_lo[:, s, :, :].rearrange("p a b -> p (a b)"), usq[:, s, :],
                                      u_hi[:, s, :, :].rearrange("p a b -> p (a b)").bitcast(F32),
                                      ALU.subtract).then_inc(ulo_s.sem, 1)

                for p in range(4):
                    square(p)
                with dve.Fori(1, 4) as it:
                    for p in range(1, 4):
                        square(p, it)
                for p in range(13, 16):
                    square(p)
                dve.wait_ge(*x_new.after(l, 4))
                residual(2, UNITS)
                dve.sem_clear(dve_step)

        @block.tensor
        def _(pe):
            pe.sem_inc(unit_used.sem, 6)
            pe.wait_ge(ident_in, 16)
            with pe.Fori(0, DEPTH) as l:
                def weights(u, it=0):
                    pe.wait_ge(*lo_ready.after(l, it * MLP_BODY + u + 1))

                def columns(o, s, tiles=KT, width=P, at=0, hi=h_hi, lo=h_lo, base=0, used=True,
                            arriving=None):
                    for k in range(tiles):
                        if arriving is not None:
                            pe.wait_ge(*hlo_s.after(l, arriving + k + 1))
                        c = slice(k * width + at, k * width + at + P)
                        pe.matmul(o, w_hi[:, s, c], hi[:, base + k, :], start=(k == 0), stop=False)
                        pe.matmul(o, w_hi[:, s, c], lo[:, base + k, :], start=False, stop=False)
                        ins = pe.matmul(o, w_lo[:, s, c], hi[:, base + k, :], start=False, stop=(k == tiles - 1))
                    if used:
                        ins.then_inc(unit_used.sem, 1)

                def norm(n, xn):
                    for t, ready in enumerate((xn_s, xn1_s)):
                        pe.wait_ge(*ready.after(l, n + 1))
                        for k in range(KT):
                            ins = pe.transpose(ht_bank(n, k)[:, t * P:(t + 1) * P], xn[:, t, k * P:(k + 1) * P], ident)
                            if t:
                                ins.then_inc(ht_ps.sem, 1)

                norm(0, xn1)
                for u in range(U_AT):
                    weights(u)
                    if u >= 4:
                        pe.wait_ge(*rw_sh.after(l, u - 3))
                    columns(bank[u % 4][:, 0:SEQ], u % RING, arriving=None if u else 0)

                def attention_inputs(a, tiles):
                    s0 = (U_AT + 3 * a) % RING
                    hi, lo = (w[:, s0:s0 + 3, :].rearrange("p a b -> p (a b)") for w in (w_hi, w_lo))
                    weights(U_AT + 3 * a + 2)
                    for t in tiles:
                        tok = slice(t * P, (t + 1) * P)
                        o = bank[6 + t][:, 0:384]
                        for k in range(KT):
                            c = slice(k * 384, (k + 1) * 384)
                            pe.matmul(o, h_hi[:, k, tok], hi[:, c], start=(k == 0), stop=False)
                            pe.matmul(o, h_hi[:, k, tok], lo[:, c], start=False, stop=False)
                            ins = pe.matmul(o, h_lo[:, k, tok], hi[:, c], start=False, stop=(k == KT - 1))
                        if t == 0:
                            ins.then_inc(at_ps.sem, 1)
                        else:
                            ins.then_inc(unit_used.sem, 3)

                def gate(g):
                    weights(U_GATE[g])
                    if g >= 7:
                        pe.wait_ge(*g3_s.after(l, g - 1 if g >= 9 else g - 3))
                    columns(bank[gate_bank(g)][:, 0:SEQ], U_GATE[g] % RING)

                def convolution_half(i, n):
                    u, k0 = U_CV[i] + n // 2, KT // 2 * (n % 2)
                    s = u % RING
                    if k0 == 0:
                        weights(u)
                    o = bank[2 + n // 2][:, 0:SEQ]
                    for k in range(k0, k0 + KT // 2):
                        c = slice(k * P, (k + 1) * P)
                        pe.matmul(o, w_hi[:, s, c], h_hi[:, k, :], start=(k == 0), stop=False)
                        pe.matmul(o, w_hi[:, s, c], h_lo[:, k, :], start=False, stop=False)
                        ins = pe.matmul(o, w_lo[:, s, c], h_hi[:, k, :], start=False, stop=(k == KT - 1))
                    if k0:
                        ins.then_inc(unit_used.sem, 1)

                attention_inputs(0, (0, 1))
                pe.wait_ge(*rw_sh.after(l, 12))
                for t in range(NT):
                    for j in range(JT):
                        ins = pe.transpose(bank[4 + t][:, j * P:(j + 1) * P], z[:, 8 + j, t * P:(t + 1) * P], ident)
                    ins.then_inc(vt_ps.sem, 1)
                def lora_products(d):
                    for part in range(2):
                        for j in range(JT):
                            ins = pe.matmul(bank[2 * part + j // 2][:, (j % 2) * SEQ:(j % 2 + 1) * SEQ],
                                            lor[HD * d:HD * (d + 1), part, j * P:(j + 1) * P],
                                            z[HD * d:HD * (d + 1), 12 + part, :], start=True, stop=True)
                            if j % 2:
                                ins.then_inc(lora_ps.sem, 1)

                for d in range(2):
                    if d == 0:
                        pe.wait_ge(lora_in, (l + 1) * 16)
                        pe.wait_ge(*lora_act.after(l, 1))
                        pe.wait_ge(*rw_sh.after(l, 15))
                    else:
                        pe.wait_ge(*y0_s.after(l, 2))
                        pe.wait_ge(*st_s.after(l, updates(4)))
                        pe.wait_ge(*cx_s.after(l, 2))
                    lora_products(d)
                    if d == 0:
                        pe.wait_ge(consts_in, (l + 1) * 16)
                        pe.wait_ge(*kksq_s.after(l, 1))
                        pe.wait_ge(*at_s.after(l, 2))
                        for t in range(NT):
                            for j in range(JT):
                                ins = pe.matmul(bank[7][:, t * H + 2 * j:t * H + 2 * j + 2],
                                                kk_sq[:, j, t * P:(t + 1) * P], con("headsum", 2), start=True, stop=True)
                        ins.then_inc(nrm_ps.sem, 1)
                        attention_inputs(1, (0,))
                        pe.wait_ge(*nrm_rs.after(l, 1))
                        pe.wait_ge(*vt_s.after(l, 2))
                        for j in range(JT):
                            for t in range(NT):
                                at = (j % 2) * SEQ + t * P
                                ins = pe.transpose(bank[4 + j // 2][0:2, at:at + P],
                                                   small[:, 1, t * H + 2 * j:t * H + 2 * j + 2], ident)
                        ins.then_inc(rnt_ps.sem, 1)
                        attention_inputs(1, (1,))
                        pe.wait_ge(*rnt_s.after(l, 2))
                        for j in range(JT):
                            ins = pe.matmul(bank[4 + j // 2][:, (j % 2) * SEQ:(j % 2 + 1) * SEQ],
                                            con("sel", P, rows=2), rn_t[:, j * SEQ:(j + 1) * SEQ], start=True, stop=True)
                            if j % 2:
                                ins.then_inc(kkn_ps.sem, 1)
                        pe.wait_ge(*lora_th.after(l, 2))
                        for k in range(3):
                            gate(k)
                    else:
                        pe.wait_ge(*cv_s.after(l, 2))
                        for k in range(3, 9):
                            gate(k)
                    for i, src in enumerate((kh, bh)):
                        pe.wait_ge(*khb_s.after(l, 2 * d + i + 1))
                        if i == 0:
                            pe.wait_ge(*(g3_s.after(l, 9) if d else at_s.after(l, 4)))
                        for t in range(NT):
                            for j in range(JT):
                                ins = pe.transpose(bank[4 + 2 * i + t][:, j * P:(j + 1) * P],
                                                   src[:, j, t * P:(t + 1) * P], ident)
                            ins.then_inc(tok_ps.sem, 1)
                    for i, t in enumerate(tiles_of[d]):
                        g = 2 * d + i
                        tok = slice(t * P, (t + 1) * P)
                        pe.wait_ge(*kr_s.after(l, d + 1))
                        pe.wait_ge(*khb_s.after(l, 2 * d + 2))

                        def hats(src, m, b, done):
                            e = slice(HD * (m % 2), HD * (m % 2 + 1))
                            for j in range(2):
                                jj = 2 * (m // 2) + j
                                ins = pe.matmul(bank[b][:, j * SEQ:(j + 1) * SEQ], src[e, jj, tok],
                                                kr[e, jj, t, :, :].rearrange("p b q -> p (b q)"),
                                                start=True, stop=True)
                            ins.then_inc(done.sem, 1)

                        if g == 0:
                            pe.wait_ge(*g3_s.after(l, 3))
                        if i:
                            pe.wait_ge(*cx_s.after(l, g))
                        for m in HATS_ORDER:
                            if i and m == 0:
                                pe.wait_ge(*(y1_s.after(l, 1) if d else y0_s.after(l, 1)))
                                pe.wait_ge(*st_s.after(l, updates(2 * g)))
                            hats(bh, m, m, bq_ps)
                        for li in range(5):
                            def transpose_half(e):
                                for j in range(JT):
                                    ins = pe.transpose(bank[4 + e][:, j * P:(j + 1) * P],
                                                       (xm if li else xt)[:, 4 * e + j, :], ident)
                                ins.then_inc(xt_ps.sem, 1)

                            if li == 0:
                                pe.wait_ge(*tok_s.after(l, 4 * d + 4))
                                if i:
                                    pe.wait_ge(*cv_s.after(l, g))
                                for e in range(2):
                                    hats(kh, e, 6 + e, kq_ps)
                                pe.wait_ge(*xi_s.after(l, 2 * g + 1))
                                transpose_half(0)
                                pe.wait_ge(*bq_s.after(l, 4 * g + 3))
                                hats(kh, 2, 3, kq_ps)
                                pe.wait_ge(*xi_s.after(l, 2 * g + 2))
                                transpose_half(1)
                            for e in range(2):
                                if li:
                                    pe.wait_ge(*x_up.after(l, 8 * g + 2 * li + e - 1))
                                    transpose_half(e)
                                else:
                                    pe.wait_ge(*xt_s.after(l, 10 * g + e + 1))
                                for j in range(JT):
                                    a = 4 * e + j
                                    ins = pe.matmul(bank[e][:, j * P:(j + 1) * P],
                                                    bq[:, a, 1:3, :].rearrange("p b q -> p (b q)"), xm[:, a, :],
                                                    start=True, stop=True)
                                ins.then_inc(zl_ps.sem, 1)
                            if li == 2:
                                pe.wait_ge(*kq_s.after(l, 4 * g + 2))
                                hats(kh, 3, 6, kq_ps)
                            for e in range(2):
                                pe.wait_ge(*zl_s.after(l, 10 * g + 2 * li + e + 1))
                                pe.wait_ge(*xt_s.after(l, 10 * g + 2 * li + e + 1))
                                if li == 0 and e:
                                    pe.wait_ge(*kq_s.after(l, 4 * g + 1))
                                for j in range(JT):
                                    a = 4 * e + j
                                    o = bank[(2 if li < 4 else 4) + e][:, j * P:(j + 1) * P]
                                    if li < 4:
                                        ins = pe.matmul(o, xt[:, a, :], zm[:, a, :], start=True, stop=True)
                                    else:
                                        ins = pe.matmul(o, zm[:, a, :], xt[:, a, :], start=True, stop=True)
                                ins.then_inc(xz_ps.sem if li < 4 else zx_ps.sem, 1)

                        def at(h):
                            return 4 * (h % 2) + h // 2

                        pe.wait_ge(*kq_s.after(l, 4 * g + 4))
                        def both(v, c):
                            return v[:, 2 * c:2 * c + 2, :].rearrange("p b q -> p (b q)")

                        for c in tiles_of[d]:
                            for h in range(H):
                                ins = pe.matmul(chunk_bank[c][:, h * HD:(h + 1) * HD], both(kq[:, at(h), :, :], c),
                                                v_tok[:, t, h * HD:(h + 1) * HD], start=(h == 0), stop=False,
                                                skip_group_check=True)
                            if i == 0 and c == tiles_of[d][0]:
                                ins.then_inc(r_ps.sem, 1)
                        pe.wait_ge(*(st_s.after(l, updates(2 * g)) if i else st_zero.after(l, d + 1)))
                        for ci, c in enumerate(tiles_of[d]):
                            n = 2 * g + ci
                            r = slice(C * c, C * (c + 1))
                            here = slice(t * P + C * c, t * P + C * (c + 1))
                            if ci:
                                pe.wait_ge(*st_s.after(l, updates(n)))
                            if i or ci:
                                for j in range(JT):
                                    ins = pe.matmul(chunk_bank[c][:, j * P:(j + 1) * P], both(kr[:, j, t, :, :], c),
                                                    state[:, j, :], start=False, stop=False, skip_group_check=True)
                                ins.then_inc(r_ps.sem, 1)
                            last = i == 1 and ci == 1
                            for j in range(0 if last else JT):
                                v = slice(j * P, (j + 1) * P)
                                pe.matmul(bank[1][:, v], kh_tok[r, t, v], v_tok[r, t, v], start=(j == 0), stop=False,
                                          skip_group_check=True)
                            convolution_half(g, 3 * ci)
                            pe.wait_ge(*xt_up.after(l, 2 * g + 2))
                            pe.wait_ge(*r_s.after(l, n + 1))
                            for h in range(H):
                                v = slice(h * HD, (h + 1) * HD)
                                ins = pe.matmul(bank[7][r, v], xt[:, at(h), r], r_b[:, v], start=True, stop=True)
                            ins.then_inc(u_ps.sem, 1)
                            convolution_half(g, 3 * ci + 1)
                            pe.wait_ge(*u_s.after(l, n + 1))

                            def own(h):
                                v = slice(h * HD, (h + 1) * HD)
                                return pe.matmul(chunk_bank[c][r, v], bq[:, at(h), 3 * c, :], u_b[:, v],
                                                 start=False, stop=True, skip_group_check=True)

                            own(0)
                            for j in range(0 if last else JT):
                                v = slice(j * P, (j + 1) * P)
                                ins = pe.matmul(bank[1][:, v], bh_tok[r, t, v], u_b[r, v], start=False, stop=True,
                                                skip_group_check=True)
                            if not last:
                                ins.then_inc(st_ps.sem, 1)
                            for h in range(1, H):
                                ins = own(h)
                            if ci:
                                ins.then_inc(y_ps.sem, 1)
                            convolution_half(g, 3 * ci + 2)

                pe.wait_ge(*bon_in.after(l, 1))
                for t in range(NT):
                    for j in range(JT):
                        ins = pe.matmul(bank[5][:, t * H + 2 * j:t * H + 2 * j + 2], cum[:, j, t * P:(t + 1) * P],
                                        con("headsum", 2), start=True, stop=True)
                ins.then_inc(bon_ps.sem, 1)
                pe.wait_ge(*cx_s.after(l, JT))
                gate(9)
                gate(10)
                pe.wait_ge(*y1_s.after(l, 2))
                pe.wait_ge(*gd_s.after(l, 1))
                for j in range(JT):
                    ins = pe.matmul(bank[6 + j // 2][:, (j % 2) * SEQ:(j % 2 + 1) * SEQ], lor[:, 2, j * P:(j + 1) * P],
                                    z[:, 14, :], start=True, stop=True)
                    if j % 2:
                        ins.then_inc(g_ps.sem, 1)
                for k in range(11, 14):
                    gate(k)

                def to_channels(src, b, done):
                    for j in range(JT):
                        for t in range(NT):
                            ins = pe.transpose(bank[b + j // 2][:, (j % 2) * SEQ + t * P:(j % 2) * SEQ + (t + 1) * P],
                                               src(t)[:, j * P:(j + 1) * P], ident)
                        if j % 2:
                            ins.then_inc(done.sem, 1)

                pe.wait_ge(*cv_s.after(l, JT))
                pe.wait_ge(*bv_s.after(l, 1))
                to_channels(lambda t: bonus_v[:, t * RW:(t + 1) * RW], 4, bt_ps)
                for k in range(14, 17):
                    gate(k)
                pe.wait_ge(*yn_s.after(l, 1))
                to_channels(lambda t: y_tok[:, t, :], 0, yt_ps)
                for k in range(17, 21):
                    gate(k)

                pe.wait_ge(*yo_s.after(l, 2))
                pe.wait_ge(*rope_s.after(l, NT))
                for m in range(4):
                    for t in range(NT):
                        ins = pe.transpose(bank[4 + m // 2][:, (m % 2) * SEQ + t * P:(m % 2) * SEQ + (t + 1) * P],
                                           q_rt[:, t, m * P:(m + 1) * P], ident)
                    if m % 2:
                        ins.then_inc(qt_ps.sem, 1)
                for t in range(NT):
                    ins = pe.transpose(bank[6][:, t * P:(t + 1) * P], q_rt[:, t, H * HD:H * HD + P], ident)
                ins.then_inc(qt_ps.sem, 1)

                def scores(i):
                    m, e = i // 2, slice(HD * (i % 2), HD * (i % 2 + 1))
                    if i >= 2:
                        pe.wait_ge(*pe_s.after(l, i - 1))
                    for t in range(NT):
                        ins = pe.matmul(bank[i % 2][:, t * SEQ:(t + 1) * SEQ],
                                        q_t[e, m, t * P:(t + 1) * P], k_t[e, :], start=True, stop=True)
                    ins.then_inc(sc_ps.sem, 1)

                def branch(i, b):
                    hi, lo, base = ((y_hi, y_lo, 0), (yb_hi, yb_lo, 0), (yb_hi, yb_lo, JT))[b]
                    u = U_BRANCH + (2 * i + b if b < 2 else KT + i)
                    weights(u)
                    for k in range(2):
                        if b == 0 and i:
                            pe.wait_ge(*part_s.after(l, 2 * i - 1 + k))
                        o = bank[2 + k][:, b * SEQ:(b + 1) * SEQ] if b < 2 else bank[4 + i][:, k * SEQ:(k + 1) * SEQ]
                        columns(o, u % RING, tiles=JT, width=2 * P, at=k * P, hi=hi, lo=lo, base=base, used=(k == 1))

                def early_branch(n):
                    if n == 0:
                        pe.wait_ge(*g3_s.after(l, 24))
                        pe.wait_ge(*ylo_s.after(l, 1))
                    elif n == 1:
                        pe.wait_ge(*cvlo_s.after(l, 1))
                    branch(n // 2, n % 2)

                gate(21)
                pe.wait_ge(*qt_s.after(l, 3))
                for i in range(2):
                    scores(i)
                gate(22)
                for i in range(H):
                    m, e = i // 2, i % 2
                    pe.wait_ge(*pn_s.after(l, i + 1))
                    if i >= 2:
                        pe.wait_ge(*pt_s.after(l, i - 1))
                    for st in range(NT):
                        for t in range(NT):
                            ins = pe.transpose(bank[4 + i % 2][:, st * SEQ + t * P:st * SEQ + (t + 1) * P],
                                               prob[:, i % 2, t, st * P:(st + 1) * P], ident)
                    ins.then_inc(pt_ps.sem, 1)
                    if i + 2 < H:
                        scores(i + 2)
                    if i:
                        early_branch(i - 1)
                    else:
                        gate(23)
                    pe.wait_ge(*pt_s.after(l, i + 1))
                    h = m + 4 * e
                    o = bank[6 + h // 4][HD * (h % 2):HD * (h % 2 + 1), (h // 2 % 2) * SEQ:(h // 2 % 2 + 1) * SEQ]
                    for st in range(NT):
                        at = (H + KV + e) * HD
                        ins = pe.matmul(o, qkv[:, st, at:at + HD], p_t[:, i % 2, st, :], start=(st == 0),
                                        stop=(st == NT - 1))
                    ins.then_inc(o_ps.sem, 1)

                early_branch(7)
                pe.wait_ge(*olo_s.after(l, 2))
                for i in range(4):
                    branch(i, 2)

                def rows(u, hi, lo, start, stop, it=0):
                    s = u % RING
                    weights(u, it)
                    for t in range(NT):
                        tok = slice(t * P, (t + 1) * P)
                        parts = ((hi, w_hi), (hi, w_lo), (lo, w_hi))
                        order = [(i, n) for i in range(3) for n in range(2)]
                        if stop and t:
                            order.sort(key=lambda p: p[1])
                        for i, n in order:
                            a, w = parts[i]
                            ins = pe.matmul(bank[2 * t + n][:, :], a[:, tok], w[:, s, n * 512:(n + 1) * 512],
                                            start=start and i == 0, stop=stop and i == 2)
                            if stop and i == 2 and t + n == 1:
                                ins.then_inc(sums_s.sem, 1)
                    ins.then_inc(unit_used.sem, 1)

                pe.wait_ge(*part_s.after(l, KT))
                for k in range(KT):
                    pe.wait_ge(*mlo_s.after(l, k + 1))
                    rows(U_OUT + k, m_hi[:, k, :], m_lo[:, k, :], k == 0, k == KT - 1)
                norm(1, xn2)

                def up(p, it=0):
                    s = p % 3
                    u0 = U_MLP + (2 + 4 * (p - 1) if p else 0)
                    if p >= 3 or not isinstance(it, int):
                        pe.wait_ge(*us_s.after(l, 3 * it + p - 2))
                    for k in range(2):
                        weights(u0 + k, it)
                        columns(bank[4 + s][:, k * SEQ:(k + 1) * SEQ], (u0 + k) % RING,
                                arriving=None if p or k else KT)

                def down(p, it=0, start=False, stop=False):
                    s = p % 3
                    pe.wait_ge(*ulo_s.after(l, 3 * it + p + 1))
                    for k in range(2):
                        rows(U_MLP + 4 + 4 * p + k if p < 15 else UNITS - 2 + k, u_hi[:, s, k, :], u_lo[:, s, k, :],
                             start and k == 0, stop and k == 1, it)

                up(0)
                for p in range(1, 4):
                    up(p)
                    down(p - 1, start=(p == 1))
                with pe.Fori(1, 4) as it:
                    for p in range(1, 4):
                        up(p, it)
                        down(p - 1, it)
                for p in range(13, 16):
                    up(p)
                    down(p - 1)
                down(15, stop=True)


def constants():
    c = np.zeros((P, NCONST), np.float32)
    i, j = np.arange(P)[:, None], np.arange(P)[None, :]

    def put(name, at, v):
        c[:v.shape[0], CONST[name] + at:CONST[name] + at + v.shape[1]] = v

    put("ident", 0, i == j)
    put("headsum", 0, i // HD == np.arange(2)[None, :])
    put("sel", 0, np.arange(2)[:, None] == j // HD)
    chunk = i // C == j // C
    for d in range(2):
        before = (i < j) if d == 0 else (i > j)
        strict, incl = chunk & before, chunk & (before | (i == j))
        put("incl", d * 2 * P, np.concatenate([incl[:, 0:C], strict, incl[:, C:]], 1))
        for n, b in enumerate(LEVELS):
            fill = (i // (2 * b) == j // (2 * b)) & (i // b % 2 == 1) & (j // b % 2 == 0)
            fill = -(fill if d == 0 else fill.T).astype(np.float32)
            if n == 0:
                put("first", d * P, fill)
            else:
                put("level", (d * 5 + n - 1) * C, fill[:, 0:C] + fill[:, C:P])
    put("reset", 0, np.repeat(np.arange(SEQ)[None, :] % C != 0, P, 0))
    half = HD // 2
    inv = (np.float32(10000.0) ** (-np.arange(0, half, 2, dtype=np.float32) / np.float32(half))).astype(np.float32)
    for t in range(NT):
        tok = t * P + np.arange(P)
        for a, pos in enumerate((tok // GRID_W, tok % GRID_W)):
            ang = pos.astype(np.float32)[:, None] * inv
            cos, sin = np.cos(ang), np.sin(ang)
            put("rope_c", t * HD + a * half, np.concatenate([cos, cos], 1))
            put("rope_s", t * HD + a * half, np.concatenate([-sin, sin], 1))
    return c


def layout(inputs):
    f = {k: np.asarray(v) for k, v in inputs.items()}
    L = DEPTH
    w = f["w_in"].reshape(L, KT, P, -1)

    def cols(at):
        return w[..., at:at + P].transpose(0, 2, 1, 3).reshape(L, P, UNIT)

    rwc, cvc = 15 * P, 12 * P
    units = [cols(u * P) for u in range(15)]
    for a in range(2):
        at = rwc + cvc + a * 3 * P
        v = w[..., at:at + 3 * P].transpose(0, 2, 1, 3).reshape(L, P, 3 * UNIT)
        units += [v[..., k * UNIT:(k + 1) * UNIT] for k in range(3)]
    conv = [[cols(rwc + s * RW + i * P) for s in (1, 2, 0)] for i in range(JT)]
    gate = rwc + cvc + QKV
    gates = [cols(gate + b * D + n * P) for n in range(KT) for b in range(3)]
    units += gates[0:3] + conv[0] + conv[1] + gates[3:9] + conv[2] + conv[3] + gates[9:]
    br = f["w_branch"].reshape(L, 3, JT, P, 4, 2 * P)
    order = [(i, b) for i in range(4) for b in range(2)] + [(i, 2) for i in range(4)]
    units += [br[:, b, :, :, i].transpose(0, 2, 1, 3).reshape(L, P, UNIT) for i, b in order]
    units += [f["w_out"].reshape(L, KT, P, D)[:, k] for k in range(KT)]
    w1 = f["w_mlp1"].reshape(L, KT, P, FF // P, P)
    w2 = f["w_mlp2"].reshape(L, FF // P, P, D)
    up = [w1[:, :, :, n].transpose(0, 2, 1, 3).reshape(L, P, UNIT) for n in range(FF // P)]
    units += up[0:2]
    for p in range(1, 16):
        units += up[2 * p:2 * p + 2] + [w2[:, 2 * p - 2], w2[:, 2 * p - 1]]
    units += [w2[:, 30], w2[:, 31]]
    assert len(units) == UNITS
    stream = np.stack(units, 1)
    names = {"mu_prev": "rw_mu_prev", "mu_next": "rw_mu_next", "w0": "rw_w0", "a0": "rw_a0", "k_k": "rw_k_k",
             "k_a": "rw_k_a", "r_k": "rw_r_k", "ln_g": "rw_ln_g", "ln_b": "rw_ln_b"}
    params = np.concatenate([f[names.get(k, k)].reshape(L, -1, P).transpose(0, 2, 1) for k in PARAMS], 2)
    lora = np.stack([f["rw_w2"].reshape(L, P, RW), f["rw_a2"].reshape(L, P, RW), f["rw_g2"]], 2)
    gains = np.concatenate([f["at_q_g"], f["at_k_g"]], 1)
    return {"x": f["x"].reshape(SEQ, D), "stream": stream, "params": params, "lora": lora, "gains": gains,
            "consts": constants()}


def kernel(**inputs):
    import concourse.bacc as _bacc
    from concourse.bass_utils import run_bass_kernel_spmd as _run

    nc = _bacc.Bacc("TRN2", target_bir_lowering=False, num_devices=1, dynamic_dma_scratch_size=1024)
    arrays, args = {}, []
    for name, a in layout(inputs).items():
        arrays[f"in_{name}"] = np.ascontiguousarray(a)
        args.append(nc.dram_tensor(f"in_{name}", a.shape, F32, kind="ExternalInput").ap())
    out = nc.dram_tensor("out_x", (SEQ, D), F32, kind="ExternalOutput").ap()
    build(nc, *args, out)
    r = _run(nc, [arrays], core_ids=[0])
    return r.results[0]["out_x"].reshape(1, SEQ, D)
```
